# Optimizing a Trainium2 kernel written in Bass

```python
import math
import jax, jax.numpy as jnp
from jax import lax
import numpy as np

D_MODEL = 1024
BATCH = 1
SEQ = 512
DEPTH = 2

N_MIXERS = 2
EPS = 1e-6

A_EXPAND = 2
A_WIDTH = A_EXPAND * D_MODEL
A_CHUNK = 128
A_HEADS = 16
A_HEAD_DIM = A_WIDTH // A_HEADS

B_GROUPS = ((128, 1), (512, 4), (2048, 16))
B_N_GROUPS = len(B_GROUPS)
B_HEADS = 16
B_HEAD_DIM = 64
B_WIDTH = B_HEADS * B_HEAD_DIM
B_QKV = B_N_GROUPS * 3 * B_WIDTH
B_TOTAL_HEADS = B_N_GROUPS * B_HEADS

REL_BUCKETS = 32
REL_EXACT = 8
REL_MAX_DISTANCE = 1024

N_A_LAYERS = (DEPTH + 1) // 2
N_B_LAYERS = DEPTH // 2
NEG_INF = -1e30


def rms_norm(x, g):
    xf = x.astype(jnp.float32)
    y = xf * lax.rsqrt(jnp.mean(xf * xf, axis=-1, keepdims=True) + EPS)
    return (y * g.astype(jnp.float32)).astype(x.dtype)

def layer_norm(x, g, b):
    xf = x.astype(jnp.float32)
    mu = jnp.mean(xf, axis=-1, keepdims=True)
    xc = xf - mu
    y = xc * lax.rsqrt(jnp.mean(xc * xc, axis=-1, keepdims=True) + EPS)
    return (y * g.astype(jnp.float32) + b.astype(jnp.float32)).astype(x.dtype)

def t5_bucket(rel):
    half = REL_BUCKETS // 2
    ret = jnp.where(rel > 0, half, 0)
    n = jnp.abs(rel)
    nf = jnp.maximum(n, 1).astype(jnp.float32)
    large = REL_EXACT + (jnp.log(nf / REL_EXACT) / math.log(REL_MAX_DISTANCE / REL_EXACT)
                         * (half - REL_EXACT)).astype(jnp.int32)
    large = jnp.minimum(large, half - 1)
    return ret + jnp.where(n < REL_EXACT, n, large)

def gmlp_mixer(h, w_in, w_s, b_s, vn_g, vn_b, w_out):
    bsz, s, _ = h.shape
    z = h @ w_in
    u, v, g = jnp.split(z, 3, axis=-1)
    u = jax.nn.gelu(u)
    v = layer_norm(jax.nn.gelu(v), vn_g, vn_b)
    nc = s // A_CHUNK
    vc = v.reshape(bsz, nc, A_CHUNK, A_HEADS, A_HEAD_DIM)
    sg = jnp.einsum('hpq,bcqhd->bcphd', w_s, vc) + b_s.T[None, None, :, :, None]
    y = u * sg.reshape(bsz, s, A_WIDTH) * jax.nn.silu(g)
    return y @ w_out

def dilated_window_group(q, k, v, table, dilation, half_w):
    bsz, s, nh, dh = q.shape
    L = s // dilation
    W = half_w
    nb = -(-L // W)
    Lp = nb * W

    def strided(t):
        return t.reshape(bsz, L, dilation, nh, dh).transpose(0, 2, 1, 3, 4)

    qs = jnp.pad(strided(q), ((0, 0), (0, 0), (0, Lp - L), (0, 0), (0, 0)))
    pad_kv = ((0, 0), (0, 0), (W, Lp - L + W), (0, 0), (0, 0))
    kp = jnp.pad(strided(k), pad_kv).reshape(bsz, dilation, nb + 2, W, nh, dh)
    vp = jnp.pad(strided(v), pad_kv).reshape(bsz, dilation, nb + 2, W, nh, dh)

    def band(t):
        return jnp.concatenate([t[:, :, 0:nb], t[:, :, 1:nb + 1], t[:, :, 2:nb + 2]], axis=3)

    kb, vb = band(kp), band(vp)
    qb = qs.reshape(bsz, dilation, nb, W, nh, dh)

    logits = jnp.einsum('bnkqhd,bnkjhd->bnkhqj', qb, kb,
                        preferred_element_type=jnp.float32) * (dh ** -0.5)
    qi = jnp.arange(W, dtype=jnp.int32)[:, None]
    kj = jnp.arange(3 * W, dtype=jnp.int32)[None, :]
    rel = kj - W - qi
    bias = table.astype(jnp.float32)[t5_bucket(rel * dilation)].transpose(2, 0, 1)
    key_pos = jnp.arange(nb, dtype=jnp.int32)[:, None] * W + kj - W
    mask = (jnp.abs(rel) <= W)[None] & ((key_pos >= 0) & (key_pos < L))[:, None, :]
    logits = jnp.where(mask[None, None, :, None], logits + bias, NEG_INF)

    m = jnp.max(logits, axis=-1, keepdims=True)
    p = jnp.exp(logits - m)
    den = jnp.sum(p, axis=-1, keepdims=True)
    o = jnp.einsum('bnkhqj,bnkjhd->bnkqhd', p / den, vb.astype(jnp.float32))
    lse = (m + jnp.log(den))[..., 0]

    o = o.reshape(bsz, dilation, Lp, nh, dh)[:, :, :L].transpose(0, 2, 1, 3, 4).reshape(bsz, s, nh, dh)
    lse = lse.transpose(0, 1, 2, 4, 3).reshape(bsz, dilation, Lp, nh)[:, :, :L]
    lse = lse.transpose(0, 2, 1, 3).reshape(bsz, s, nh)
    return o, lse

def dilated_attention_mixer(h, w_in, w_out, rel_table):
    bsz, s, _ = h.shape
    z = h @ w_in
    qkv = z[..., :B_QKV].reshape(bsz, s, B_N_GROUPS, 3, B_HEADS, B_HEAD_DIM)
    gate = z[..., B_QKV:]
    outs, lses = [], []
    for gi, (window, dil) in enumerate(B_GROUPS):
        o, lse = dilated_window_group(qkv[:, :, gi, 0], qkv[:, :, gi, 1], qkv[:, :, gi, 2],
                                      rel_table[:, gi * B_HEADS:(gi + 1) * B_HEADS],
                                      dil, window // (2 * dil))
        outs.append(o)
        lses.append(lse)
    wts = jax.nn.softmax(jnp.stack(lses), axis=0)
    o = jnp.einsum('gbsh,gbshd->bshd', wts, jnp.stack(outs))
    y = o.reshape(bsz, s, B_WIDTH).astype(h.dtype) * jax.nn.silu(gate)
    return y @ w_out

def first_inputs(seed: int = 0) -> dict:
    key = jax.random.key(seed)
    ks = jax.random.split(key, 16)
    f32 = jnp.float32
    x = jax.random.normal(ks[0], (BATCH, SEQ, D_MODEL), f32)
    norm_pre = 1.0 + 0.1 * jax.random.normal(ks[1], (DEPTH, D_MODEL), f32)
    norm_post = 1.0 + 0.1 * jax.random.normal(ks[2], (DEPTH, D_MODEL), f32)
    a_w_in = jax.random.normal(ks[3], (N_A_LAYERS, D_MODEL, 3 * A_WIDTH), f32) * D_MODEL ** -0.5
    a_w_s = jax.random.normal(ks[4], (N_A_LAYERS, A_HEADS, A_CHUNK, A_CHUNK), f32) * A_CHUNK ** -0.5
    a_b_s = 1.0 + 0.1 * jax.random.normal(ks[5], (N_A_LAYERS, A_HEADS, A_CHUNK), f32)
    a_vnorm_g = 1.0 + 0.1 * jax.random.normal(ks[6], (N_A_LAYERS, A_WIDTH), f32)
    a_vnorm_b = 0.1 * jax.random.normal(ks[7], (N_A_LAYERS, A_WIDTH), f32)
    a_w_out = jax.random.normal(ks[8], (N_A_LAYERS, A_WIDTH, D_MODEL), f32) * A_WIDTH ** -0.5
    b_w_in = jax.random.normal(ks[9], (N_B_LAYERS, D_MODEL, B_QKV + B_WIDTH), f32) * D_MODEL ** -0.5
    b_w_out = jax.random.normal(ks[10], (N_B_LAYERS, B_WIDTH, D_MODEL), f32) * B_WIDTH ** -0.5
    rel_bias = 0.5 * jax.random.normal(ks[11], (REL_BUCKETS, B_TOTAL_HEADS), f32)
    return {"x": x, "norm_pre": norm_pre, "norm_post": norm_post,
            "a_w_in": a_w_in, "a_w_s": a_w_s, "a_b_s": a_b_s,
            "a_vnorm_g": a_vnorm_g, "a_vnorm_b": a_vnorm_b, "a_w_out": a_w_out,
            "b_w_in": b_w_in, "b_w_out": b_w_out, "rel_bias": rel_bias}

def first_block(x, norm_pre, norm_post, a_w_in, a_w_s, a_b_s, a_vnorm_g, a_vnorm_b, a_w_out,
              b_w_in, b_w_out, rel_bias):
    for i in range(DEPTH):
        h = rms_norm(x, norm_pre[i])
        j = i // N_MIXERS
        if i % N_MIXERS == 0:
            y = gmlp_mixer(h, a_w_in[j], a_w_s[j], a_b_s[j], a_vnorm_g[j], a_vnorm_b[j], a_w_out[j])
        else:
            y = dilated_attention_mixer(h, b_w_in[j], b_w_out[j], rel_bias)
        x = x + rms_norm(y, norm_post[i])
    return x


N_MEM = 256
N_A_LAYERS_2 = DEPTH // 2
N_B_LAYERS_2 = DEPTH - N_A_LAYERS_2
QBLOCK = 128

TOK_HEADS = 12
HEAD_DIM = 64
MEM_HEADS = 4
MEM_HEAD_DIM = 64
TOK_WIDTH = TOK_HEADS * HEAD_DIM
MEM_WIDTH = MEM_HEADS * MEM_HEAD_DIM
MIX_WIDTH = TOK_WIDTH + MEM_WIDTH

MLA_Q_RANK = 256
MLA_KV_RANK = 128
MLA_NOPE = 64
MLA_ROPE = 32
MLA_V = HEAD_DIM
ROPE_THETA = 10000.0
MLA_IN = MLA_Q_RANK + MLA_KV_RANK + MLA_ROPE + MEM_WIDTH

NSA_GROUPS = 2
NSA_HPG = TOK_HEADS // NSA_GROUPS
NSA_BRANCHES = 3
CMP_LEN = 32
CMP_STRIDE = 16
CMP_HIDDEN = 256
SEL_LEN = 64
SEL_TOPK = 16
WINDOW = 512
NSA_IN = TOK_WIDTH + TOK_HEADS * NSA_BRANCHES + MEM_WIDTH
NSA_KV = NSA_BRANCHES * 2 * NSA_GROUPS * HEAD_DIM

D_FF = 2816

DN_ALPHA = (2 * DEPTH) ** 0.25
DN_BETA = (8 * DEPTH) ** -0.25

LN_EPS = 1e-5
RMS_EPS = 1e-6
NEG = -1e30
FORCE_BONUS = 1e4


def layer_norm_2(x, g, b):
    xf = x.astype(jnp.float32)
    mu = jnp.mean(xf, -1, keepdims=True)
    var = jnp.mean(jnp.square(xf - mu), -1, keepdims=True)
    return ((xf - mu) * lax.rsqrt(var + LN_EPS) * g + b).astype(x.dtype)

def rms_norm_2(x, g):
    xf = x.astype(jnp.float32)
    return (xf * lax.rsqrt(jnp.mean(xf * xf, -1, keepdims=True) + RMS_EPS) * g).astype(x.dtype)

def masked_softmax(s, mask, axis=-1):
    s = jnp.where(mask, s.astype(jnp.float32), NEG)
    m = jnp.max(s, axis=axis, keepdims=True)
    e = jnp.exp(s - m) * mask
    return e / jnp.maximum(jnp.sum(e, axis=axis, keepdims=True), 1e-30)

def swiglu(x, w_gu, w_down):
    g, u = jnp.split(x @ w_gu, 2, axis=-1)
    return (jax.nn.silu(g) * u) @ w_down

def rope(x, pos):
    half = x.shape[-1] // 2
    freq = ROPE_THETA ** (-jnp.arange(half, dtype=jnp.float32) / half)
    ang = pos.astype(jnp.float32)[:, None] * freq[None, :]
    cos, sin = jnp.cos(ang), jnp.sin(ang)
    x1, x2 = x[..., :half], x[..., half:]
    return jnp.concatenate([x1 * cos - x2 * sin, x2 * cos + x1 * sin], -1).astype(x.dtype)

def alibi_slopes(n):
    def pow2(k):
        start = 2.0 ** (-8.0 / k)
        return [start ** (i + 1) for i in range(k)]
    if math.log2(n).is_integer():
        s = pow2(n)
    else:
        c = 2 ** math.floor(math.log2(n))
        s = pow2(c) + pow2(2 * c)[0::2][: n - c]
    return np.asarray(s, np.float32)

def memory_attention(q_mem, mem, w_mem_kv):
    B, T, _ = q_mem.shape
    M = mem.shape[1]
    k, v = jnp.split(mem @ w_mem_kv, 2, axis=-1)
    q = q_mem.reshape(B, T, MEM_HEADS, MEM_HEAD_DIM)
    k = k.reshape(B, M, MEM_HEADS, MEM_HEAD_DIM)
    v = v.reshape(B, M, MEM_HEADS, MEM_HEAD_DIM)
    s = jnp.einsum('bthd,bmhd->bhtm', q, k).astype(jnp.float32) * (MEM_HEAD_DIM ** -0.5)
    p = jax.nn.softmax(s, axis=-1).astype(v.dtype)
    return jnp.einsum('bhtm,bmhd->bthd', p, v).reshape(B, T, MEM_WIDTH)

def mla_mix(x, w_in, q_norm_g, kv_norm_g, w_uq, w_ukv, pos):
    B, T, _ = x.shape
    H = TOK_HEADS
    c_q, c_kv, k_r, q_mem = jnp.split(
        x @ w_in, [MLA_Q_RANK, MLA_Q_RANK + MLA_KV_RANK, MLA_Q_RANK + MLA_KV_RANK + MLA_ROPE], axis=-1)
    q = (rms_norm_2(c_q, q_norm_g) @ w_uq).reshape(B, T, H, MLA_NOPE + MLA_ROPE).transpose(0, 2, 1, 3)
    q = jnp.concatenate([q[..., :MLA_NOPE], rope(q[..., MLA_NOPE:], pos)], -1)
    kv = (rms_norm_2(c_kv, kv_norm_g) @ w_ukv).reshape(B, T, H, MLA_NOPE + MLA_V).transpose(0, 2, 1, 3)
    k_nope, v = kv[..., :MLA_NOPE], kv[..., MLA_NOPE:]
    k_r = rope(k_r, pos)
    k = jnp.concatenate([k_nope, jnp.broadcast_to(k_r[:, None], (B, H, T, MLA_ROPE))], -1)
    scale = (MLA_NOPE + MLA_ROPE) ** -0.5
    key_pos = jnp.arange(T)

    def block(c):
        t0 = c * QBLOCK
        tq = t0 + jnp.arange(QBLOCK)
        qb = lax.dynamic_slice_in_dim(q, t0, QBLOCK, axis=2)
        s = jnp.einsum('bhqd,bhkd->bhqk', qb, k) * scale
        p = masked_softmax(s, key_pos[None, :] <= tq[:, None]).astype(v.dtype)
        return jnp.einsum('bhqk,bhkd->bqhd', p, v)

    o = lax.map(block, jnp.arange(T // QBLOCK))
    o = o.transpose(1, 0, 2, 3, 4).reshape(B, T, TOK_WIDTH)
    return o, q_mem

def nsa_shared_kv(h, w_kv, cmp_pos, cmp_w1, cmp_b1, cmp_w2):
    B, T, _ = h.shape
    G = NSA_GROUPS
    kv = (h @ w_kv).reshape(B, T, NSA_BRANCHES, 2, G, HEAD_DIM).transpose(2, 3, 0, 4, 1, 5)
    n_cmp = (T - CMP_LEN) // CMP_STRIDE + 1
    idx = np.arange(n_cmp)[:, None] * CMP_STRIDE + np.arange(CMP_LEN)[None, :]

    def compress(z, j):
        blocks = z[:, :, idx] + cmp_pos[j]
        flat = blocks.reshape(B, G, n_cmp, CMP_LEN * HEAD_DIM)
        return jax.nn.gelu(flat @ cmp_w1[j] + cmp_b1[j]) @ cmp_w2[j]

    kc = compress(kv[0, 0], 0)
    vc = compress(kv[0, 1], 1)
    n_sel = T // SEL_LEN
    ks = kv[1, 0].reshape(B, G, n_sel, SEL_LEN, HEAD_DIM)
    vs = kv[1, 1].reshape(B, G, n_sel, SEL_LEN, HEAD_DIM)
    pad = ((0, 0), (0, 0), (WINDOW, 0), (0, 0))
    kw_pad = jnp.pad(kv[2, 0], pad)
    vw_pad = jnp.pad(kv[2, 1], pad)
    return kc, vc, ks, vs, kw_pad, vw_pad

def nsa_mix(x, w_in, kc, vc, ks, vs, kw_pad, vw_pad, slopes):
    B, T, _ = x.shape
    G, HPG = NSA_GROUPS, NSA_HPG
    q, gates, q_mem = jnp.split(x @ w_in, [TOK_WIDTH, TOK_WIDTH + TOK_HEADS * NSA_BRANCHES], axis=-1)
    q = q.reshape(B, T, G, HPG, HEAD_DIM).transpose(0, 2, 3, 1, 4)
    gates = jax.nn.sigmoid(gates.reshape(B, T, G, HPG, NSA_BRANCHES).transpose(0, 2, 3, 1, 4))
    m = slopes.reshape(G, HPG)[None, :, :, None, None]
    n_cmp = kc.shape[2]
    n_sel = ks.shape[2]
    topk = min(SEL_TOPK, n_sel)
    cmp_start = np.arange(n_cmp) * CMP_STRIDE
    cmp_end = jnp.asarray(cmp_start + CMP_LEN - 1)
    cmp_center = jnp.asarray(cmp_start + (CMP_LEN - 1) * 0.5, dtype=jnp.float32)
    sel_start = np.arange(n_sel) * SEL_LEN
    overlap = np.clip(np.minimum(cmp_start[:, None] + CMP_LEN, sel_start[None, :] + SEL_LEN)
                      - np.maximum(cmp_start[:, None], sel_start[None, :]), 0, None)
    agg = jnp.asarray(overlap / CMP_LEN, dtype=jnp.float32)
    blk = jnp.arange(n_sel)
    scale = HEAD_DIM ** -0.5
    gather = jax.vmap(jax.vmap(lambda blocks, i: blocks[i]))

    def block(c):
        t0 = c * QBLOCK
        tq = t0 + jnp.arange(QBLOCK)
        qb = lax.dynamic_slice_in_dim(q, t0, QBLOCK, axis=3)
        gb = lax.dynamic_slice_in_dim(gates, t0, QBLOCK, axis=3)
        dist_c = tq[:, None].astype(jnp.float32) - cmp_center[None, :]
        s_c = jnp.einsum('bghqd,bgnd->bghqn', qb, kc) * scale - m * dist_c
        p_c = masked_softmax(s_c, cmp_end[None, :] <= tq[:, None])
        o_c = jnp.einsum('bghqn,bgnd->bghqd', p_c.astype(vc.dtype), vc)
        imp = jnp.einsum('bghqn,nj->bgqj', p_c, agg)
        cur = tq // SEL_LEN
        forced = (blk[None] == 0) | (blk[None] == cur[:, None]) | (blk[None] == cur[:, None] - 1)
        imp = jnp.where(forced, imp + FORCE_BONUS, imp)
        imp = jnp.where(blk[None] * SEL_LEN <= tq[:, None], imp, NEG)
        _, sel = lax.top_k(imp, topk)
        k_sel = gather(ks, sel)
        v_sel = gather(vs, sel)
        pos_s = sel[..., None] * SEL_LEN + jnp.arange(SEL_LEN)
        dist_s = (tq[None, None, :, None, None] - pos_s)[:, :, None]
        s_s = jnp.einsum('bghqd,bgqkld->bghqkl', qb, k_sel) * scale - m[..., None] * dist_s
        p_s = masked_softmax(s_s, dist_s >= 0, axis=(-2, -1))
        o_s = jnp.einsum('bghqkl,bgqkld->bghqd', p_s.astype(v_sel.dtype), v_sel)
        kw = lax.dynamic_slice_in_dim(kw_pad, t0, WINDOW + QBLOCK, axis=2)
        vw = lax.dynamic_slice_in_dim(vw_pad, t0, WINDOW + QBLOCK, axis=2)
        pos_w = t0 - WINDOW + jnp.arange(WINDOW + QBLOCK)
        dist_w = tq[:, None] - pos_w[None, :]
        mask_w = (dist_w >= 0) & (dist_w < WINDOW) & (pos_w[None, :] >= 0)
        s_w = jnp.einsum('bghqd,bgkd->bghqk', qb, kw) * scale - m * dist_w
        p_w = masked_softmax(s_w, mask_w)
        o_w = jnp.einsum('bghqk,bgkd->bghqd', p_w.astype(vw.dtype), vw)
        o = gb[..., 0:1] * o_c + gb[..., 1:2] * o_s + gb[..., 2:3] * o_w
        return o.transpose(0, 3, 1, 2, 4).reshape(B, QBLOCK, TOK_WIDTH)

    o = lax.map(block, jnp.arange(T // QBLOCK))
    o = o.transpose(1, 0, 2, 3).reshape(B, T, TOK_WIDTH)
    return o, q_mem

def second_inputs(seed: int = 0) -> dict:
    key = jax.random.key(seed)
    ks = jax.random.split(key, 20)

    def nrm(k, shape, fan_in, gain=1.0):
        return jax.random.normal(k, shape, jnp.float32) * (gain * fan_in ** -0.5)

    def gain(k, shape):
        return 1.0 + 0.02 * jax.random.normal(k, shape, jnp.float32)

    return {
        "x": jax.random.normal(ks[0], (BATCH, SEQ, D_MODEL), jnp.float32),
        "mem": jax.random.normal(ks[1], (BATCH, N_MEM, D_MODEL), jnp.float32),
        "ln_g": gain(ks[2], (DEPTH, 3, D_MODEL)),
        "ln_b": 0.02 * jax.random.normal(ks[3], (DEPTH, 3, D_MODEL), jnp.float32),
        "ffn_w_gu": nrm(ks[4], (DEPTH, 2, D_MODEL, 2 * D_FF), D_MODEL),
        "ffn_w_down": nrm(ks[5], (DEPTH, 2, D_FF, D_MODEL), D_FF, DN_BETA),
        "w_mem_kv": nrm(ks[6], (DEPTH, D_MODEL, 2 * MEM_WIDTH), D_MODEL),
        "w_out": nrm(ks[7], (DEPTH, MIX_WIDTH, D_MODEL), MIX_WIDTH, DN_BETA),
        "mla_w_in": nrm(ks[8], (N_A_LAYERS_2, D_MODEL, MLA_IN), D_MODEL),
        "mla_q_norm_g": gain(ks[9], (N_A_LAYERS_2, MLA_Q_RANK)),
        "mla_kv_norm_g": gain(ks[10], (N_A_LAYERS_2, MLA_KV_RANK)),
        "mla_w_uq": nrm(ks[11], (N_A_LAYERS_2, MLA_Q_RANK, TOK_HEADS * (MLA_NOPE + MLA_ROPE)), MLA_Q_RANK),
        "mla_w_ukv": nrm(ks[12], (N_A_LAYERS_2, MLA_KV_RANK, TOK_HEADS * (MLA_NOPE + MLA_V)), MLA_KV_RANK),
        "nsa_w_in": nrm(ks[13], (N_B_LAYERS_2, D_MODEL, NSA_IN), D_MODEL),
        "nsa_w_kv": nrm(ks[14], (D_MODEL, NSA_KV), D_MODEL),
        "cmp_pos": 0.1 * jax.random.normal(ks[15], (2, CMP_LEN, HEAD_DIM), jnp.float32),
        "cmp_w1": nrm(ks[16], (2, CMP_LEN * HEAD_DIM, CMP_HIDDEN), CMP_LEN * HEAD_DIM),
        "cmp_b1": 0.02 * jax.random.normal(ks[17], (2, CMP_HIDDEN), jnp.float32),
        "cmp_w2": nrm(ks[18], (2, CMP_HIDDEN, HEAD_DIM), CMP_HIDDEN),
    }

def second_block(x, mem, ln_g, ln_b, ffn_w_gu, ffn_w_down, w_mem_kv, w_out,
              mla_w_in, mla_q_norm_g, mla_kv_norm_g, mla_w_uq, mla_w_ukv,
              nsa_w_in, nsa_w_kv, cmp_pos, cmp_w1, cmp_b1, cmp_w2):
    T = x.shape[1]
    pos = jnp.arange(T)
    slopes = jnp.asarray(alibi_slopes(TOK_HEADS))
    shared = None
    for layer in range(DEPTH):
        x = layer_norm_2(DN_ALPHA * x + 0.5 * swiglu(x, ffn_w_gu[layer, 0], ffn_w_down[layer, 0]),
                       ln_g[layer, 0], ln_b[layer, 0])
        if layer < N_A_LAYERS_2:
            o_tok, q_mem = mla_mix(x, mla_w_in[layer], mla_q_norm_g[layer], mla_kv_norm_g[layer],
                                   mla_w_uq[layer], mla_w_ukv[layer], pos)
        else:
            b = layer - N_A_LAYERS_2
            kc, vc, ks_, vs_, kw_pad, vw_pad = shared
            o_tok, q_mem = nsa_mix(x, nsa_w_in[b], kc, vc, ks_, vs_, kw_pad, vw_pad, slopes)
        o_mem = memory_attention(q_mem, mem, w_mem_kv[layer])
        mix = jnp.concatenate([o_tok, o_mem], axis=-1) @ w_out[layer]
        x = layer_norm_2(DN_ALPHA * x + mix, ln_g[layer, 1], ln_b[layer, 1])
        x = layer_norm_2(DN_ALPHA * x + 0.5 * swiglu(x, ffn_w_gu[layer, 1], ffn_w_down[layer, 1]),
                       ln_g[layer, 2], ln_b[layer, 2])
        if layer == N_A_LAYERS_2 - 1:
            shared = nsa_shared_kv(x, nsa_w_kv, cmp_pos, cmp_w1, cmp_b1, cmp_w2)
    return x


def setup_inputs(seed=0):
    out = dict(first_inputs(seed))
    for name, value in second_inputs(seed + 1).items():
        if name != "x":
            out[name + "_2"] = value
    return out


def reference(
    x, norm_pre, norm_post, a_w_in, a_w_s, a_b_s, a_vnorm_g, a_vnorm_b, a_w_out, b_w_in,
    b_w_out, rel_bias, mem_2, ln_g_2, ln_b_2, ffn_w_gu_2, ffn_w_down_2, w_mem_kv_2, w_out_2,
    mla_w_in_2, mla_q_norm_g_2, mla_kv_norm_g_2, mla_w_uq_2, mla_w_ukv_2, nsa_w_in_2,
    nsa_w_kv_2, cmp_pos_2, cmp_w1_2, cmp_b1_2, cmp_w2_2,
):
    x = first_block(
        x, norm_pre, norm_post, a_w_in, a_w_s, a_b_s, a_vnorm_g, a_vnorm_b, a_w_out, b_w_in,
        b_w_out, rel_bias,
    )
    return second_block(
        x, mem_2, ln_g_2, ln_b_2, ffn_w_gu_2, ffn_w_down_2, w_mem_kv_2, w_out_2, mla_w_in_2,
        mla_q_norm_g_2, mla_kv_norm_g_2, mla_w_uq_2, mla_w_ukv_2, nsa_w_in_2, nsa_w_kv_2,
        cmp_pos_2, cmp_w1_2, cmp_b1_2, cmp_w2_2,
    )


_drawn_inputs = setup_inputs


def setup_inputs(seed=0):
    import zlib

    import numpy as np

    out = dict(_drawn_inputs(seed))
    spreads = {}
    factors = {'mla_q_norm_g_2': 8.0,
     'mla_kv_norm_g_2': 8.0,
     'cmp_pos_2': 5.051,
     'cmp_b1_2': 28.338,
     'mem_2': 2.824,
     'w_mem_kv_2': 2.788}
    for name, (base, spread) in spreads.items():
        noise = np.random.default_rng([zlib.crc32(name.encode()), seed]).standard_normal(out[name].shape)
        drawn = base * np.exp(spread * noise) if base else spread * noise
        out[name] = __import__('jax').numpy.asarray(drawn.astype(out[name].dtype))
    for name, factor in factors.items():
        out[name] = (out[name] * factor).astype(out[name].dtype)
    return out
```

```python
import math
from contextlib import ExitStack

import numpy as np

import concourse.bass as bass
from concourse import mybir

F32 = mybir.dt.float32
F32R = mybir.dt.float32r
ALU = mybir.AluOpType
ACT = mybir.ActivationFunctionType
AX = mybir.AxisListType

P = 128
SEQ, D = 512, 1024
TT = SEQ // P
KD = D // P
A_WIDTH = 2048
A_HEADS = 16
B_HEADS, B_DIM = 16, 64
B_SCALE = B_DIM ** -0.5
HALF_W = 64
REL_BUCKETS = 32
D_FF = 2816
KF = D_FF // P
N_MEM = 256
HEADS = 12
MLA_QR, MLA_KVR, MLA_NOPE, MLA_ROPE = 256, 128, 64, 32
MLA_QD = MLA_NOPE + MLA_ROPE
MLA_SCALE = MLA_QD ** -0.5
HD = 64
HD_SCALE = HD ** -0.5
CMP_LEN, CMP_STRIDE, CMP_HIDDEN = 32, 16, 256
N_CMP = (SEQ - CMP_LEN) // CMP_STRIDE + 1
NC = 32
ALPHA = 4.0 ** 0.25
RMS_EPS, LN_EPS = 1e-6, 1e-5
NEG = -1e30
BIAS_W = (384, 256, 256)
BIAS_AT = (0, 384, 640)
BIAS_ALL = 896


def alibi_slopes(n):
    def pow2(k):
        start = 2.0 ** (-8.0 / k)
        return [start ** (i + 1) for i in range(k)]
    c = 2 ** math.floor(math.log2(n))
    return pow2(n) if c == n else pow2(c) + pow2(2 * c)[0::2][: n - c]


class Counts:

    def __init__(self, known):
        self.known, self.total, self.value = known, {}, {}

    def step(self, name, *labels, by=1):
        self.total[name] = self.total.get(name, 0) + by
        for label in labels or (None,):
            self.value[name, label] = self.total[name]
        return by

    def at(self, name, label=None):
        return self.known[name, label] if self.known else 1


SIGNALS = """
    b_s_loaded bgate_read bias_copied bias_loaded bias_multiplied bias_stored
    bk_read blocks_ready bq_read bv_read c_high c_normed
    c_read c_rows c_split c_turned cmp_done cmp_exp
    cmp_hidden_done cmp_hidden_ready cmp_kept cmp_o_read cmp_p_ready cmp_p_turned
    cmp_pt_copied cmp_scored cmp_shifted cmp_weighted dve_step exp_done
    g_read gains_loaded gate_read group_diffs group_exps group_weights
    h1_zeroed half_ready head_turned heads_turned hidden_high hidden_split
    hot_loaded ident_loaded kv_copied kv_kept kvf_read masked
    maxed mem_high mem_kv_back mem_kv_copied mem_kv_stored mem_loaded
    mem_split mem_turned mix_const0 mix_ready mix_split ngates_read
    nq_read nsa_const o0_permuted o1_weighted o_read p_turned
    panel_loaded0 panel_loaded1 pool_step pos_loaded product_done pt_copied
    qmem_read rope_loaded roped rows_done rstd rstd_x
    scored spatial_done spatial_read squared squared_x stored
    table_ones turned turned_high u_read ukv_read_k ukv_read_v
    up_read uq_read uq_tail_read v_normed v_read variance
    w1_loaded w_high_ready w_low_ready weighted wrap_ready ws_copied
    ws_loaded ws_turned x_added x_loaded0 x_loaded1 x_loaded2
    x_loaded3 xt_ready y_high_ready y_multiplied y_split
"""


def weight_panels(A):
    panels, ids = [], {}

    def rows(w, k0, nk, c0, n):
        return w[k0 * P:(k0 + nk) * P, c0:c0 + n].rearrange("(k p) n -> p k n", p=P)

    def add(name, pieces):
        ids.setdefault(name, []).append(len(panels))
        panels.append(pieces)

    def deep(name, w, c0, n):
        for k0 in (0, 4):
            add(name, [(0, 4, n, n, rows(w, k0, 4, c0, n))])

    def down(name, w, kt):
        for k0 in range(0, kt, 2):
            add(name, [(0, 2, D, D, rows(w, k0, 2, 0, D))])

    for l in range(2):
        deep(("mem", l), A["w_mem_kv_2"][l], 0, 512)
    wa = A["a_w_in"][0]
    for c in range(4):
        deep(("v", c), wa, A_WIDTH + 512 * c, 512)
    for part, c in (("u", 0), ("u", 1), ("g", 0), ("g", 1), ("u", 2), ("g", 2), ("u", 3), ("g", 3)):
        deep((part, c), wa, (0 if part == "u" else 2 * A_WIDTH) + 512 * c, 512)
    down("a_out", A["a_w_out"][0], A_WIDTH // P)
    wb = A["b_w_in"][0]
    for g in range(3):
        for hf in range(2):
            for i, part in enumerate("qkv"):
                deep(("b", g, hf, part), wb, g * 3072 + i * 1024 + hf * 512, 512)
    for c in range(2):
        deep(("b_gate", c), wb, 9216 + 512 * c, 512)
    down("b_out", A["b_w_out"][0], 8)

    def ffn(l, i):
        w = A["ffn_w_gu_2"][l, i]
        for c in range(5):
            deep(("gate", l, i, c), w, 512 * c, 512)
            deep(("up", l, i, c), w, D_FF + 512 * c, 512)
        for k0 in (0, 4):
            add(("last", l, i), [(0, 4, 512, 256, rows(w, k0, 4, 2560, 256)),
                                 (256, 4, 512, 256, rows(w, k0, 4, D_FF + 2560, 256))])
        down(("down", l, i), A["ffn_w_down_2"][l, i], KF)

    ffn(0, 0)
    wm = A["mla_w_in_2"][0]
    deep("mla_in", wm, 0, 416)
    add("mla_mem", [(0, 8, 256, 256, rows(wm, 0, 8, 416, 256))])
    add("uq", [(0, 2, 1024, 1024, rows(A["mla_w_uq_2"][0], 0, 2, 0, 1024))])
    add("uq_tail", [(0, 2, 128, 128, rows(A["mla_w_uq_2"][0], 0, 2, 1024, 128))])
    add("ukv", [(0, 1, 1536, 1536, rows(A["mla_w_ukv_2"][0], 0, 1, 0, 1536))])
    down(("w_out", 0), A["w_out_2"][0], 8)
    ffn(0, 1)
    deep("kv_a", A["nsa_w_kv_2"], 0, 512)
    deep("kv_b", A["nsa_w_kv_2"], 512, 256)
    ffn(1, 0)
    wn = A["nsa_w_in_2"][0]
    for name in ("nsa_a", "nsa_b"):
        for k0 in (0, 4):
            pieces = []
            for kk in range(4):
                for g in range(2):
                    n = 4 if name == "nsa_a" else 2
                    c0 = g * 384 + (0 if name == "nsa_a" else 256)
                    src = wn[(k0 + kk) * P:(k0 + kk + 1) * P, c0:c0 + 64 * n].rearrange("p (i d) -> p i d", d=64)
                    pieces.append((kk * 512 + g * 64, n, 128, 64, src))
            if name == "nsa_b":
                pieces.append((256, 4, 512, 256, rows(wn, k0, 4, 804, 256)))
            add(name, pieces)
    add("nsa_gates", [(0, 8, 36, 36, rows(wn, 0, 8, 768, 36))])
    down(("w_out", 1), A["w_out_2"][1], 8)
    ffn(1, 1)
    widths = [max(off + (n - 1) * pitch + w for off, n, pitch, w, _ in pieces) for pieces in panels]
    return panels, ids, widths


def build(nc, A, out, scratch, ctx, counts):
    step, at = counts.step, counts.at
    sem = {name: ctx.enter_context(nc.semaphore(name)) for name in SIGNALS.split()}
    panels, ids, widths = weight_panels(A)

    base = [(nc.sbuf_base + 63) // 64 * 64]

    def at_off(name, shape, off, dt=F32):
        return nc.alloc_sbuf_tensor_at(name, shape, dt, offset=off)

    def place(nbytes):
        base[0] += nbytes
        return base[0] - nbytes

    KB = 1024
    ident = at_off("ident", [P, P], place(512))
    small = at_off("small", [P, 512], place(2 * KB))
    X = at_off("x_rows", [P, TT, D], place(16 * KB))
    xt0 = place(32 * KB)
    XTH = at_off("xt_high", [P, KD, SEQ], xt0, F32R)
    XTL = at_off("xt_low", [P, KD, SEQ], xt0 + 16 * KB, F32R)
    gb0 = place(8 * KB)
    GB = [at_off(f"gain{i}", [P, D], gb0 + 4 * KB * i) for i in range(2)]
    r0 = place(8 * KB)
    R = [at_off(f"row{i}", [P, D], r0 + 4 * KB * i) for i in range(2)]
    G = at_off("gate_rows", [P, 4, 512], r0)
    raw0 = place(16 * KB)
    RAW = [at_off(f"raw{i}", [P, 2048], raw0 + 8 * KB * i) for i in range(2)]
    w0 = place(32 * KB)
    WH = [at_off(f"w_high{i}", [P, 2048], w0 + 8 * KB * i, F32R) for i in range(2)]
    WL = [at_off(f"w_low{i}", [P, 2048], w0 + 16 * KB + 8 * KB * i, F32R) for i in range(2)]
    kept0 = place(3 * KB)
    KCT = at_off("cmp_keys", [P, NC], kept0)
    VC4 = at_off("cmp_values", [P, 2, 64], kept0 + 256)
    rg = place(88 * KB)
    assert base[0] <= nc.sbuf_usable_end, base[0]
    HTH = at_off("hidden_high", [P, KF, SEQ], rg, F32R)
    HTL = at_off("hidden_low", [P, KF, SEQ], rg + 44 * KB, F32R)
    ps = [ctx.enter_context(nc.psum_tensor(f"bank{i}", [P, 512], F32)) for i in range(8)]

    V = at_off("v_rows", [P, TT, A_WIDTH], rg)
    SG = at_off("spatial", [P, A_HEADS, SEQ], rg + 32 * KB)
    YH = at_off("y_high", [P, A_HEADS, SEQ], rg + 32 * KB, F32R)
    YL = at_off("y_low", [P, A_HEADS, SEQ], rg, F32R)
    U = at_off("u_t", [P, 2, 4, SEQ], rg + 64 * KB)
    GT = at_off("g_t", [P, 4, SEQ], rg + 80 * KB)
    WS = at_off("ws_rows", [P, A_HEADS, P], rg + 64 * KB)
    WST = at_off("ws_t", [P, A_HEADS, P], rg + 80 * KB)
    BS = at_off("b_s_all", [P, 2048], r0)
    MTH = at_off("mem_high", [P, KD, N_MEM], rg, F32R)
    MTL = at_off("mem_low", [P, KD, N_MEM], rg + 8 * KB, F32R)
    KVS = at_off("mem_kv_out", [P, 2, 4, N_MEM], rg + 32 * KB)
    MEM = at_off("mem_rows", [P, 2, D], rg + 40 * KB)
    BROW = at_off("bias_rows", [P, BIAS_ALL], rg + 48 * KB)
    HOT = at_off("bucket_hot", [P, BIAS_ALL], rg + 52 * KB)
    RB = at_off("rel_table", [P, 48], rg + 56 * KB)
    bQT = at_off("b_q_t", [P, 4, SEQ], rg)
    bKT = at_off("b_k_t", [P, 4, SEQ], rg + 8 * KB)
    bV = at_off("b_v_rows", [P, TT, 512], rg + 16 * KB)
    bO = [at_off(f"b_o{g}", [P, TT, D], rg + (24 + 16 * g) * KB) for g in range(3)]
    bON = at_off("b_o0_natural", [P, TT, D], rg + 40 * KB)
    bSB = [at_off(f"b_p{i}", [P, 512], rg + (72 + 2 * i) * KB) for i in range(2)]
    bPT = [at_off(f"b_pt{i}", [P, 512], rg + (76 + 2 * i) * KB) for i in range(2)]
    bM = at_off("b_negmax", [P, 3, TT, 16], rg + 80 * KB)
    bD = at_off("b_sums", [P, 3, TT, 16], rg + 80 * KB + 768)
    bE = at_off("b_weights", [P, 3, TT, 16], rg + 80 * KB + 1536)
    bS = at_off("b_norm", [P, TT, 16], rg + 80 * KB + 2304)
    bMN = at_off("b_negmax_natural", [P, TT, 16], rg + 83 * KB)
    bDN = at_off("b_sums_natural", [P, TT, 16], rg + 83 * KB + 256)
    BG = at_off("b_bias", [P, 2048], gb0)
    XWH = at_off("xt_wrap_high", [P, KD, P], r0, F32R)
    XWL = at_off("xt_wrap_low", [P, KD, P], r0 + 4 * KB, F32R)
    bG = at_off("b_gate", [P, TT, D], rg)
    bHH = at_off("b_y_high", [P, KD, SEQ], rg + 40 * KB, F32R)
    bHL = at_off("b_y_low", [P, KD, SEQ], rg + 56 * KB, F32R)
    ZR = at_off("mla_c", [P, TT, 416], r0)
    CTH = at_off("mla_c_high", [P, 3, SEQ], xt0, F32R)
    CTL = at_off("mla_c_low", [P, 3, SEQ], xt0 + 6 * KB, F32R)
    mV = at_off("mla_v", [P, TT, 768], xt0 + 12 * KB)
    RT = at_off("rope_tmp", [P, 4, 192], xt0 + 24 * KB)
    mF = at_off("mla_qk_rows", [P, TT, HEADS, MLA_QD], rg)
    O = at_off("mix_rows", [P, TT, D], rg)
    qT = at_off("mla_q_t", [P, HEADS, SEQ], rg + 18 * KB)
    kT = at_off("mla_k_t", [P, HEADS, SEQ], rg + 42 * KB)
    mSB = [at_off(f"m_p{i}", [P, 512], rg + (66 + 2 * i) * KB) for i in range(2)]
    mPT = [at_off(f"m_pt{i}", [P, 512], rg + (70 + 2 * i) * KB) for i in range(2)]
    mCM = at_off("mla_causal", [P, 896], rg + 74 * KB)
    mKV = at_off("mla_mem_kv", [P, 4, N_MEM], rg + 78 * KB)
    KR = at_off("mla_k_rope", [P, TT, MLA_ROPE], rg + 82 * KB)
    mQM = at_off("mla_q_mem", [P, 2, SEQ], rg + 82 * KB + 512)
    COS = at_off("cos", [P, TT, 16], rg + 87 * KB)
    SIN = at_off("sin", [P, TT, 16], rg + 87 * KB + 256)
    mHH = at_off("mix0_high", [P, KD, SEQ], rg + 18 * KB, F32R)
    mHL = at_off("mix0_low", [P, KD, SEQ], rg + 42 * KB, F32R)
    KVF = at_off("kv_t", [P, 4, SEQ], rg)
    VV = at_off("kv_v_rows", [P, TT, 2, P], rg + 8 * KB)
    W1 = [at_off(f"cmp_w1_{j}", [P, CMP_LEN, CMP_HIDDEN], rg + (12 + 32 * j) * KB) for j in range(2)]
    FZ = at_off("cmp_blocks", [P, 2, CMP_LEN, N_CMP], rg + 76 * KB)
    POS = at_off("cmp_pos_t", [P, 2, CMP_LEN], rg + 84 * KB)
    B1 = at_off("cmp_b1_t", [P, 2, 2], rg + 84 * KB + 512)
    W2 = at_off("cmp_w2_t", [P, 2, 2, 64], rg + 85 * KB)
    H1 = at_off("cmp_hidden", [P, 2, 2, 2, 4, NC], rg + 44 * KB)
    nQT = at_off("nsa_q_t", [P, 6, SEQ], rg + 16 * KB)
    nQM = at_off("nsa_q_mem", [P, 2, SEQ], rg + 28 * KB)
    nK = at_off("nsa_k_t", [P, 2, SEQ], rg + 32 * KB)
    nV = at_off("nsa_v_rows", [P, TT, 2, P], rg + 36 * KB)
    nG = at_off("nsa_gates", [P, TT, HEADS, 3], rg + 40 * KB)
    nSB = [at_off(f"n_p{i}", [P, 512], rg + (41 + 2 * i) * KB) for i in range(2)]
    nPT = [at_off(f"n_pt{i}", [P, 512], rg + (45 + 2 * i) * KB) for i in range(2)]
    nAB = [at_off(f"n_bias{i}", [P, 896], rg + 49 * KB + 3584 * i) for i in range(2)]
    nCM = at_off("nsa_causal", [P, 896], rg + 56 * KB)
    nDI = at_off("nsa_dist", [P, 896], rg + 56 * KB + 3584)
    nKV = at_off("nsa_mem_kv", [P, 4, N_MEM], rg + 63 * KB)
    nCD = at_off("cmp_dist", [P, TT, NC], rg + 67 * KB)
    nCN = at_off("cmp_mask_add", [P, TT, NC], rg + 67 * KB + 512)
    nC1 = at_off("cmp_mask", [P, TT, NC], rg + 68 * KB)
    nBC = at_off("cmp_bias", [P, TT, HEADS, NC], rg + 69 * KB)
    nCP = at_off("cmp_p", [P, HEADS, NC], rg + 75 * KB)
    nCT = at_off("cmp_pt", [P, 3, P], rg + 77 * KB)
    nHH = at_off("mix1_high", [P, KD, SEQ], rg + 16 * KB, F32R)
    nHL = at_off("mix1_low", [P, KD, SEQ], rg + 56 * KB, F32R)

    slopes = alibi_slopes(HEADS)
    MW = 384

    ROWS = {"s0": ("pre", 0), "s1": ("post_pre", 0), "s2": ("post", 0),
            "l00": ("ln", 0.5 / ALPHA), "l01": ("ln", 1.0 / ALPHA), "l02": ("ln", 0.5 / ALPHA),
            "l10": ("ln", 0.5 / ALPHA), "l11": ("ln", 1.0 / ALPHA), "l12": ("ln", 0.5 / ALPHA)}
    GAINS = {"s0": (A["norm_pre"][0], None), "s1": (A["norm_post"][0], A["norm_pre"][1]),
             "s2": (A["norm_post"][1], None)}
    for l in range(2):
        for i in range(3):
            GAINS[f"l{l}{i}"] = (A["ln_g_2"][l, i], A["ln_b_2"][l, i])
    SS = small[:, 0:16]
    RS = small[:, 16:32]
    RM = small[:, 32:48]
    HALF = small[:, 48:64]
    BN = small[:, 64:64 + 96]
    NM = small[:, 192:208]
    DS = small[:, 208:224]
    RD = small[:, 224:240]
    CM_ = small[:, 256:272]
    CD_ = small[:, 272:288]
    CF_ = small[:, 288:304]
    DG = small[:, 304:320]

    def row(vec, n):
        return vec.rearrange("(a d) -> a d", a=1).to_broadcast([P, n])

    def task(scores, view, scale, bias, heads, turns, values, finish, width):
        return dict(scores=scores, view=view, scale=scale, bias=bias, heads=heads, turns=turns,
                    values=values, finish=finish, width=width)

    def heads_of(rows, t, h0, n):
        return rows[:, t, :].rearrange("p (h d) -> p h d", d=64)[:, h0:h0 + 2 * n - 1:2, :]

    def dilated_tasks(g, hf):
        out = []
        if g == 0:
            for b in range(TT):
                lo, hi = (64 if b == 0 else 0), (192 if b == TT - 1 else 256)
                for j in range(4):
                    sc, hd, tn, va = [], [], [], []
                    for e in range(2):
                        h = 4 * (j // 2) + 2 * e + j % 2
                        s = 64 * (j % 2)
                        sc.append((e * 256 + lo, e * 256 + hi, bQT[s:s + 64, h // 2, P * b:P * b + P],
                                   bKT[s:s + 64, h // 2, P * b - 64 + lo:P * b - 64 + hi]))
                        gh = hf * 8 + h
                        hd.append((e * 256 + lo, e * 256 + hi, bMN[:, b, gh:gh + 1], bDN[:, b, gh:gh + 1]))
                        tn += [(e * 256 + P * w, P) for w in range(2)]
                        va.append((e * 64, [(P, (e * 2 + w) * P, bV[:, (b + w) % TT, h * 64:h * 64 + 64])
                                            for w in range(2)]))
                    h0 = 4 * (j // 2) + j % 2
                    g0 = hf * 8 + h0
                    out.append(task(sc, lambda t, lo=lo, hi=hi: t.rearrange("p (e c) -> p e c", e=2)[:, :, lo:hi],
                                    B_SCALE, BG[:].rearrange("p (h c) -> p h c", h=8)[:, h0:h0 + 3:2, lo:hi], hd, tn, va,
                                    ("copy", heads_of(bON, b, g0, 2), 128),
                                    (bMN[:, b, g0:g0 + 3:2], 2, b)))
            return out
        for r in range(TT):
            for q in range(2):
                sc, hd, tn, va = [], [], [], []
                for e in range(4):
                    h = 2 * e + q
                    j, s = e, 64 * q
                    sc.append((e * P, e * P + P, bQT[s:s + 64, j, r:SEQ:4], bKT[s:s + 64, j, r:SEQ:4]))
                    gh = hf * 8 + h
                    hd.append((e * P, e * P + P, bM[:, g, r, gh:gh + 1], bD[:, g, r, gh:gh + 1]))
                    tn.append((e * P, P))
                    va.append((e * 64, [(P, e * P, bV[:, r, h * 64:h * 64 + 64])]))
                g0 = hf * 8 + q
                out.append(task(sc, lambda t: t.rearrange("p (e c) -> p e c", e=4), B_SCALE,
                                BG[:, 0:1024].rearrange("p (h c) -> p h c", h=8)[:, q:8:2, :], hd, tn, va,
                                ("copy", heads_of(bO[g], r, g0, 4), 256),
                                (bM[:, g, r, g0:g0 + 7:2], 4, r)))
        return out

    def row_task(n, q, k, scale, bias, W, v, finish):
        s = n % 4
        return task([(0, W, q, k)], lambda t, W=W: t[:, 0:W], scale, bias,
                    [(0, W, NM[:, s:s + 1], DS[:, s:s + 1])],
                    [(P * w, P) for w in range(W // P)],
                    [(0, [(P, P * w, v(w)) for w in range(W // P)])], finish,
                    (NM[:, s:s + 1], 1, 0))

    def mem_tasks(n0, q_mem, kv):
        out = []
        for t in range(TT):
            for h in range(4):
                j, s = h // 2, 64 * (h % 2)
                out.append(row_task(n0 + len(out), q_mem[s:s + 64, j, P * t:P * t + P], kv[s:s + 64, j, :],
                                    HD_SCALE, None, N_MEM,
                                    lambda w, h=h: kv[:, 2 + w, h * 64:h * 64 + 64],
                                    ("norm", O[:, t, 768 + h * 64:832 + h * 64], None)))
        return out

    def mla_tasks():
        out = []
        for t in range(TT):
            for h in range(HEADS):
                W = P * (t + 1)
                out.append(row_task(len(out), qT[0:96, h, P * t:P * t + P], kT[0:96, h, 0:W], MLA_SCALE,
                                    mCM[:, MW - P * t:MW - P * t + W], W,
                                    lambda w, h=h: mV[:, w, h * 64:h * 64 + 64],
                                    ("norm", O[:, t, h * 64:h * 64 + 64], None)))
        return out + mem_tasks(len(out), mQM, mKV)

    def nsa_tasks():
        out = []
        for h in range(HEADS):
            g, i = h // 6, h % 6
            for t in range(TT):
                for br in range(2):
                    W = P * (t + 1)
                    out.append(row_task(len(out), nQT[64 * g:64 * g + 64, i, P * t:P * t + P],
                                        nK[64 * g:64 * g + 64, br, 0:W], HD_SCALE,
                                        nAB[h % 2][:, MW - P * t:MW - P * t + W], W,
                                        lambda w, g=g, br=br: nV[:, w, br, g * 64:g * 64 + 64],
                                        ("add", O[:, t, h * 64:h * 64 + 64], nG[:, t, h, br + 1:br + 2])))
        return out + mem_tasks(len(out), nQM, nKV)

    ATT = {}
    for g in range(3):
        for hf in range(2):
            ATT[("b", g, hf)] = (dilated_tasks(g, hf), bSB, bPT)
    ATT["mla"] = (mla_tasks(), mSB, mPT)
    ATT["nsa"] = (nsa_tasks(), nSB, nPT)

    mixes = {"b": (bO[0], bHH, bHL, True), "mla": (O, mHH, mHL, False), "nsa": (O, nHH, nHL, False)}

    block = ctx.enter_context(nc.Block())

    @block.sync
    def _(sp):
        sp.dma_start(ident[:], A["ident"]).then_inc(sem["ident_loaded"], step("ident_loaded", by=16))
        for t in range(TT):
            sp.dma_start(X[:, t, :], A["x"][t * P:(t + 1) * P, :]).then_inc(sem[f"x_loaded{t}"], step(f"x_loaded{t}", by=16))
        for g, pieces in enumerate(panels):
            if g >= 2:
                sp.wait_ge(sem["w_low_ready"], at("w_low_ready", g - 2))
            for off, n, pitch, w, src in pieces:
                if pitch == w:
                    dst = RAW[g % 2][:, off:off + n * w].rearrange("p (n w) -> p n w", n=n)
                else:
                    dst = bass.AP(RAW[g % 2], off, [[2048, P], [pitch, n], [1, w]])
                sp.dma_start(dst, src).then_inc(sem[f"panel_loaded{g % 2}"], step(f"panel_loaded{g % 2}", g, by=16))
        for t in range(TT):
            sp.wait_ge(sem["rows_done"], at("rows_done", ("l12", t)))
            sp.dma_start(out[t * P:(t + 1) * P, :], X[:, t, :]).then_inc(sem["stored"], step("stored", by=16))
        sp.wait_ge(sem["stored"], 16 * TT)

    @block.tensor
    def _(pe):
        def mm3(o, lh, ll, rh, rl, start, stop):
            pe.matmul(o, lh, rh, start=start, stop=False, skip_group_check=True)
            pe.matmul(o, lh, rl, start=False, stop=False, skip_group_check=True)
            return pe.matmul(o, ll, rh, start=False, stop=stop, skip_group_check=True)

        def early_half(name, jobs, s):
            g = ids[name][0]
            pe.wait_ge(sem["w_low_ready"], at("w_low_ready", g))
            for a in (0, 1):
                pe.wait_ge(sem["xt_ready"], at("xt_ready", (s, 2 * a + 1)))
                cols = slice(256 * a, 256 * a + 256)
                for o, operands in jobs:
                    for kk in range(4):
                        lh, ll, rh, rl = operands(kk, kk, WH[g % 2], WL[g % 2])
                        pe.matmul(o[:, cols], lh, rh[:, cols], start=a == 0 and kk == 0, stop=False,
                                  skip_group_check=True)
                        pe.matmul(o[:, cols], lh, rl[:, cols], start=False, stop=False, skip_group_check=True)
                        ins = pe.matmul(o[:, cols], ll, rh[:, cols], start=False, stop=False, skip_group_check=True)
            ins.then_inc(sem["product_done"], step("product_done", ("panel", g)))

        def product(name, nk, jobs, free, after_rows=None):
            gs = ids[name]
            for i, g in enumerate(gs):
                if after_rows and i == 0:
                    early_half(name, jobs, after_rows)
                    continue
                pe.wait_ge(sem["w_low_ready"], at("w_low_ready", g))
                for j, (o, operands) in enumerate(jobs):
                    if i == 0:
                        free(j)
                    for kk in range(nk):
                        ins = mm3(o, *operands(kk, i * nk + kk, WH[g % 2], WL[g % 2]),
                                  i == 0 and kk == 0, i == len(gs) - 1 and kk == nk - 1)
                    last = i == len(gs) - 1
                    labels = ([("acc", name, j)] if last else []) + ([("panel", g)] if j == len(jobs) - 1 else [])
                    if labels:
                        ins.then_inc(sem["product_done"], step("product_done", *labels))

        def feature(w, c, xh, xl, n=SEQ):
            def operands(kk, k, wh, wl):
                a = kk * w + c
                return wh[:, a:a + P], wl[:, a:a + P], xh[:, k, 0:n], xl[:, k, 0:n]
            return operands

        def token(w, c, n, tokens, xh, xl):
            def operands(kk, k, wh, wl):
                a = kk * w + c
                return xh[:, k, tokens], xl[:, k, tokens], wh[:, a:a + n], wl[:, a:a + n]
            return operands

        def down(name, kt, hh, hl, ready, free, s):
            gs = ids[name]

            def accumulate(g, i, kk, t, start, stop):
                k = 2 * i + kk
                for half in range(2):
                    a = kk * D + half * 512
                    ins = mm3(ps[2 * t + half][:], hh[:, k, t * P:t * P + P], hl[:, k, t * P:t * P + P],
                              WH[g % 2][:, a:a + 512], WL[g % 2][:, a:a + 512], start, stop)
                return ins
            free()
            for i, g in enumerate(gs[:-2]):
                pe.wait_ge(sem["w_low_ready"], at("w_low_ready", g))
                for kk in range(2):
                    ready(2 * i + kk)
                    for t in range(TT):
                        ins = accumulate(g, i, kk, t, i == 0 and kk == 0, False)
                ins.then_inc(sem["product_done"], step("product_done", ("panel", g)))
            for t in range(TT):
                if t >= 2:
                    turn_row(s, t - 2)
                for i in (len(gs) - 2, len(gs) - 1):
                    g = gs[i]
                    if t == 0:
                        pe.wait_ge(sem["w_low_ready"], at("w_low_ready", g))
                    for kk in range(2):
                        ready(2 * i + kk)
                        ins = accumulate(g, i, kk, t, False, i == len(gs) - 1 and kk == 1)
                labels = [("acc", name, t)]
                if t == TT - 1:
                    labels += [("panel", gs[-2]), ("panel", gs[-1])]
                ins.then_inc(sem["product_done"], step("product_done", *labels))
            for t in (TT - 2, TT - 1):
                turn_row(s, t)

        def turn_row(s, t):
            if s == "l12":
                return
            kind = ROWS[s][0]
            pe.wait_ge(sem["rows_done"], at("rows_done", (s, t)))
            src = R[t % 2][:, :] if kind in ("pre", "post_pre") else X[:, t, :]
            for k in range(KD):
                ins = pe.transpose(ps[2 * t + k // 4][:, (k % 4) * P:(k % 4 + 1) * P],
                                   src[:, k * P:(k + 1) * P], ident[:])
            ins.then_inc(sem["turned"], step("turned", (s, t)))

        def attend(name):
            tasks = ATT[name][0]
            SBs, PTs = ATT[name][1:]
            N = len(tasks)
            for n in range(N + 2):
                if n < N:
                    tk = tasks[n]
                    if n >= 2:
                        pe.wait_ge(sem["masked"], at("masked", (name, n - 2)))
                    for a, b, q, k in tk["scores"]:
                        ins = pe.matmul(ps[n % 2][:, a:b], q, k, start=True, stop=True)
                    ins.then_inc(sem["scored"], step("scored", (name, n)))
                if 1 <= n <= N:
                    m = n - 1
                    pe.wait_ge(sem["exp_done"], at("exp_done", (name, m)))
                    if m >= 2:
                        pe.wait_ge(sem["pt_copied"], at("pt_copied", (name, m - 2)))
                    for i, (a, w) in enumerate(tasks[m]["turns"]):
                        ins = pe.transpose(ps[2 + m % 2][0:w, i * P:(i + 1) * P], SBs[m % 2][:, a:a + w], ident[:])
                    ins.then_inc(sem["p_turned"], step("p_turned", (name, m)))
                if n >= 2:
                    m = n - 2
                    pe.wait_ge(sem["pt_copied"], at("pt_copied", (name, m)))
                    if m >= 2:
                        pe.wait_ge(sem["o_read"], at("o_read", (name, m - 2)))
                    for c, parts in tasks[m]["values"]:
                        for i, (K, a, v) in enumerate(parts):
                            ins = pe.matmul(ps[4 + m % 2][:, c:c + 64], PTs[m % 2][0:K, a:a + P], v,
                                            start=i == 0, stop=i == len(parts) - 1)
                    ins.then_inc(sem["weighted"], step("weighted", (name, m)))

        def after_attention(name):
            N = len(ATT[name][0])
            pe.wait_ge(sem["masked"], at("masked", (name, N - 1)))
            pe.wait_ge(sem["pt_copied"], at("pt_copied", (name, N - 1)))
            pe.wait_ge(sem["o_read"], at("o_read", (name, N - 1)))

        def turn_mix(name):
            src = mixes[name][0]
            for t in range(TT):
                pe.wait_ge(sem["mix_ready"], at("mix_ready", (name, t)))
                for k in range(KD):
                    ins = pe.transpose(ps[2 * t + k // 4][:, (k % 4) * P:(k % 4 + 1) * P],
                                       src[:, t, k * P:(k + 1) * P], ident[:])
                ins.then_inc(sem["turned"], step("turned", (name, t)))

        pe.wait_ge(sem["ident_loaded"], at("ident_loaded"))
        pe.wait_ge(sem["hot_loaded"], at("hot_loaded"))
        pe.wait_ge(sem["table_ones"], at("table_ones"))
        for g in range(3):
            o = ps[0][0:16, 0:384] if g == 0 else ps[1][0:16, (g - 1) * 256:g * 256]
            ins = pe.matmul(o, RB[0:33, 16 * g:16 * g + 16], HOT[0:33, BIAS_AT[g]:BIAS_AT[g] + BIAS_W[g]],
                            start=True, stop=True)
        ins.then_inc(sem["bias_multiplied"], step("bias_multiplied"))
        pe.wait_ge(sem["mem_loaded"], at("mem_loaded"))
        for k in range(KD):
            for m in range(2):
                ins = pe.transpose(ps[2 + k // 2][:, (k % 2) * 256 + m * P:(k % 2) * 256 + m * P + P],
                                   MEM[:, m, k * P:(k + 1) * P], ident[:])
            if k % 2:
                ins.then_inc(sem["mem_turned"], step("mem_turned", k // 2))
        pe.wait_ge(sem["mem_split"], at("mem_split", 3))
        pe.wait_ge(sem["bias_copied"], at("bias_copied"))
        for l in range(2):
            banks = (0, 1, 6, 7) if l == 0 else (2, 3, 4, 5)
            jobs = [(ps[banks[j]][:, 0:256], feature(512, j * P, MTH, MTL, N_MEM)) for j in range(2)]
            jobs += [(ps[banks[2 + m]][:, 0:256], token(512, 256, 256, slice(m * P, m * P + P), MTH, MTL))
                     for m in range(2)]
            product(("mem", l), 4, jobs, lambda j: None)
        pe.wait_ge(sem["ws_loaded"], at("ws_loaded"))
        pe.wait_ge(sem["mem_kv_copied"], at("mem_kv_copied", (0, 3)))
        pe.wait_ge(sem["mem_kv_copied"], at("mem_kv_copied", (1, 3)))
        for h in range(A_HEADS):
            ins = pe.transpose(ps[h // 4][:, (h % 4) * P:(h % 4 + 1) * P], WS[:, h, :], ident[:])
            if h % 4 == 3:
                ins.then_inc(sem["ws_turned"], step("ws_turned", h // 4))
        pe.wait_ge(sem["ws_copied"], at("ws_copied", 3))
        for t in range(TT):
            turn_row("s0", t)

        setA, setB = (0, 1, 2, 3), (4, 5, 6, 7)

        def tile(t):
            return slice(t * P, t * P + P)

        for c in range(4):
            banks = setA if c % 2 == 0 else setB
            product(("v", c), 4, [(ps[banks[t]][:], token(512, 0, 512, tile(t), XTH, XTL)) for t in range(TT)],
                    lambda j, c=c: pe.wait_ge(sem["v_read"], at("v_read", (c - 2, j))) if c >= 2 else
                    (pe.wait_ge(sem["xt_ready"], at("xt_ready", ("s0", j))) if c == 0 else None))
        for c in range(2):
            banks = setA if c % 2 == 0 else setB
            product(("u", c), 4, [(ps[banks[j]][:], feature(512, j * P, XTH, XTL)) for j in range(4)],
                    lambda j, c=c: pe.wait_ge(sem["v_read"], at("v_read", (c + 2, j))))
        for h in range(A_HEADS):
            b = h % 8
            pe.wait_ge(sem["v_normed"], at("v_normed", h // 8))
            if h < 8:
                pe.wait_ge(sem["u_read"], at("u_read", (h // 4, h % 4)))
            else:
                pe.wait_ge(sem["spatial_read"], at("spatial_read", h - 8))
            for c in range(TT):
                ins = pe.matmul(ps[b][:, tile(c)], V[:, c, h * P:h * P + P], WST[:, h, :], start=True, stop=True)
            ins.then_inc(sem["spatial_done"], step("spatial_done", h))
        for c in range(4):
            if c >= 2:
                product(("u", c), 4, [(ps[setB[j]][:], feature(512, j * P, XTH, XTL)) for j in range(4)],
                        lambda j, c=c: pe.wait_ge(sem["spatial_read"], at("spatial_read", 12 + j)) if c == 2 else pe.wait_ge(sem["u_read"], at("u_read", (c - 1, j))))
            product(("g", c), 4, [(ps[setA[j]][:], feature(512, j * P, XTH, XTL)) for j in range(4)],
                    lambda j, c=c: pe.wait_ge(sem["spatial_read"], at("spatial_read", 8 + j)) if c == 0 else pe.wait_ge(sem["g_read"], at("g_read", (c - 1, j))))

        def gmlp_free():
            pe.wait_ge(sem["u_read"], at("u_read", (3, 3)))
            pe.wait_ge(sem["g_read"], at("g_read", (3, 3)))
        down("a_out", 16, YH, YL, lambda k: pe.wait_ge(sem["y_split"], at("y_split", k)), gmlp_free, "s1")

        for g in range(3):
            for hf in range(2):
                prev = None if (g, hf) == (0, 0) else (("b", g, hf - 1) if hf else ("b", g - 1, 1))
                if prev:
                    after_attention(prev)
                product(("b", g, hf, "q"), 4, [(ps[setA[j]][:], feature(512, j * P, XTH, XTL)) for j in range(4)],
                        lambda j: None, "s1" if (g, hf) == (0, 0) else None)
                product(("b", g, hf, "k"), 4, [(ps[setB[j]][:], feature(512, j * P, XTH, XTL)) for j in range(4)],
                        lambda j: None)
                if g == 0:
                    pe.wait_ge(sem["wrap_ready"], at("wrap_ready"))
                    jobs = [(ps[setA[0]][:], token(512, 0, 512, slice(0, P), XWH, XWL))]
                    jobs += [(ps[setA[t]][:], token(512, 0, 512, slice(t * P - 64, t * P + 64), XTH, XTL))
                             for t in range(1, TT)]
                else:
                    jobs = [(ps[setA[t]][:], token(512, 0, 512, slice(t, SEQ, 4), XTH, XTL)) for t in range(TT)]
                product(("b", g, hf, "v"), 4, jobs, lambda j, g=g, hf=hf: pe.wait_ge(sem["bq_read"], at("bq_read", (g, hf, j))))
                pe.wait_ge(sem["bk_read"], at("bk_read", (g, hf, 3)))
                pe.wait_ge(sem["bv_read"], at("bv_read", (g, hf, 3)))
                attend(("b", g, hf))
        after_attention(("b", 2, 1))
        for c in range(2):
            product(("b_gate", c), 4, [(ps[4 * c + t][:], token(512, 0, 512, slice(t, SEQ, 4), XTH, XTL))
                                       for t in range(TT)], lambda j: None)
        pe.wait_ge(sem["bgate_read"], at("bgate_read", 1))
        turn_mix("b")
        down("b_out", 8, bHH, bHL, lambda k: None, lambda: pe.wait_ge(sem["mix_split"], at("mix_split", ("b", TT - 1))), "s2")

        def ffn(l, i, s, then):
            f = (l, i)
            for c in range(5):
                product(("gate", l, i, c), 4, [(ps[setA[j]][:], feature(512, j * P, XTH, XTL)) for j in range(4)],
                        lambda j, c=c: pe.wait_ge(sem["gate_read"], at("gate_read", (f, c - 1, j))) if c else None,
                        s if c == 0 else None)
                product(("up", l, i, c), 4, [(ps[setB[j]][:], feature(512, j * P, XTH, XTL)) for j in range(4)],
                        lambda j, c=c: pe.wait_ge(sem["up_read"], at("up_read", (f, c - 1, j))) if c else None)
            product(("last", l, i), 4, [(ps[setA[j]][:], feature(512, j * P, XTH, XTL)) for j in range(4)],
                    lambda j: pe.wait_ge(sem["gate_read"], at("gate_read", (f, 4, j))))

            def free():
                pe.wait_ge(sem["up_read"], at("up_read", (f, 5, 1)))
            down(("down", l, i), KF, HTH, HTL,
                 lambda k: pe.wait_ge(sem["hidden_split"], at("hidden_split", (f, k // 4))) if k % 4 == 0 else None, free, then)

        ffn(0, 0, "s2", "l00")
        product("mla_in", 4, [(ps[t][:, 0:416], token(416, 0, 416, tile(t), XTH, XTL)) for t in range(TT)],
                lambda j: pe.wait_ge(sem["xt_ready"], at("xt_ready", ("l00", j))))
        product("mla_mem", 8, [(ps[4 + j][:], feature(256, j * P, XTH, XTL)) for j in range(2)], lambda j: None)
        for t in range(TT):
            pe.wait_ge(sem["c_normed"], at("c_normed", t))
            if t == 0:
                pe.wait_ge(sem["c_read"], at("c_read", TT - 1))
            for j in range(3):
                ins = pe.transpose(ps[j][:, tile(t)], ZR[:, t, j * P:(j + 1) * P], ident[:])
        ins.then_inc(sem["c_turned"], step("c_turned"))
        pe.wait_ge(sem["c_split"], at("c_split", 2))
        pe.wait_ge(sem["qmem_read"], at("qmem_read", 1))
        product("uq", 2, [(ps[2 * t + n][:], token(1024, 512 * n, 512, tile(t), CTH, CTL))
                          for t in range(TT) for n in range(2)], lambda j: None)
        product("uq_tail", 2, [(ps[2 * t][:, 0:128], token(128, 0, 128, tile(t), CTH, CTL)) for t in range(TT)],
                lambda j: pe.wait_ge(sem["uq_read"], at("uq_read", (j, 0))))
        for which in ("q", "k"):
            if which == "k":
                def kv_operands(t, n):
                    def operands(kk, k, wh, wl):
                        return (CTH[:, 2, tile(t)], CTL[:, 2, tile(t)], wh[:, n * 512:n * 512 + 512],
                                wl[:, n * 512:n * 512 + 512])
                    return operands

                def kv_free(j):
                    pe.wait_ge(sem["heads_turned"], at("heads_turned", ("q", 11)))
                    if j >= 8:
                        pe.wait_ge(sem["ukv_read_k"], at("ukv_read_k", j - 8))
                        pe.wait_ge(sem["ukv_read_v"], at("ukv_read_v", j - 8))
                product("ukv", 1, [(ps[(3 * t + n) % 8][:], kv_operands(t, n)) for t in range(TT) for n in range(3)],
                        kv_free)
                pe.wait_ge(sem["ukv_read_v"], at("ukv_read_v", 11))
            for h in range(HEADS):
                if which == "q" and h == 0:
                    pe.wait_ge(sem["uq_tail_read"], at("uq_tail_read", 3))
                    pe.wait_ge(sem["uq_read"], at("uq_read", (3, 1)))
                if h == 0:
                    pe.wait_ge(sem["roped"], at("roped", which))
                if h >= 8:
                    pe.wait_ge(sem["heads_turned"], at("heads_turned", (which, h - 8)))
                for t in range(TT):
                    ins = pe.transpose(ps[h % 8][0:96, tile(t)], mF[:, t, h, :], ident[:])
                ins.then_inc(sem["head_turned"], step("head_turned", (which, h)))
        pe.wait_ge(sem["heads_turned"], at("heads_turned", ("k", 11)))
        pe.wait_ge(sem["mix_const0"], at("mix_const0"))
        pe.wait_ge(sem["mem_kv_back"], at("mem_kv_back", 0))
        attend("mla")
        after_attention("mla")
        turn_mix("mla")
        down(("w_out", 0), 8, mHH, mHL, lambda k: None, lambda: pe.wait_ge(sem["mix_split"], at("mix_split", ("mla", TT - 1))), "l01")
        ffn(0, 1, "l01", "l02")


        def shared_product(name, w, f_jobs, t_bank, t_col):
            gs = ids[name]
            for g in gs:
                pe.wait_ge(sem["w_low_ready"], at("w_low_ready", g))
            for b, c in f_jobs:
                for i, g in enumerate(gs):
                    for kk in range(4):
                        ins = mm3(ps[b][:], *feature(w, c, XTH, XTL)(kk, 4 * i + kk, WH[g % 2], WL[g % 2]),
                                  i == 0 and kk == 0, i == 1 and kk == 3)
            for t in range(TT):
                for i, g in enumerate(gs):
                    for kk in range(4):
                        ins = mm3(ps[t_bank][:, tile(t)],
                                  *token(w, t_col, 128, tile(t), XTH, XTL)(kk, 4 * i + kk, WH[g % 2], WL[g % 2]),
                                  i == 0 and kk == 0, i == 1 and kk == 3)
            ins.then_inc(sem["product_done"], step("product_done", ("acc", name, 0), ("panel", gs[0]), ("panel", gs[1])))

        pe.wait_ge(sem["xt_ready"], at("xt_ready", ("l02", TT - 1)))
        shared_product("kv_a", 512, [(0, 0), (1, 128), (2, 256)], 3, 384)
        shared_product("kv_b", 256, [(4, 0)], 5, 128)
        pe.wait_ge(sem["w1_loaded"], at("w1_loaded"))
        pe.wait_ge(sem["blocks_ready"], at("blocks_ready"))
        for j in range(2):
            for g in range(2):
                for ht in range(2):
                    n = 2 * j + ht
                    for l in range(CMP_LEN):
                        ins = pe.matmul(ps[6 + g][:, n * NC:n * NC + N_CMP], W1[j][64 * g:64 * g + 64, l, ht * P:(ht + 1) * P],
                                        FZ[64 * g:64 * g + 64, j, l, :], start=l == 0, stop=l == CMP_LEN - 1)
        ins.then_inc(sem["cmp_hidden_done"], step("cmp_hidden_done"))
        pe.wait_ge(sem["cmp_hidden_ready"], at("cmp_hidden_ready"))
        pe.wait_ge(sem["kv_copied"], at("kv_copied"))
        for g in range(2):
            for ht in range(2):
                pe.matmul(ps[4][64 * g:64 * g + 64, 0:NC], W2[:, 0, ht, :], H1[:, 0, g, ht, 0, :],
                          start=ht == 0, stop=ht == 1)
        for g in range(2):
            for ht in range(2):
                ins = pe.matmul(ps[5][:, g * 64:64 + g * 64],
                                H1[:, 1, g, ht].rearrange("p r n -> p (r n)"), W2[:, 1, ht, :],
                                start=ht == 0, stop=ht == 1)
        ins.then_inc(sem["cmp_done"], step("cmp_done"))
        pe.wait_ge(sem["cmp_kept"], at("cmp_kept"))
        ffn(1, 0, "l02", "l10")

        product("nsa_a", 4, [(ps[setA[j]][:], feature(512, j * P, XTH, XTL)) for j in range(4)], lambda j: None, "l10")
        product("nsa_b", 4, [(ps[setB[j]][:], feature(512, j * P, XTH, XTL)) for j in range(4)], lambda j: None)
        product("nsa_gates", 8, [(ps[t][:, 0:36], token(36, 0, 36, tile(t), XTH, XTL)) for t in range(TT)],
                lambda j: pe.wait_ge(sem["nq_read"], at("nq_read", ("a", j))))
        pe.wait_ge(sem["nsa_const"], at("nsa_const"))
        pe.wait_ge(sem["ngates_read"], at("ngates_read", 3))
        pe.wait_ge(sem["nq_read"], at("nq_read", ("b", 3)))
        for t in range(TT):
            for h in range(HEADS):
                g, i = h // 6, h % 6
                ins = pe.matmul(ps[g][:, i * NC:i * NC + NC], nQT[64 * g:64 * g + 64, i, tile(t)],
                                KCT[64 * g:64 * g + 64, :], start=True, stop=True)
            ins.then_inc(sem["cmp_scored"], step("cmp_scored", t))
            pe.wait_ge(sem["cmp_p_ready"], at("cmp_p_ready", t))
            for u in range(3):
                ins = pe.transpose(ps[2][:, u * P:(u + 1) * P],
                                   nCP[:, 4 * u:4 * u + 4, :].rearrange("p h n -> p (h n)"), ident[:])
            ins.then_inc(sem["cmp_p_turned"], step("cmp_p_turned", t))
            pe.wait_ge(sem["cmp_pt_copied"], at("cmp_pt_copied", t))
            if t:
                pe.wait_ge(sem["cmp_o_read"], at("cmp_o_read", t - 1))
            for h in range(HEADS):
                u, e, g = h // 4, h % 4, h // 6
                ins = pe.matmul(ps[4 + e][:, u * 64:u * 64 + 64], nCT[32 * e:32 * e + 32, u, :],
                                VC4[32 * e:32 * e + 32, g, :], start=True, stop=True)
            ins.then_inc(sem["cmp_weighted"], step("cmp_weighted", t))
        pe.wait_ge(sem["cmp_o_read"], at("cmp_o_read", TT - 1))
        pe.wait_ge(sem["mem_kv_back"], at("mem_kv_back", 1))
        attend("nsa")
        after_attention("nsa")
        turn_mix("nsa")
        down(("w_out", 1), 8, nHH, nHL, lambda k: None, lambda: pe.wait_ge(sem["mix_split"], at("mix_split", ("nsa", TT - 1))), "l11")
        ffn(1, 1, "l11", "l12")

    @block.scalar
    def _(act):
        done = [0]

        def prepare(g):
            while done[0] <= min(g, len(panels) - 1):
                n = done[0]
                act.wait_ge(sem[f"panel_loaded{n % 2}"], at(f"panel_loaded{n % 2}", n))
                if n >= 2:
                    act.wait_ge(sem["product_done"], at("product_done", ("panel", n - 2)))
                w = widths[n]
                act.activation(WH[n % 2][:, 0:w], RAW[n % 2][:, 0:w], ACT.Copy).then_inc(sem["w_high_ready"], step("w_high_ready", n))
                done[0] += 1

        def after(name, j, labels_only=False):
            if j == 0:
                prepare(ids[name][-1] + 1)
            act.wait_ge(sem["product_done"], at("product_done", ("acc", name, j)))

        def split_turned(s, t, hh, perm=False):
            act.wait_ge(sem["turned"], at("turned", (s, t)))
            for b in range(2):
                dst = hh[:, 4 * b:4 * b + 4, t:SEQ:4] if perm else hh[:, 4 * b:4 * b + 4, t * P:(t + 1) * P]
                ins = act.activation(dst, ps[2 * t + b][:].rearrange("p (k n) -> p k n", k=4), ACT.Copy)
            ins.then_inc(sem["turned_high"], step("turned_high", (s, t)))

        def rows(s, y=None):
            kind = ROWS[s][0]
            if y:
                prepare(ids[y][-1])
            for t in range(TT + 1):
                if t < TT:
                    if kind in ("post", "post_pre"):
                        act.wait_ge(sem["product_done"], at("product_done", ("acc", y, t)))
                        if t >= 2 and kind == "post_pre":
                            act.wait_ge(sem["turned"], at("turned", (s, t - 2)))
                        if t >= 2 and kind == "post":
                            act.wait_ge(sem["rows_done"], at("rows_done", (s, t - 2)))
                        for half in range(2):
                            ins = act.activation(R[t % 2][:, 512 * half:512 * half + 512], ps[2 * t + half][:], ACT.Square,
                                                 accum_out=SS[:, 4 * t + half:4 * t + half + 1])
                        ins.then_inc(sem["squared"], step("squared", (s, t)))
                    if kind == "pre":
                        act.wait_ge(sem[f"x_loaded{t}"], at(f"x_loaded{t}"))
                        if t >= 2:
                            act.wait_ge(sem["turned"], at("turned", (s, t - 2)))
                    if kind == "post_pre":
                        act.wait_ge(sem["x_added"], at("x_added", (s, t)))
                    if kind in ("pre", "post_pre"):
                        act.activation(R[t % 2][:], X[:, t, :], ACT.Square,
                                              accum_out=SS[:, 4 * t + 2:4 * t + 3]).then_inc(sem["squared_x"], step("squared_x", (s, t)))
                if y and t == TT - 1:
                    act.wait_ge(sem["product_done"], at("product_done", ("acc", y, t)))
                    prepare(ids[y][-1] + 1)
                if t >= 1 and s != "l12":
                    split_turned(s, t - 1, XTH)
                if y and t == TT - 1:
                    prepare(ids[y][-1] + 2)

        def attend(name):
            tasks, SBs, PTs = ATT[name]
            N = len(tasks)
            for n in range(N + 1):
                if n < N:
                    act.wait_ge(sem["maxed"], at("maxed", (name, n)))
                    for a, b, m, d in tasks[n]["heads"]:
                        ins = act.activation(SBs[n % 2][:, a:b], SBs[n % 2][:, a:b], ACT.Exp, bias=m, accum_out=d)
                    ins.then_inc(sem["exp_done"], step("exp_done", (name, n)))
                if n >= 1:
                    m = n - 1
                    act.wait_ge(sem["p_turned"], at("p_turned", (name, m)))
                    if m >= 2:
                        act.wait_ge(sem["weighted"], at("weighted", (name, m - 2)))
                    w = P * len(tasks[m]["turns"])
                    act.activation(PTs[m % 2][:, 0:w], ps[2 + m % 2][:, 0:w], ACT.Copy).then_inc(sem["pt_copied"], step("pt_copied", (name, m)))

        def turned_mix(name):
            _, hh, _, perm = mixes[name]
            for t in range(TT):
                split_turned(name, t, hh, perm)

        for b in range(4):
            act.wait_ge(sem["mem_turned"], at("mem_turned", b))
            act.activation(MTH[:, 2 * b:2 * b + 2, :], ps[2 + b][:].rearrange("p (k n) -> p k n", k=2), ACT.Copy).then_inc(sem["mem_high"], step("mem_high", b))
        for l in range(2):
            banks = (0, 1, 6, 7) if l == 0 else (2, 3, 4, 5)
            for j in range(4):
                after(("mem", l), j)
                act.activation(KVS[:, l, j, :], ps[banks[j]][:, 0:256], ACT.Copy).then_inc(sem["mem_kv_copied"], step("mem_kv_copied", (l, j)))
            prepare(ids["mem", l][-1] + 2)
        rows("s0")

        for c in range(4):
            for t in range(TT):
                after(("v", c), t)
                act.activation(V[:, t, 512 * c:512 * c + 512], ps[4 * (c % 2) + t][:], ACT.Gelu_apprx_tanh).then_inc(sem["v_read"], step("v_read", (c, t)))
            prepare(ids["v", c][-1] + 2)

        def u_part(c, bank):
            for j in range(4):
                after(("u", c), j)
                if j == 0 and c >= 2:
                    act.wait_ge(sem["y_split"], at("y_split", 4 * (c - 2) + 3))
                act.activation(U[:, c % 2, j, :], ps[bank + j][:], ACT.Gelu_apprx_tanh).then_inc(sem["u_read"], step("u_read", (c, j)))
            prepare(ids["u", c][-1] + 2)

        def g_part(c):
            for j in range(4):
                after(("g", c), j)
                if c == 0:
                    act.wait_ge(sem["spatial_read"], at("spatial_read", 15))
                if c >= 1:
                    act.wait_ge(sem["y_multiplied"], at("y_multiplied", 4 * (c - 1) + j))
                act.activation(GT[:, j, :], ps[j][:], ACT.Silu).then_inc(sem["g_read"], step("g_read", (c, j)))
            for j in range(4):
                h = 4 * c + j
                act.wait_ge(sem["y_multiplied"], at("y_multiplied", h))
                act.activation(YH[:, h, :], U[:, c % 2, j, :], ACT.Copy).then_inc(sem["y_high_ready"], step("y_high_ready", h))
            prepare(ids["g", c][-1] + 2)

        u_part(0, 0)
        u_part(1, 4)
        g_part(0)
        g_part(1)
        u_part(2, 4)
        g_part(2)
        u_part(3, 4)
        g_part(3)
        rows("s1", "a_out")

        act.wait_ge(sem["xt_ready"], at("xt_ready", ("s1", TT - 1)))
        act.wait_ge(sem["rows_done"], at("rows_done", ("s1", TT - 1)))
        for src, dst, a in ((XTH, XWH, SEQ - 64), (XTH, XWH, 0), (XTL, XWL, SEQ - 64), (XTL, XWL, 0)):
            b = 0 if a else 64
            ins = act.activation(dst[:, :, b:b + 64], src[:, :, a:a + 64].bitcast(F32), ACT.Copy)
        ins.then_inc(sem["wrap_ready"], step("wrap_ready"))
        for g in range(3):
            for hf in range(2):
                for j in range(4):
                    after(("b", g, hf, "q"), j)
                    act.activation(bQT[:, j, :], ps[j][:], ACT.Copy).then_inc(sem["bq_read"], step("bq_read", (g, hf, j)))
                prepare(ids["b", g, hf, "q"][-1] + 2)
                for j in range(4):
                    after(("b", g, hf, "k"), j)
                    act.activation(bKT[:, j, :], ps[4 + j][:], ACT.Copy).then_inc(sem["bk_read"], step("bk_read", (g, hf, j)))
                prepare(ids["b", g, hf, "k"][-1] + 2)
                for t in range(4):
                    after(("b", g, hf, "v"), t)
                    act.activation(bV[:, t, :], ps[t][:], ACT.Copy).then_inc(sem["bv_read"], step("bv_read", (g, hf, t)))
                prepare(ids["b", g, hf, "v"][-1] + 2)
                attend(("b", g, hf))
        act.wait_ge(sem["group_diffs"], at("group_diffs"))
        act.activation(bE[:], bE[:], ACT.Exp).then_inc(sem["group_exps"], step("group_exps"))
        for c in range(2):
            for t in range(TT):
                after(("b_gate", c), t)
                ins = act.activation(bG[:, t, 512 * c:512 * c + 512], ps[4 * c + t][:], ACT.Silu)
            ins.then_inc(sem["bgate_read"], step("bgate_read", c))
            prepare(ids["b_gate", c][-1] + 2)
        turned_mix("b")
        rows("s2", "b_out")

        def ffn(l, i):
            f = (l, i)
            for c in range(6):
                gname = ("gate", l, i, c) if c < 5 else ("last", l, i)
                ng = 4 if c < 5 else 2
                for j in range(ng):
                    after(gname, j)
                    if c:
                        act.wait_ge(sem["hidden_split"], at("hidden_split", (f, c - 1)))
                    act.activation(G[:, j, :], ps[j][:], ACT.Silu).then_inc(sem["gate_read"], step("gate_read", (f, c, j)))
                prepare(ids[gname][-1] + 2)
                if c < 5:
                    prepare(ids["up", l, i, c][-1] + 1)
                for j in range(ng):
                    act.wait_ge(sem["up_read"], at("up_read", (f, c, j)))
                    ins = act.activation(HTH[:, 4 * c + j, :], G[:, j, :], ACT.Copy)
                ins.then_inc(sem["hidden_high"], step("hidden_high", (f, c)))
                if c < 5:
                    prepare(ids["up", l, i, c][-1] + 2)

        ffn(0, 0)
        rows("l00", ("down", 0, 0))

        for t in range(TT):
            after("mla_in", t)
            act.activation(ZR[:, t, :], ps[t][:, 0:416], ACT.Copy).then_inc(sem["c_rows"], step("c_rows", t))
            act.wait_ge(sem["c_rows"], at("c_rows", t))
            act.activation(mPT[1][:, 0:128], ZR[:, t, 256:384], ACT.Square, accum_out=SS[:, 4 + t:5 + t])
            act.activation(mPT[0][:, 0:256], ZR[:, t, 0:256], ACT.Square,
                                  accum_out=SS[:, t:t + 1]).then_inc(sem["c_read"], step("c_read", t))
        prepare(ids["mla_in"][-1] + 2)
        for j in range(2):
            after("mla_mem", j)
            act.activation(mQM[:, j, :], ps[4 + j][:], ACT.Copy).then_inc(sem["qmem_read"], step("qmem_read", j))
        prepare(ids["mla_mem"][-1] + 2)
        act.wait_ge(sem["c_turned"], at("c_turned"))
        for j in range(3):
            act.activation(CTH[:, j, :], ps[j][:], ACT.Copy).then_inc(sem["c_high"], step("c_high", j))
        qv = mF[:].rearrange("p t h d -> p t (h d)")
        for t in range(TT):
            for n in range(2):
                after("uq", 2 * t + n)
                act.activation(qv[:, t, 512 * n:512 * n + 512], ps[2 * t + n][:], ACT.Copy).then_inc(sem["uq_read"], step("uq_read", (t, n)))
        prepare(ids["uq"][-1] + 2)
        for t in range(TT):
            after("uq_tail", t)
            act.activation(qv[:, t, 1024:1152], ps[2 * t][:, 0:128], ACT.Copy).then_inc(sem["uq_tail_read"], step("uq_tail_read", t))
        prepare(ids["uq_tail"][-1] + 2)
        for h in range(HEADS):
            act.wait_ge(sem["head_turned"], at("head_turned", ("q", h)))
            act.activation(qT[0:96, h, :], ps[h % 8][0:96, :], ACT.Copy).then_inc(sem["heads_turned"], step("heads_turned", ("q", h)))
        for t in range(TT):
            for n in range(3):
                j = 3 * t + n
                after("ukv", j)
                act.activation(mF[:, t, 4 * n:4 * n + 4, 0:64],
                                      ps[j % 8][:].rearrange("p (h d) -> p h d", h=4)[:, :, 0:64], ACT.Copy).then_inc(sem["ukv_read_k"], step("ukv_read_k", j))
        prepare(ids["ukv"][-1] + 2)
        for h in range(HEADS):
            act.wait_ge(sem["head_turned"], at("head_turned", ("k", h)))
            act.activation(kT[0:96, h, :], ps[h % 8][0:96, :], ACT.Copy).then_inc(sem["heads_turned"], step("heads_turned", ("k", h)))
        attend("mla")
        turned_mix("mla")
        rows("l01", ("w_out", 0))
        ffn(0, 1)
        rows("l02", ("down", 0, 1))

        after("kv_a", 0)
        for j in range(3):
            act.activation(KVF[:, j, :], ps[j][:], ACT.Copy).then_inc(sem["kvf_read"], step("kvf_read", j))
        ins = act.activation(VV[:, :, 0, :], ps[3][:].rearrange("p (t n) -> p t n", t=TT), ACT.Copy)
        ins.then_inc(sem["kvf_read"], step("kvf_read", 3))
        prepare(ids["kv_a"][-1] + 2)
        after("kv_b", 0)
        act.activation(KVF[:, 3, :], ps[4][:], ACT.Copy)
        act.activation(VV[:, :, 1, :], ps[5][:].rearrange("p (t n) -> p t n", t=TT), ACT.Copy).then_inc(sem["kv_copied"], step("kv_copied"))
        prepare(ids["kv_b"][-1] + 2)
        act.wait_ge(sem["cmp_hidden_done"], at("cmp_hidden_done"))
        act.wait_ge(sem["h1_zeroed"], at("h1_zeroed"))
        for j in range(2):
            for g in range(2):
                for ht in range(2):
                    n = 2 * j + ht
                    src = ps[6 + g][:, n * NC:n * NC + N_CMP].rearrange("p (r n) -> p r n", r=1).to_broadcast([P, 4, N_CMP])
                    ins = act.activation(H1[:, j, g, ht, :, 0:N_CMP], src, ACT.Gelu_apprx_tanh, bias=B1[:, j, ht:ht + 1])
        ins.then_inc(sem["cmp_hidden_ready"], step("cmp_hidden_ready"))
        act.wait_ge(sem["cmp_done"], at("cmp_done"))
        act.activation(KCT[:], ps[4][:, 0:NC], ACT.Copy)
        act.activation(VC4[:], ps[5][:, 0:128].rearrange("p (g d) -> p g d", g=2), ACT.Copy).then_inc(sem["cmp_kept"], step("cmp_kept"))
        act.wait_ge(sem["kv_kept"], at("kv_kept"))
        ffn(1, 0)
        rows("l10", ("down", 1, 0))

        for j in range(4):
            after("nsa_a", j)
            act.activation(nQT[:, j, :], ps[j][:], ACT.Copy).then_inc(sem["nq_read"], step("nq_read", ("a", j)))
        prepare(ids["nsa_a"][-1] + 2)
        for j in range(4):
            after("nsa_b", j)
            dst = nQT[:, 4 + j, :] if j < 2 else nQM[:, j - 2, :]
            act.activation(dst, ps[4 + j][:], ACT.Copy).then_inc(sem["nq_read"], step("nq_read", ("b", j)))
        prepare(ids["nsa_b"][-1] + 2)
        for t in range(TT):
            after("nsa_gates", t)
            act.activation(nG[:, t], ps[t][:, 0:36].rearrange("p (h b) -> p h b", b=3), ACT.Sigmoid).then_inc(sem["ngates_read"], step("ngates_read", t))
        prepare(ids["nsa_gates"][-1] + 2)
        for t in range(TT):
            act.wait_ge(sem["cmp_shifted"], at("cmp_shifted", t))
            act.activation(nCP[:], nCP[:], ACT.Exp).then_inc(sem["cmp_exp"], step("cmp_exp", t))
            act.wait_ge(sem["cmp_p_turned"], at("cmp_p_turned", t))
            if t:
                act.wait_ge(sem["cmp_weighted"], at("cmp_weighted", t - 1))
            act.activation(nCT[:], ps[2][:, 0:384].rearrange("p (u n) -> p u n", u=3), ACT.Copy).then_inc(sem["cmp_pt_copied"], step("cmp_pt_copied", t))
        attend("nsa")
        turned_mix("nsa")
        rows("l11", ("w_out", 1))
        ffn(1, 1)
        prepare(len(panels) - 1)

    @block.vector
    def _(dve):
        done = [0]
        chain = [0]

        def prepare(g):
            while done[0] <= min(g, len(panels) - 1):
                n = done[0]
                w = widths[n]
                dve.wait_ge(sem["w_high_ready"], at("w_high_ready", n))
                dve.tensor_tensor(WL[n % 2][:, 0:w], RAW[n % 2][:, 0:w], WH[n % 2][:, 0:w].bitcast(F32),
                                         ALU.subtract).then_inc(sem["w_low_ready"], step("w_low_ready", n))
                done[0] += 1

        def link(ins):
            chain[0] += 1
            ins.then_inc(sem["dve_step"], 1)
            dve.wait_ge(sem["dve_step"], chain[0])

        def after(name, j):
            if j == 0:
                prepare(ids[name][-1] + 1)
            dve.wait_ge(sem["product_done"], at("product_done", ("acc", name, j)))

        def low_turned(s, t, hh, hl, signal, perm=False):
            dve.wait_ge(sem["turned_high"], at("turned_high", (s, t)))
            for b in range(2):
                cols = slice(t, SEQ, 4) if perm else slice(t * P, (t + 1) * P)
                ins = dve.tensor_tensor(hl[:, 4 * b:4 * b + 4, cols], ps[2 * t + b][:].rearrange("p (k n) -> p k n", k=4),
                                        hh[:, 4 * b:4 * b + 4, cols].bitcast(F32), ALU.subtract)
            ins.then_inc(sem[signal], step(signal, (s, t)))

        def rows(s, y=None):
            kind, coef = ROWS[s]
            if y:
                prepare(ids[y][-1])
            for t in range(TT + 1):
                if t < TT:
                    r = R[t % 2]
                    if t == 0:
                        dve.wait_ge(sem["gains_loaded"], at("gains_loaded", s))
                    if kind == "ln":
                        dve.wait_ge(sem["product_done"], at("product_done", ("acc", y, t)))
                        for half in range(2):
                            c = slice(512 * half, 512 * half + 512)
                            link(dve.scalar_tensor_tensor(out=r[:, c], in0=ps[2 * t + half][:], scalar=coef,
                                                          in1=X[:, t, c], op0=ALU.mult, op1=ALU.add))
                            link(dve.bn_stats(BN[:, 6 * half:6 * half + 6], r[:, c]))
                        dve.bn_aggr(SS[:, 4 * t:4 * t + 2], BN[:, 0:12]).then_inc(sem["variance"], step("variance", (s, t)))
                    if kind in ("post", "post_pre"):
                        dve.wait_ge(sem["rstd"], at("rstd", (s, t)))
                        dve.wait_ge(sem["squared"], at("squared", (s, t)))
                        for half in range(2):
                            c = slice(512 * half, 512 * half + 512)
                            link(dve.scalar_tensor_tensor(out=r[:, c], in0=ps[2 * t + half][:], scalar=RS[:, 4 * t:4 * t + 1],
                                                          in1=GB[0][:, c], op0=ALU.mult, op1=ALU.mult))
                        ins = dve.tensor_tensor(X[:, t, :], X[:, t, :], r[:], ALU.add)
                        if kind == "post":
                            ins.then_inc(sem["rows_done"], step("rows_done", (s, t)))
                        else:
                            ins.then_inc(sem["x_added"], step("x_added", (s, t)))
                if t < TT:
                    if kind == "ln":
                        dve.wait_ge(sem["variance"], at("variance", (s, t)))
                        link(dve.scalar_tensor_tensor(out=r[:], in0=r[:], scalar=SS[:, 4 * t:4 * t + 1], in1=GB[0][:],
                                                      op0=ALU.subtract, op1=ALU.mult))
                        dve.wait_ge(sem["rstd"], at("rstd", (s, t)))
                        dve.scalar_tensor_tensor(out=X[:, t, :], in0=r[:], scalar=RS[:, 4 * t:4 * t + 1], in1=GB[1][:],
                                                        op0=ALU.mult, op1=ALU.add).then_inc(sem["rows_done"], step("rows_done", (s, t)))
                    if kind in ("pre", "post_pre"):
                        dve.wait_ge(sem["rstd_x"], at("rstd_x", (s, t)))
                        dve.wait_ge(sem["squared_x"], at("squared_x", (s, t)))
                        dve.scalar_tensor_tensor(out=r[:], in0=X[:, t, :], scalar=RS[:, 4 * t + 2:4 * t + 3],
                                                        in1=GB[0 if kind == "pre" else 1][:], op0=ALU.mult, op1=ALU.mult).then_inc(sem["rows_done"], step("rows_done", (s, t)))
                if y and t == TT - 1:
                    prepare(ids[y][-1] + 1)
                if t >= 1 and s != "l12":
                    low_turned(s, t - 1, XTH, XTL, "xt_ready")

        def attend(name):
            tasks, SBs, PTs = ATT[name]
            N = len(tasks)
            for n in range(N + 2):
                if n < N:
                    tk = tasks[n]
                    m_ap, nh, b = tk["width"]
                    if name[0] == "b" and name[1] == 0 and n in (0, 12):
                        c = 0 if n == 0 else 192
                        if n == 12:
                            dve.wait_ge(sem["p_turned"], at("p_turned", (name, 11)))
                        elif name[2] == 1:
                            dve.wait_ge(sem["p_turned"], at("p_turned", (("b", 0, 0), 15)))
                        for sb in SBs:
                            link(dve.memset(sb[:].rearrange("p (e c) -> p e c", e=2)[:, :, c:c + 64], 0.0))
                    if name == "nsa" and n < 96 and n % 8 == 0:
                        h = n // 8
                        if h >= 2:
                            dve.wait_ge(sem["masked"], at("masked", (name, 8 * (h - 1) - 1)))
                        link(dve.scalar_tensor_tensor(out=nAB[h % 2][:], in0=nDI[:], scalar=-slopes[h], in1=nCM[:],
                                                      op0=ALU.mult, op1=ALU.add))
                    dve.wait_ge(sem["scored"], at("scored", (name, n)))
                    if n >= 2:
                        dve.wait_ge(sem["p_turned"], at("p_turned", (name, n - 2)))
                    sv = tk["view"]
                    if tk["bias"] is not None:
                        dve.scalar_tensor_tensor(out=sv(SBs[n % 2][:]), in0=sv(ps[n % 2][:]), scalar=tk["scale"],
                                                        in1=tk["bias"], op0=ALU.mult, op1=ALU.add).then_inc(sem["masked"], step("masked", (name, n)))
                    else:
                        dve.tensor_scalar(sv(SBs[n % 2][:]), sv(ps[n % 2][:]), tk["scale"], None, ALU.mult).then_inc(sem["masked"], step("masked", (name, n)))
                    dve.wait_ge(sem["masked"], at("masked", (name, n)))
                    dve.tensor_reduce(m_ap, sv(SBs[n % 2][:]), AX.X, ALU.max, negate=True).then_inc(sem["maxed"], step("maxed", (name, n)))
                if n >= 2:
                    m = n - 2
                    kind, dst, arg = tasks[m]["finish"]
                    if kind == "copy":
                        if m == 0 and name == ("b", 1, 0):
                            dve.wait_ge(sem["o0_permuted"], at("o0_permuted"))
                        dve.wait_ge(sem["weighted"], at("weighted", (name, m)))
                        dve.tensor_copy(dst, ps[4 + m % 2][:, 0:arg].rearrange("p (h d) -> p h d", d=64)).then_inc(sem["o_read"], step("o_read", (name, m)))
                    else:
                        d = DS[:, m % 4:m % 4 + 1]
                        rd = RD[:, m % 4:m % 4 + 1]
                        link(dve.reciprocal(rd, d))
                        if kind == "add":
                            link(dve.tensor_tensor(rd, rd, arg, ALU.mult))
                        dve.wait_ge(sem["weighted"], at("weighted", (name, m)))
                        if kind == "norm":
                            ins = dve.tensor_scalar(dst, ps[4 + m % 2][:, 0:64], rd, None, ALU.mult)
                        else:
                            ins = dve.scalar_tensor_tensor(out=dst, in0=ps[4 + m % 2][:, 0:64], scalar=rd, in1=dst,
                                                           op0=ALU.mult, op1=ALU.add)
                        ins.then_inc(sem["o_read"], step("o_read", (name, m)))
                        if kind == "add":
                            dve.wait_ge(sem["o_read"], at("o_read", (name, m)))

        def low_mix(name):
            _, hh, hl, perm = mixes[name]
            for t in range(TT):
                low_turned(name, t, hh, hl, "mix_split", perm)

        def mix_rows_done(name):
            N = len(ATT[name][0])
            dve.wait_ge(sem["o_read"], at("o_read", (name, N - 1)))
            for t in range(TT):
                dve.tensor_copy(DG[:, t:t + 1], small[:, 48:49]).then_inc(sem["mix_ready"], step("mix_ready", (name, t)))

        dve.memset(HALF, -0.5).then_inc(sem["half_ready"], step("half_ready"))
        dve.memset(RB[32:33, :], 1.0).then_inc(sem["table_ones"], step("table_ones"))
        dve.wait_ge(sem["bias_multiplied"], at("bias_multiplied"))
        dve.tensor_copy(BROW[0:16, 0:384], ps[0][0:16, 0:384])
        dve.tensor_copy(BROW[0:16, 384:896], ps[1][0:16, :]).then_inc(sem["bias_copied"], step("bias_copied"))
        for b in range(4):
            dve.wait_ge(sem["mem_high"], at("mem_high", b))
            dve.tensor_tensor(MTL[:, 2 * b:2 * b + 2, :], ps[2 + b][:].rearrange("p (k n) -> p k n", k=2),
                                     MTH[:, 2 * b:2 * b + 2, :].bitcast(F32), ALU.subtract).then_inc(sem["mem_split"], step("mem_split", b))
        prepare(ids["mem", 1][-1] + 1)
        for b in range(4):
            dve.wait_ge(sem["ws_turned"], at("ws_turned", b))
            dve.tensor_copy(WST[:, 4 * b:4 * b + 4, :], ps[b][:].rearrange("p (h n) -> p h n", h=4)).then_inc(sem["ws_copied"], step("ws_copied", b))
        prepare(ids["mem", 1][-1] + 2)
        rows("s0")

        for c in range(4):
            prepare(ids["v", c][-1] + 1)
            for t in range(TT):
                dve.wait_ge(sem["v_read"], at("v_read", (c, t)))
                link(dve.bn_stats(BN[:, 24 * t + 6 * c:24 * t + 6 * c + 6], V[:, t, 512 * c:512 * c + 512]))
            prepare(ids["v", c][-1] + 2)
        for t in range(TT):
            ins = dve.bn_aggr(SS[:, 4 * t:4 * t + 2], BN[:, 24 * t:24 * t + 24])
        ins.then_inc(sem["variance"], step("variance", "v"))
        prepare(ids["u", 0][-1] + 1)
        for hh in range(2):
            dve.wait_ge(sem["gains_loaded"], at("gains_loaded", ("v", hh)))
            if hh == 0:
                dve.wait_ge(sem["variance"], at("variance", "v"))
                dve.wait_ge(sem["rstd"], at("rstd", "v"))
            if hh == 1:
                prepare(ids["u", 0][-1] + 2)
            for t in range(TT):
                v = V[:, t, 1024 * hh:1024 * hh + 1024]
                link(dve.scalar_tensor_tensor(out=v, in0=v, scalar=SS[:, 4 * t:4 * t + 1], in1=GB[0][:],
                                              op0=ALU.subtract, op1=ALU.mult))
                ins = dve.scalar_tensor_tensor(out=v, in0=v, scalar=RS[:, t:t + 1], in1=GB[1][:],
                                               op0=ALU.mult, op1=ALU.add)
            ins.then_inc(sem["v_normed"], step("v_normed", hh))
        prepare(ids["u", 1][-1] + 2)
        dve.wait_ge(sem["b_s_loaded"], at("b_s_loaded"))
        dve.wait_ge(sem["mem_kv_stored"], at("mem_kv_stored"))
        for h in range(A_HEADS):
            dve.wait_ge(sem["spatial_done"], at("spatial_done", h))
            bias = BS[:, h * P:h * P + P].rearrange("p (c n) -> p c n", c=1).to_broadcast([P, TT, P])
            dve.tensor_tensor(SG[:, h, :].rearrange("p (c n) -> p c n", c=TT),
                                     ps[h % 8][:].rearrange("p (c n) -> p c n", c=TT), bias, ALU.add).then_inc(sem["spatial_read"], step("spatial_read", h))

        def y_part(c):
            prepare(ids["g", c][-1] + 1)
            for j in range(4):
                h = 4 * c + j
                u = U[:, c % 2, j, :]
                dve.wait_ge(sem["spatial_read"], at("spatial_read", h))
                dve.wait_ge(sem["u_read"], at("u_read", (c, j)))
                link(dve.tensor_tensor(u, u, SG[:, h, :], ALU.mult))
                dve.wait_ge(sem["g_read"], at("g_read", (c, j)))
                dve.tensor_tensor(u, u, GT[:, j, :], ALU.mult).then_inc(sem["y_multiplied"], step("y_multiplied", h))
            for j in range(4):
                h = 4 * c + j
                dve.wait_ge(sem["y_high_ready"], at("y_high_ready", h))
                dve.tensor_tensor(YL[:, h, :], U[:, c % 2, j, :], YH[:, h, :].bitcast(F32), ALU.subtract).then_inc(sem["y_split"], step("y_split", h))
            prepare(ids["g", c][-1] + 2)

        y_part(0)
        y_part(1)
        prepare(ids["u", 2][-1] + 2)
        y_part(2)
        prepare(ids["u", 3][-1] + 2)
        y_part(3)
        rows("s1", "a_out")

        for g in range(3):
            for hf in range(2):
                prepare(ids["b", g, hf, "v"][-1] + 2)
                dve.wait_ge(sem["bias_loaded"], at("bias_loaded", (g, hf)))
                attend(("b", g, hf))
        link(dve.tensor_tensor(bS[:], bM[:, 0], bM[:, 1], ALU.min))
        link(dve.tensor_tensor(bS[:], bS[:], bM[:, 2], ALU.min))
        for g in range(3):
            ins = dve.tensor_tensor(bE[:, g], bS[:], bM[:, g], ALU.subtract)
        ins.then_inc(sem["group_diffs"], step("group_diffs"))
        dve.wait_ge(sem["group_exps"], at("group_exps"))
        link(dve.tensor_tensor(bD[:], bD[:], bE[:], ALU.mult))
        link(dve.tensor_tensor(bS[:], bD[:, 0], bD[:, 1], ALU.add))
        link(dve.tensor_tensor(bS[:], bS[:], bD[:, 2], ALU.add))
        link(dve.reciprocal(bS[:], bS[:]))
        for g in range(3):
            ins = dve.tensor_tensor(bE[:, g], bE[:, g], bS[:], ALU.mult)
        ins.then_inc(sem["group_weights"], step("group_weights"))
        dve.wait_ge(sem["group_weights"], at("group_weights"))
        prepare(ids["b_gate", 0][-1] + 1)

        def weighted(g, t):
            o = bO[g][:, t, :].rearrange("p (h d) -> p h d", d=64)
            w = bE[:, g, t, :].rearrange("p (h d) -> p h d", d=1).to_broadcast([P, 16, 64])
            return o, w
        for t in range(TT):
            if t == 1:
                prepare(ids["b_gate", 0][-1] + 2)
            if t == 2:
                prepare(ids["b_gate", 1][-1] + 1)
            for g in (0, 2):
                o, w = weighted(g, t)
                link(dve.tensor_tensor(o, o, w, ALU.mult))
            link(dve.tensor_tensor(bO[0][:, t, :], bO[0][:, t, :], bO[2][:, t, :], ALU.add))
            dve.wait_ge(sem["o1_weighted"], at("o1_weighted", t))
            link(dve.tensor_tensor(bO[0][:, t, :], bO[0][:, t, :], bO[1][:, t, :], ALU.add))
        dve.wait_ge(sem["bgate_read"], at("bgate_read", 1))
        prepare(ids["b_gate", 1][-1] + 2)
        for t in range(TT):
            ins = dve.tensor_tensor(bO[0][:, t, :], bO[0][:, t, :], bG[:, t, :], ALU.mult)
            ins.then_inc(sem["mix_ready"], step("mix_ready", ("b", t)))
        low_mix("b")
        rows("s2", "b_out")

        def ffn(l, i):
            f = (l, i)
            for c in range(6):
                if c < 5:
                    prepare(ids["gate", l, i, c][-1] + 2)
                    uname, ng, bank = ("up", l, i, c), 4, 4
                else:
                    uname, ng, bank = ("last", l, i), 2, 2
                for j in range(ng):
                    if j == 0:
                        prepare(ids[uname][-1] + 1)
                    dve.wait_ge(sem["product_done"], at("product_done", ("acc", uname, j if c < 5 else j + 2)))
                    dve.wait_ge(sem["gate_read"], at("gate_read", (f, c, j)))
                    dve.tensor_tensor(G[:, j, :], ps[bank + j][:], G[:, j, :], ALU.mult).then_inc(sem["up_read"], step("up_read", (f, c, j)))
                dve.wait_ge(sem["hidden_high"], at("hidden_high", (f, c)))
                a = 4 * c
                dve.tensor_tensor(HTL[:, a:a + ng, :], G[:, 0:ng, :], HTH[:, a:a + ng, :].bitcast(F32),
                                         ALU.subtract).then_inc(sem["hidden_split"], step("hidden_split", (f, c)))
                prepare(ids[uname][-1] + 2)

        ffn(0, 0)
        rows("l00", ("down", 0, 0))

        prepare(ids["mla_in"][-1] + 1)
        dve.wait_ge(sem["gains_loaded"], at("gains_loaded", "mla"))
        dve.wait_ge(sem["rstd"], at("rstd", "mla"))
        for t in range(TT):
            dve.wait_ge(sem["c_read"], at("c_read", t))
            dve.scalar_tensor_tensor(out=ZR[:, t, 0:256], in0=ZR[:, t, 0:256], scalar=RS[:, t:t + 1], in1=GB[0][:, 0:256],
                                     op0=ALU.mult, op1=ALU.mult)
            dve.scalar_tensor_tensor(out=ZR[:, t, 256:384], in0=ZR[:, t, 256:384], scalar=RS[:, 4 + t:5 + t],
                                            in1=GB[0][:, 256:384], op0=ALU.mult, op1=ALU.mult).then_inc(sem["c_normed"], step("c_normed", t))
        prepare(ids["mla_mem"][-1] + 1)
        for j in range(3):
            dve.wait_ge(sem["c_high"], at("c_high", j))
            dve.tensor_tensor(CTL[:, j, :], ps[j][:], CTH[:, j, :].bitcast(F32), ALU.subtract).then_inc(sem["c_split"], step("c_split", j))
        prepare(ids["mla_mem"][-1] + 2)
        dve.wait_ge(sem["rope_loaded"], at("rope_loaded"))

        def rope(x1, x2, o1, o2, c, s, shape, tmp):
            for i, (a, b) in enumerate(((x1, c), (x2, s), (x2, c), (x1, s))):
                ins = dve.tensor_tensor(tmp[i], a, b, ALU.mult)
            link(ins)
            dve.tensor_tensor(o1, tmp[0], tmp[1], ALU.subtract)
            return dve.tensor_tensor(o2, tmp[2], tmp[3], ALU.add)

        tmp = [RT[:, i, 0:64].rearrange("p (t d) -> p t d", t=TT) for i in range(4)]
        link(rope(ZR[:, :, 384:400], ZR[:, :, 400:416], KR[:, :, 0:16], KR[:, :, 16:32], COS[:], SIN[:], None, tmp))
        prepare(ids["uq"][-1] + 2)
        tmp = [RT[:, i, :].rearrange("p (h d) -> p h d", h=HEADS) for i in range(4)]
        dve.wait_ge(sem["uq_read"], at("uq_read", (3, 1)))
        for t in range(TT):
            dve.wait_ge(sem["uq_tail_read"], at("uq_tail_read", t))
            x1, x2 = mF[:, t, :, 64:80], mF[:, t, :, 80:96]
            cb, sn = (z[:, t, :].rearrange("p (h d) -> p h d", h=1).to_broadcast([P, HEADS, 16]) for z in (COS, SIN))
            ins = rope(x1, x2, x1, x2, cb, sn, None, tmp)
            if t < TT - 1:
                link(ins)
        ins.then_inc(sem["roped"], step("roped", "q"))
        prepare(ids["uq_tail"][-1] + 2)
        for t in range(TT):
            for n in range(3):
                j = 3 * t + n
                after("ukv", j)
                dve.wait_ge(sem["ukv_read_k"], at("ukv_read_k", j))
                dve.tensor_copy(mV[:, t, 256 * n:256 * n + 256].rearrange("p (h d) -> p h d", h=4),
                                       ps[j % 8][:].rearrange("p (h d) -> p h d", h=4)[:, :, 64:128]).then_inc(sem["ukv_read_v"], step("ukv_read_v", j))
            ins = dve.tensor_copy(mF[:, t, :, 64:96],
                                  KR[:, t, :].rearrange("p (h d) -> p h d", h=1).to_broadcast([P, HEADS, 32]))
        ins.then_inc(sem["roped"], step("roped", "k"))
        prepare(ids["ukv"][-1] + 2)
        dve.wait_ge(sem["mix_const0"], at("mix_const0"))
        attend("mla")
        mix_rows_done("mla")
        low_mix("mla")
        rows("l01", ("w_out", 0))
        ffn(0, 1)
        rows("l02", ("down", 0, 1))

        prepare(ids["kv_a"][-1] + 1)
        dve.wait_ge(sem["pos_loaded"], at("pos_loaded"))
        for j in range(2):
            dve.wait_ge(sem["kvf_read"], at("kvf_read", j))
            src = bass.AP(KVF, j * SEQ, [[4 * SEQ, P], [1, CMP_LEN], [CMP_STRIDE, N_CMP]])
            pos = POS[:, j, :].rearrange("p (l n) -> p l n", n=1).to_broadcast([P, CMP_LEN, N_CMP])
            ins = dve.tensor_tensor(FZ[:, j], src, pos, ALU.add)
        ins.then_inc(sem["blocks_ready"], step("blocks_ready"))
        prepare(ids["kv_a"][-1] + 2)
        prepare(ids["kv_b"][-1] + 2)
        dve.wait_ge(sem["cmp_hidden_done"], at("cmp_hidden_done"))
        dve.memset(H1[:].rearrange("p a b c r n -> p (a b c r n)"), 0.0).then_inc(sem["h1_zeroed"], step("h1_zeroed"))
        dve.wait_ge(sem["kv_kept"], at("kv_kept"))
        ffn(1, 0)
        rows("l10", ("down", 1, 0))

        prepare(ids["nsa_gates"][-1] + 1)
        dve.wait_ge(sem["nsa_const"], at("nsa_const"))
        for h in range(HEADS):
            ins = dve.scalar_tensor_tensor(out=nBC[:, :, h, :], in0=nCD[:], scalar=-slopes[h], in1=nCN[:],
                                           op0=ALU.mult, op1=ALU.add)
        link(ins)
        prepare(ids["nsa_gates"][-1] + 2)

        def over_keys(v):
            return v.rearrange("p (h n) -> p h n", n=1).to_broadcast([P, HEADS, NC])
        for t in range(TT):
            dve.wait_ge(sem["cmp_scored"], at("cmp_scored", t))
            if t:
                dve.wait_ge(sem["cmp_p_turned"], at("cmp_p_turned", t - 1))
            for g in range(2):
                ins = dve.scalar_tensor_tensor(out=nCP[:, 6 * g:6 * g + 6, :],
                                               in0=ps[g][:, 0:192].rearrange("p (h n) -> p h n", n=NC), scalar=HD_SCALE,
                                               in1=nBC[:, t, 6 * g:6 * g + 6, :], op0=ALU.mult, op1=ALU.add)
            link(ins)
            link(dve.tensor_reduce(CM_[:, 0:HEADS], nCP[:], AX.X, ALU.max))
            dve.tensor_tensor(nCP[:], nCP[:], over_keys(CM_[:, 0:HEADS]), ALU.subtract).then_inc(sem["cmp_shifted"], step("cmp_shifted", t))
            dve.wait_ge(sem["cmp_exp"], at("cmp_exp", t))
            mask = nC1[:, t, :].rearrange("p (h n) -> p h n", h=1).to_broadcast([P, HEADS, NC])
            dve.tensor_tensor(nCP[:], nCP[:], mask, ALU.mult).then_inc(sem["cmp_p_ready"], step("cmp_p_ready", t))
            dve.wait_ge(sem["cmp_p_ready"], at("cmp_p_ready", t))
            link(dve.tensor_reduce(CD_[:, 0:HEADS], nCP[:], AX.X, ALU.add))
            link(dve.tensor_scalar(CD_[:, 0:HEADS], CD_[:, 0:HEADS], 1e-30, None, ALU.max))
            link(dve.reciprocal(CF_[:, 0:HEADS], CD_[:, 0:HEADS]))
            dve.wait_ge(sem["ngates_read"], at("ngates_read", t))
            link(dve.tensor_tensor(CF_[:, 0:HEADS], CF_[:, 0:HEADS], nG[:, t, :, 0], ALU.mult))
            dve.wait_ge(sem["cmp_weighted"], at("cmp_weighted", t))
            for e in range(4):
                ins = dve.tensor_tensor(O[:, t, 0:768].rearrange("p (h d) -> p h d", d=64)[:, e:HEADS:4, :],
                                        ps[4 + e][:, 0:192].rearrange("p (h d) -> p h d", d=64),
                                        CF_[:, e:HEADS:4].rearrange("p (h d) -> p h d", d=1).to_broadcast([P, 3, 64]),
                                        ALU.mult)
            ins.then_inc(sem["cmp_o_read"], step("cmp_o_read", t))
            dve.wait_ge(sem["cmp_o_read"], at("cmp_o_read", t))
        attend("nsa")
        mix_rows_done("nsa")
        low_mix("nsa")
        rows("l11", ("w_out", 1))
        ffn(1, 1)
        rows("l12", ("down", 1, 1))

    @block.gpsimd
    def _(pool):
        chain = [0]

        def load(dst, src, name, label=None):
            pool.dma_start(dst, src).then_inc(sem[name], step(name, label, by=16))

        def gains(label, a, b, wa=D, wb=D):
            load(GB[0][:, 0:wa], row(a, wa), "gains_loaded", label)
            if b is not None:
                load(GB[1][:, 0:wb], row(b, wb), "gains_loaded", label)
            pool.wait_ge(sem["gains_loaded"], at("gains_loaded", label))

        def link(ins):
            chain[0] += 1
            ins.then_inc(sem["pool_step"], 1)
            pool.wait_ge(sem["pool_step"], chain[0])

        def rsqrt(ss, n, scale, eps, rs, name, label):
            link(pool.tensor_scalar(RM[:, 0:n], ss, scale, eps, ALU.mult, ALU.add))
            pool.tensor_tensor(rs, RM[:, 0:n], HALF[:, 0:n], ALU.pow).then_inc(sem[name], step(name, label))
            pool.wait_ge(sem[name], at(name, label))

        def rows(s):
            kind, coef = ROWS[s]
            for t in range(TT):
                a = 4 * t
                if kind == "ln":
                    pool.wait_ge(sem["variance"], at("variance", (s, t)))
                    rsqrt(SS[:, a + 1:a + 2], 1, 1.0, LN_EPS / ALPHA ** 2, RS[:, a:a + 1], "rstd", (s, t))
                if kind in ("post", "post_pre"):
                    pool.wait_ge(sem["squared"], at("squared", (s, t)))
                    link(pool.tensor_tensor(SS[:, a:a + 1], SS[:, a:a + 1], SS[:, a + 1:a + 2], ALU.add))
                    rsqrt(SS[:, a:a + 1], 1, 1.0 / D, RMS_EPS, RS[:, a:a + 1], "rstd", (s, t))
                if kind in ("pre", "post_pre"):
                    pool.wait_ge(sem["squared_x"], at("squared_x", (s, t)))
                    rsqrt(SS[:, a + 2:a + 3], 1, 1.0 / D, RMS_EPS, RS[:, a + 2:a + 3], "rstd_x", (s, t))

        load(HOT[0:33, :], A["hot"], "hot_loaded")
        load(RB[0:32, :], A["rel_bias"], "hot_loaded")
        load(MEM[:], A["mem_2"].rearrange("(m p) d -> p m d", p=P), "mem_loaded")
        gains("s0", *GAINS["s0"])
        load(WS[:], A["a_w_s"][0].rearrange("h p q -> p h q"), "ws_loaded")
        pool.wait_ge(sem["half_ready"], at("half_ready"))
        rows("s0")
        pool.wait_ge(sem["bias_copied"], at("bias_copied"))
        for g in range(3):
            L = BIAS_W[g]
            src = BROW[0:16, BIAS_AT[g]:BIAS_AT[g] + L].rearrange("h (p x) -> h p x", p=1).to_broadcast([16, P, L])
            load(bass.AP(scratch[f"bias{g}"].tensor, 0, [[P * (L + 1), 16], [L + 1, P], [1, L]]), src, "bias_stored")
        pool.wait_ge(sem["bias_stored"], at("bias_stored"))
        for l in range(2):
            pool.wait_ge(sem["mem_kv_copied"], at("mem_kv_copied", (l, 3)))
            load(scratch["mem_kv"][l], KVS[:, l].rearrange("p j n -> p (j n)"), "mem_kv_stored")
        for hh in range(2):
            if hh == 0:
                pool.wait_ge(sem["rows_done"], at("rows_done", ("s0", 3)))
                pool.wait_ge(sem["turned"], at("turned", ("s0", 3)))
                load(BS[:], row(A["a_b_s"][0].rearrange("h p -> (h p)"), 2048), "b_s_loaded")
            else:
                pool.wait_ge(sem["v_normed"], at("v_normed", 0))
            gains(("v", hh), A["a_vnorm_g"][0, 1024 * hh:1024 * hh + 1024], A["a_vnorm_b"][0, 1024 * hh:1024 * hh + 1024])
            if hh == 0:
                pool.wait_ge(sem["variance"], at("variance", "v"))
                var = bass.AP(small, 1, [[512, P], [4, TT]])
                rsqrt(var, 4, 1.0, 1e-6, RS[:, 0:4], "rstd", "v")
        pool.wait_ge(sem["v_normed"], at("v_normed", 1))
        gains("s1", *GAINS["s1"])
        rows("s1")
        pool.wait_ge(sem["rows_done"], at("rows_done", ("s1", 3)))
        for g in range(3):
            for hf in range(2):
                if (g, hf) != (0, 0):
                    prev = ("b", g, hf - 1) if hf else ("b", g - 1, 1)
                    pool.wait_ge(sem["masked"], at("masked", (prev, len(ATT[prev][0]) - 1)))
                L, w = BIAS_W[g], 256 if g == 0 else 128
                src = bass.AP(scratch[f"bias{g}"].tensor, hf * 8 * P * (L + 1) + 127, [[L, P], [P * (L + 1), 8], [1, w]])
                load(BG[:, 0:8 * w].rearrange("p (h w) -> p h w", h=8), src, "bias_loaded", (g, hf))
                pool.wait_ge(sem["bias_loaded"], at("bias_loaded", (g, hf)))
                if (g, hf) == (0, 1):
                    pool.wait_ge(sem["o_read"], at("o_read", (("b", 0, 1), 15)))
                    pool.wait_ge(sem["exp_done"], at("exp_done", (("b", 0, 1), 15)))
                    for b in range(TT):
                        for r in range(4):
                            q = slice(32 * b, 32 * b + 32)
                            for dst, srct in ((bO[0][q, r, :], bON[r:P:4, b, :]), (bM[q, 0, r, :], bMN[r:P:4, b, :]),
                                              (bD[q, 0, r, :], bDN[r:P:4, b, :])):
                                load(dst, srct, "o0_permuted")
                    pool.wait_ge(sem["o0_permuted"], at("o0_permuted"))
        pool.wait_ge(sem["group_weights"], at("group_weights"))
        for t in range(TT):
            o = bO[1][:, t, :].rearrange("p (h d) -> p h d", d=64)
            w = bE[:, 1, t, :].rearrange("p (h d) -> p h d", d=1).to_broadcast([P, 16, 64])
            pool.tensor_tensor(o, o, w, ALU.mult).then_inc(sem["o1_weighted"], step("o1_weighted", t))
        gains("s2", *GAINS["s2"])
        rows("s2")
        pool.wait_ge(sem["rows_done"], at("rows_done", ("s2", 3)))
        gains("l00", *GAINS["l00"])
        rows("l00")
        pool.wait_ge(sem["rows_done"], at("rows_done", ("l00", 3)))
        load(GB[0][:, 0:256], row(A["mla_q_norm_g_2"][0], 256), "gains_loaded", "mla")
        load(GB[0][:, 256:384], row(A["mla_kv_norm_g_2"][0], 128), "gains_loaded", "mla")
        load(COS[:], A["cos"].rearrange("(t p) d -> p t d", p=P), "rope_loaded")
        load(SIN[:], A["sin"].rearrange("(t p) d -> p t d", p=P), "rope_loaded")
        load(mCM[:], A["causal"], "mix_const0")
        load(mKV[:].rearrange("p j n -> p (j n)"), scratch["mem_kv"][0], "mem_kv_back", 0)
        pool.wait_ge(sem["gains_loaded"], at("gains_loaded", "mla"))
        pool.wait_ge(sem["c_read"], at("c_read", TT - 1))
        rsqrt(SS[:, 0:4], 4, 1.0 / MLA_QR, RMS_EPS, RS[:, 0:4], "rstd", "mla_q")
        rsqrt(SS[:, 4:8], 4, 1.0 / MLA_KVR, RMS_EPS, RS[:, 4:8], "rstd", "mla")
        pool.wait_ge(sem["c_normed"], at("c_normed", TT - 1))
        gains("l01", *GAINS["l01"])
        rows("l01")
        pool.wait_ge(sem["rows_done"], at("rows_done", ("l01", 3)))
        gains("l02", *GAINS["l02"])
        rows("l02")
        for j in range(2):
            for half in range(2):
                q = slice(64 * half, 64 * half + 64)
                load(W1[j][q], A["cmp_w1_2"][j].rearrange("(l d) n -> d l n", d=64), "w1_loaded")
                with nc.allow_non_contiguous_dma(reason="4 KB of positions"):
                    load(POS[q, j, :], A["cmp_pos_2"][j].rearrange("l d -> d l"), "pos_loaded")
        with nc.allow_non_contiguous_dma(reason="512 biases"):
            load(B1[:], A["cmp_b1_2"].rearrange("j (h p) -> p j h", p=P), "w1_loaded")
        load(W2[:], A["cmp_w2_2"].rearrange("j (h p) d -> p j h d", p=P), "w1_loaded")
        pool.wait_ge(sem["kv_copied"], at("kv_copied"))
        load(scratch["kv"][0], KVF[:, 2:4].rearrange("p j n -> p (j n)"), "kv_kept")
        load(scratch["kv"][1], VV[:].rearrange("p t b n -> p (t b n)"), "kv_kept")
        pool.wait_ge(sem["kv_kept"], at("kv_kept"))
        pool.wait_ge(sem["rows_done"], at("rows_done", ("l02", 3)))
        gains("l10", *GAINS["l10"])
        rows("l10")
        pool.wait_ge(sem["rows_done"], at("rows_done", ("l10", 3)))
        load(nK[:].rearrange("p j n -> p (j n)"), scratch["kv"][0], "nsa_const")
        load(nV[:].rearrange("p t b n -> p (t b n)"), scratch["kv"][1], "nsa_const")
        load(nCM[:], A["causal"], "nsa_const")
        load(nDI[:], A["dist"], "nsa_const")
        load(nCD[:], A["cmp_dist"], "nsa_const")
        load(nCN[:], A["cmp_add"], "nsa_const")
        load(nC1[:], A["cmp_mask"], "nsa_const")
        load(nKV[:].rearrange("p j n -> p (j n)"), scratch["mem_kv"][1], "mem_kv_back", 1)
        gains("l11", *GAINS["l11"])
        rows("l11")
        pool.wait_ge(sem["rows_done"], at("rows_done", ("l11", 3)))
        gains("l12", *GAINS["l12"])
        rows("l12")


def constants():
    def bucket(rel):
        n = np.abs(rel)
        large = 8 + (np.log(np.maximum(n, 1) / 8) / math.log(128) * 8).astype(np.int64)
        return np.where(rel > 0, 16, 0) + np.where(n < 8, n, np.minimum(large, 15))

    hot = np.zeros((33, BIAS_ALL), np.float32)
    for g, (w, at) in enumerate(zip(BIAS_W, BIAS_AT)):
        x = np.arange(w)
        diff = x - 191 if g == 0 else x - 127
        valid = np.abs(diff) <= HALF_W if g < 2 else diff % 4 == 0
        tokens = diff if g == 0 else 4 * diff
        b = bucket(tokens)
        for i in range(w):
            if valid[i]:
                hot[b[i], at + i] = 1.0
            else:
                hot[32, at + i] = NEG
    p, x = np.arange(P)[:, None], np.arange(896)[None, :]
    causal = np.where(x <= 384 + p, 0.0, NEG).astype(np.float32)
    dist = (384 + p - x).astype(np.float32)
    tq = (np.arange(TT)[None, :, None] * P + np.arange(P)[:, None, None])
    n = np.arange(NC)[None, None, :]
    seen = (n * CMP_STRIDE + CMP_LEN - 1 <= tq) & (n < N_CMP)
    half = MLA_ROPE // 2
    freq = (np.float32(10000.0) ** (-np.arange(half, dtype=np.float32) / half)).astype(np.float32)
    ang = np.arange(SEQ, dtype=np.float32)[:, None] * freq[None, :]
    return {"ident": np.eye(P, dtype=np.float32), "hot": hot, "causal": causal, "dist": dist,
            "cmp_dist": (tq - (n * CMP_STRIDE + (CMP_LEN - 1) * 0.5)).astype(np.float32),
            "cmp_add": np.where(seen, 0.0, NEG).astype(np.float32), "cmp_mask": seen.astype(np.float32),
            "cos": np.cos(ang).astype(np.float32), "sin": np.sin(ang).astype(np.float32)}


def kernel(**inputs):
    import concourse.bacc as bacc
    from concourse.bass_utils import run_bass_kernel_spmd

    arrays = {k: np.ascontiguousarray(v) for k, v in inputs.items()}
    arrays["x"] = arrays["x"].reshape(SEQ, D)
    arrays["mem_2"] = arrays["mem_2"].reshape(N_MEM, D)
    arrays.update(constants())

    known = {}
    for _ in range(2):
        nc = bacc.Bacc("TRN2", target_bir_lowering=False, num_devices=1)
        A = {k: nc.dram_tensor(f"in_{k}", v.shape, F32, kind="ExternalInput").ap() for k, v in arrays.items()}
        out = nc.dram_tensor("out_rows", (SEQ, D), F32, kind="ExternalOutput").ap()
        scratch = {f"bias{g}": nc.dram_tensor(f"bias{g}", (16, P * (w + 1)), F32, kind="Internal").ap()
                   for g, w in enumerate(BIAS_W)}
        scratch["mem_kv"] = nc.dram_tensor("mem_kv", (2, P, 1024), F32, kind="Internal").ap()
        scratch["kv"] = nc.dram_tensor("kv", (2, P, 1024), F32, kind="Internal").ap()
        counts = Counts(known)
        with ExitStack() as ctx:
            build(nc, A, out, scratch, ctx, counts)
        known = counts.value
    r = run_bass_kernel_spmd(nc, [{f"in_{k}": v for k, v in arrays.items()}], core_ids=[0])
    return r.results[0]["out_rows"].reshape(1, SEQ, D)
```

```python
import math
from contextlib import ExitStack

import numpy as np

import concourse.bass as bass
from concourse import mybir

F32 = mybir.dt.float32
F32R = mybir.dt.float32r
ALU = mybir.AluOpType
ACT = mybir.ActivationFunctionType
AX = mybir.AxisListType

P = 128
SEQ, D = 512, 1024
TT = SEQ // P
KD = D // P
A_WIDTH = 2048
A_HEADS = 16
B_HEADS, B_DIM = 16, 64
B_SCALE = B_DIM ** -0.5
HALF_W = 64
REL_BUCKETS = 32
D_FF = 2816
KF = D_FF // P
N_MEM = 256
HEADS = 12
MLA_QR, MLA_KVR, MLA_NOPE, MLA_ROPE = 256, 128, 64, 32
MLA_QD = MLA_NOPE + MLA_ROPE
MLA_SCALE = MLA_QD ** -0.5
HD = 64
HD_SCALE = HD ** -0.5
CMP_LEN, CMP_STRIDE, CMP_HIDDEN = 32, 16, 256
N_CMP = (SEQ - CMP_LEN) // CMP_STRIDE + 1
NC = 32
ALPHA = 4.0 ** 0.25
RMS_EPS, LN_EPS = 1e-6, 1e-5
NEG = -1e30
BIAS_W = (384, 256, 256)
BIAS_AT = (0, 384, 640)
BIAS_ALL = 896


def alibi_slopes(n):
    def pow2(k):
        start = 2.0 ** (-8.0 / k)
        return [start ** (i + 1) for i in range(k)]
    c = 2 ** math.floor(math.log2(n))
    return pow2(n) if c == n else pow2(c) + pow2(2 * c)[0::2][: n - c]


class Counts:

    def __init__(self, known):
        self.known, self.total, self.value = known, {}, {}

    def step(self, name, *labels, by=1):
        self.total[name] = self.total.get(name, 0) + by
        for label in labels or (None,):
            self.value[name, label] = self.total[name]
        return by

    def at(self, name, label=None):
        return self.known[name, label] if self.known else 1


SIGNALS = """
    b_s_loaded bgate_read bias_copied bias_loaded bias_multiplied bias_stored
    bk_read blocks_ready bq_read bv_read c_high c_normed
    c_read c_rows c_split c_turned cmp_done cmp_exp
    cmp_hidden_done cmp_hidden_ready cmp_kept cmp_o_read cmp_p_ready cmp_p_turned
    cmp_pt_copied cmp_scored cmp_shifted cmp_weighted dve_step exp_done
    g_read gains_loaded gate_read group_diffs group_exps group_weights
    h1_zeroed half_ready head_turned heads_turned hidden_high hidden_split
    hot_loaded ident_loaded kv_copied kv_kept kvf_read masked
    maxed mem_high mem_kv_back mem_kv_copied mem_kv_stored mem_loaded
    mem_split mem_turned mix_const0 mix_ready mix_split ngates_read
    nq_read nsa_const o0_permuted o1_weighted o_read p_turned
    panel_loaded0 panel_loaded1 pool_step pos_loaded product_done pt_copied
    qmem_read rope_loaded roped rows_done rstd rstd_x
    scored spatial_done spatial_read squared squared_x stored
    table_ones turned turned_high u_read ukv_read_k ukv_read_v
    up_read uq_read uq_tail_read v_normed v_read variance
    w1_loaded w_high_ready w_low_ready weighted wrap_ready ws_copied
    ws_loaded ws_turned x_added x_loaded0 x_loaded1 x_loaded2
    x_loaded3 xt_ready y_high_ready y_multiplied y_split p_scaled
    pair_done pair_high pair_split pair_summed cmp_v_spread gates_turned gates_t_read
"""


def weight_panels(A):
    panels, ids = [], {}

    def rows(w, k0, nk, c0, n):
        return w[k0 * P:(k0 + nk) * P, c0:c0 + n].rearrange("(k p) n -> p k n", p=P)

    def add(name, pieces):
        ids.setdefault(name, []).append(len(panels))
        panels.append(pieces)

    def deep(name, w, c0, n):
        for k0 in (0, 4):
            add(name, [(0, 4, n, n, rows(w, k0, 4, c0, n))])

    def down(name, w, kt):
        for k0 in range(0, kt, 2):
            add(name, [(0, 2, D, D, rows(w, k0, 2, 0, D))])

    for l in range(2):
        deep(("mem", l), A["w_mem_kv_2"][l], 0, 512)
    wa = A["a_w_in"][0]
    for c in range(4):
        deep(("v", c), wa, A_WIDTH + 512 * c, 512)
    for part, c in (("u", 0), ("u", 1), ("g", 0), ("g", 1), ("u", 2), ("g", 2), ("u", 3), ("g", 3)):
        deep((part, c), wa, (0 if part == "u" else 2 * A_WIDTH) + 512 * c, 512)
    down("a_out", A["a_w_out"][0], A_WIDTH // P)
    wb = A["b_w_in"][0]
    for g in range(3):
        for hf in range(2):
            for i, part in enumerate("qkv"):
                deep(("b", g, hf, part), wb, g * 3072 + i * 1024 + hf * 512, 512)
    for c in range(2):
        deep(("b_gate", c), wb, 9216 + 512 * c, 512)
    down("b_out", A["b_w_out"][0], 8)

    def ffn(l, i):
        w = A["ffn_w_gu_2"][l, i]
        for c in range(5):
            deep(("gate", l, i, c), w, 512 * c, 512)
            deep(("up", l, i, c), w, D_FF + 512 * c, 512)
        for k0 in (0, 4):
            add(("last", l, i), [(0, 4, 512, 256, rows(w, k0, 4, 2560, 256)),
                                 (256, 4, 512, 256, rows(w, k0, 4, D_FF + 2560, 256))])
        down(("down", l, i), A["ffn_w_down_2"][l, i], KF)

    ffn(0, 0)
    wm = A["mla_w_in_2"][0]
    deep("mla_in", wm, 0, 416)
    add("mla_mem", [(0, 8, 256, 256, rows(wm, 0, 8, 416, 256))])
    add("uq", [(0, 2, 1024, 1024, rows(A["mla_w_uq_2"][0], 0, 2, 0, 1024))])
    add("uq_tail", [(0, 2, 128, 128, rows(A["mla_w_uq_2"][0], 0, 2, 1024, 128))])
    add("ukv", [(0, 1, 1536, 1536, rows(A["mla_w_ukv_2"][0], 0, 1, 0, 1536))])
    down(("w_out", 0), A["w_out_2"][0], 8)
    ffn(0, 1)
    deep("kv_a", A["nsa_w_kv_2"], 0, 512)
    deep("kv_b", A["nsa_w_kv_2"], 512, 256)
    ffn(1, 0)
    wn = A["nsa_w_in_2"][0]
    for name in ("nsa_a", "nsa_b"):
        for k0 in (0, 4):
            pieces = []
            for kk in range(4):
                for g in range(2):
                    n = 4 if name == "nsa_a" else 2
                    c0 = g * 384 + (0 if name == "nsa_a" else 256)
                    src = wn[(k0 + kk) * P:(k0 + kk + 1) * P, c0:c0 + 64 * n].rearrange("p (i d) -> p i d", d=64)
                    pieces.append((kk * 512 + g * 64, n, 128, 64, src))
            if name == "nsa_b":
                pieces.append((256, 4, 512, 256, rows(wn, k0, 4, 804, 256)))
            add(name, pieces)
    add("nsa_gates", [(0, 8, 36, 36, rows(wn, 0, 8, 768, 36))])
    down(("w_out", 1), A["w_out_2"][1], 8)
    ffn(1, 1)
    widths = [max(off + (n - 1) * pitch + w for off, n, pitch, w, _ in pieces) for pieces in panels]
    return panels, ids, widths


def build(nc, A, out, scratch, ctx, counts):
    step, at = counts.step, counts.at
    sem = {name: ctx.enter_context(nc.semaphore(name)) for name in SIGNALS.split()}
    panels, ids, widths = weight_panels(A)

    base = [(nc.sbuf_base + 63) // 64 * 64]

    def at_off(name, shape, off, dt=F32):
        return nc.alloc_sbuf_tensor_at(name, shape, dt, offset=off)

    def place(nbytes):
        base[0] += nbytes
        return base[0] - nbytes

    KB = 1024
    ident = at_off("ident", [P, P], place(512))
    small = at_off("small", [P, 512], place(2 * KB))
    X = at_off("x_rows", [P, TT, D], place(16 * KB))
    xt0 = place(32 * KB)
    XTH = at_off("xt_high", [P, KD, SEQ], xt0, F32R)
    XTL = at_off("xt_low", [P, KD, SEQ], xt0 + 16 * KB, F32R)
    gb0 = place(8 * KB)
    GB = [at_off(f"gain{i}", [P, D], gb0 + 4 * KB * i) for i in range(2)]
    r0 = place(8 * KB)
    R = [at_off(f"row{i}", [P, D], r0 + 4 * KB * i) for i in range(2)]
    G = at_off("gate_rows", [P, 4, 512], r0)
    raw0 = place(16 * KB)
    RAW = [at_off(f"raw{i}", [P, 2048], raw0 + 8 * KB * i) for i in range(2)]
    w0 = place(32 * KB)
    WH = [at_off(f"w_high{i}", [P, 2048], w0 + 8 * KB * i, F32R) for i in range(2)]
    WL = [at_off(f"w_low{i}", [P, 2048], w0 + 16 * KB + 8 * KB * i, F32R) for i in range(2)]
    kept0 = place(3 * KB)
    KCT = at_off("cmp_keys", [P, NC], kept0)
    VC4 = at_off("cmp_values", [P, 2, 64], kept0 + 256)
    rg = place(88 * KB)
    assert base[0] <= nc.sbuf_usable_end, base[0]
    HTH = at_off("hidden_high", [P, KF, SEQ], rg, F32R)
    HTL = at_off("hidden_low", [P, KF, SEQ], rg + 44 * KB, F32R)
    ps = [ctx.enter_context(nc.psum_tensor(f"bank{i}", [P, 512], F32)) for i in range(8)]

    V = at_off("v_rows", [P, TT, A_WIDTH], rg)
    SG = at_off("spatial", [P, A_HEADS, SEQ], rg + 32 * KB)
    YH = at_off("y_high", [P, A_HEADS, SEQ], rg + 32 * KB, F32R)
    YL = at_off("y_low", [P, A_HEADS, SEQ], rg, F32R)
    U = at_off("u_t", [P, 2, 4, SEQ], rg + 64 * KB)
    GT = at_off("g_t", [P, 4, SEQ], rg + 80 * KB)
    WS = at_off("ws_rows", [P, A_HEADS, P], rg + 64 * KB)
    WST = at_off("ws_t", [P, A_HEADS, P], rg + 80 * KB)
    BS = at_off("b_s_all", [P, 2048], r0)
    MTH = at_off("mem_high", [P, KD, N_MEM], rg, F32R)
    MTL = at_off("mem_low", [P, KD, N_MEM], rg + 8 * KB, F32R)
    KVS = at_off("mem_kv_out", [P, 2, 4, N_MEM], rg + 32 * KB)
    MEM = at_off("mem_rows", [P, 2, D], rg + 40 * KB)
    BROW = at_off("bias_rows", [P, BIAS_ALL], rg + 48 * KB)
    HOT = at_off("bucket_hot", [P, BIAS_ALL], rg + 52 * KB)
    RB = at_off("rel_table", [P, 48], rg + 56 * KB)
    bQT = at_off("b_q_t", [P, 4, SEQ], rg)
    bKT = at_off("b_k_t", [P, 4, SEQ], rg + 8 * KB)
    bV = at_off("b_v_rows", [P, TT, 512], rg + 16 * KB)
    bO = [at_off(f"b_o{g}", [P, TT, D], rg + (24 + 16 * g) * KB) for g in range(3)]
    bON = at_off("b_o0_natural", [P, TT, D], rg + 40 * KB)
    bSB = [at_off(f"b_p{i}", [P, 512], rg + a * KB) for i, a in enumerate((72, 74, 84, 86))]
    bPT = [at_off(f"b_pt{i}", [P, 512], rg + (76 + 2 * i) * KB) for i in range(2)]
    bM = at_off("b_negmax", [P, 3, TT, 16], rg + 80 * KB)
    bD = at_off("b_sums", [P, 3, TT, 16], rg + 80 * KB + 768)
    bE = at_off("b_weights", [P, 3, TT, 16], rg + 80 * KB + 1536)
    bS = at_off("b_norm", [P, TT, 16], rg + 80 * KB + 2304)
    bMN = at_off("b_negmax_natural", [P, TT, 16], rg + 83 * KB)
    bDN = at_off("b_sums_natural", [P, TT, 16], rg + 83 * KB + 256)
    BG = at_off("b_bias", [P, 2048], gb0)
    XWH = at_off("xt_wrap_high", [P, KD, P], r0, F32R)
    XWL = at_off("xt_wrap_low", [P, KD, P], r0 + 4 * KB, F32R)
    bG = at_off("b_gate", [P, TT, D], rg)
    bHH = at_off("b_y_high", [P, KD, SEQ], rg + 40 * KB, F32R)
    bHL = at_off("b_y_low", [P, KD, SEQ], rg + 56 * KB, F32R)
    ZR = at_off("mla_c", [P, TT, 416], r0)
    CTH = at_off("mla_c_high", [P, 3, SEQ], xt0, F32R)
    CTL = at_off("mla_c_low", [P, 3, SEQ], xt0 + 6 * KB, F32R)
    mV = at_off("mla_v", [P, TT, 768], xt0 + 12 * KB)
    RT = at_off("rope_tmp", [P, 4, 192], xt0 + 24 * KB)
    mF = at_off("mla_qk_rows", [P, TT, HEADS, MLA_QD], rg)
    qT = at_off("mla_q_t", [P, HEADS, SEQ], rg + 18 * KB)
    kT = at_off("mla_k_t", [P, HEADS, SEQ], rg + 42 * KB)
    mSB = [at_off(f"m_p{i}", [P, 512], a) for i, a in enumerate((rg + 66 * KB, rg + 68 * KB, xt0, xt0 + 2 * KB, xt0 + 4 * KB,
                                                                     xt0 + 6 * KB))]
    mPT = [at_off(f"m_pt{i}", [P, 512], rg + (70 + 2 * i) * KB) for i in range(2)]
    mCM = at_off("mla_causal", [P, 896], rg + 74 * KB)
    mKV = at_off("mla_mem_kv", [P, 4, N_MEM], rg + 78 * KB)
    KR = at_off("mla_k_rope", [P, TT, MLA_ROPE], rg + 82 * KB)
    mQM = at_off("mla_q_mem", [P, 2, SEQ], rg + 82 * KB + 512)
    COS = at_off("cos", [P, TT, 16], rg + 87 * KB)
    SIN = at_off("sin", [P, TT, 16], rg + 87 * KB + 256)
    mHH = at_off("mix0_high", [P, KD, SEQ], rg, F32R)
    mHL = at_off("mix0_low", [P, KD, SEQ], rg + 18 * KB, F32R)
    KVF = at_off("kv_t", [P, 4, SEQ], rg)
    VV = at_off("kv_v_rows", [P, TT, 2, P], rg + 8 * KB)
    LT = CMP_LEN // 2
    W1 = [at_off(f"cmp_w1_{j}", [P, LT, CMP_HIDDEN], rg + (12 + 36 * j) * KB) for j in range(2)]
    FZ = at_off("cmp_blocks", [P, 2, LT, 2, N_CMP], rg + 64 * KB)
    POS = at_off("cmp_pos_t", [P, 2, CMP_LEN], rg + 72 * KB)
    B1 = at_off("cmp_b1_t", [P, 2, 2], rg + 72 * KB + 512)
    W2 = at_off("cmp_w2_t", [P, 2, 2, 64], rg + 73 * KB)
    H1 = at_off("cmp_hidden", [P, 2, 2, 2, 4, NC], rg + 75 * KB)
    nQT = at_off("nsa_q_t", [P, 6, SEQ], rg + 16 * KB)
    nQM = at_off("nsa_q_mem", [P, 2, SEQ], rg + 28 * KB)
    nK = at_off("nsa_k_t", [P, 2, SEQ], rg + 32 * KB)
    nV = at_off("nsa_v_rows", [P, TT, 2, P], rg + 36 * KB)
    nG = at_off("nsa_gates", [P, TT, HEADS, 3], rg + 40 * KB)
    nSB = [at_off(f"n_p{i}", [P, 512], xt0 + (12 + 2 * i) * KB) for i in range(6)]
    nPT = [at_off(f"n_pt{i}", [P, 512], xt0 + (24 + 2 * i) * KB) for i in range(2)]
    nBC = at_off("cmp_bias", [P, TT, HEADS, NC], rg + 41 * KB)
    nOC = at_off("cmp_o_t", [P, 6, SEQ], xt0)
    nHH = at_off("mix1_high", [P, KD, SEQ], rg, F32R)
    nHL = at_off("mix1_low", [P, KD, SEQ], rg + 41 * KB, F32R)
    nAB = [at_off(f"n_bias{i}", [P, 896], rg + 57 * KB + 3584 * i) for i in range(2)]
    nCM = at_off("nsa_causal", [P, 896], rg + 64 * KB)
    nDI = at_off("nsa_dist", [P, 896], rg + 64 * KB + 3584)
    nKV = at_off("nsa_mem_kv", [P, 4, N_MEM], rg + 71 * KB)
    nCD = at_off("cmp_dist", [P, TT, NC], rg + 75 * KB)
    nCN = at_off("cmp_mask_add", [P, TT, NC], rg + 75 * KB + 512)
    nC1 = at_off("cmp_mask", [P, TT, NC], rg + 76 * KB)
    nCPs = [at_off(f"cmp_p{i}", [P, HEADS, NC], rg + 77 * KB + 1536 * i) for i in range(2)]
    nCTs = [at_off(f"cmp_pt{i}", [P, 3, P], rg + 80 * KB + 1536 * i) for i in range(2)]
    VBD = at_off("cmp_v_spread", [P, 2, 2, P], rg + 83 * KB)
    KBD = at_off("cmp_k_spread", [P, 2, NC], rg + 85 * KB)
    nGT = at_off("nsa_gates_t", [P, SEQ], xt0 + 30 * KB)

    slopes = alibi_slopes(HEADS)
    MW = 384

    ROWS = {"s0": ("pre", 0), "s1": ("post_pre", 0), "s2": ("post", 0),
            "l00": ("ln", 0.5 / ALPHA), "l01": ("ln", 1.0 / ALPHA), "l02": ("ln", 0.5 / ALPHA),
            "l10": ("ln", 0.5 / ALPHA), "l11": ("ln", 1.0 / ALPHA), "l12": ("ln", 0.5 / ALPHA)}
    GAINS = {"s0": (A["norm_pre"][0], None), "s1": (A["norm_post"][0], A["norm_pre"][1]),
             "s2": (A["norm_post"][1], None)}
    for l in range(2):
        for i in range(3):
            GAINS[f"l{l}{i}"] = (A["ln_g_2"][l, i], A["ln_b_2"][l, i])
    SS = small[:, 0:16]
    RS = small[:, 16:32]
    RM = small[:, 32:48]
    HALF = small[:, 48:64]
    BN = small[:, 64:64 + 96]
    NM = small[:, 192:208]
    DS = small[:, 208:224]
    RD = small[:, 224:240]
    CM_ = small[:, 256:272]
    CD_ = small[:, 272:288]
    CF_ = small[:, 288:304]

    def row(vec, n):
        return vec.rearrange("(a d) -> a d", a=1).to_broadcast([P, n])

    def task(scores, view, scale, bias, heads, turns, values, finish, width):
        return dict(scores=scores, view=view, scale=scale, bias=bias, heads=heads, turns=turns,
                    values=values, finish=finish, width=width)

    def heads_of(rows, t, h0, n):
        return rows[:, t, :].rearrange("p (h d) -> p h d", d=64)[:, h0:h0 + 2 * n - 1:2, :]

    def dilated_tasks(g, hf):
        out = []
        if g == 0:
            for b in range(TT):
                lo, hi = (64 if b == 0 else 0), (192 if b == TT - 1 else 256)
                for j in range(4):
                    sc, hd, tn, va = [], [], [], []
                    for e in range(2):
                        h = 4 * (j // 2) + 2 * e + j % 2
                        s = 64 * (j % 2)
                        sc.append((e * 256 + lo, e * 256 + hi, bQT[s:s + 64, h // 2, P * b:P * b + P],
                                   bKT[s:s + 64, h // 2, P * b - 64 + lo:P * b - 64 + hi]))
                        gh = hf * 8 + h
                        hd.append((e * 256 + lo, e * 256 + hi, bMN[:, b, gh:gh + 1], bDN[:, b, gh:gh + 1]))
                        tn += [(e * 256 + P * w, P) for w in range(2)]
                        va.append((e * 64, [(P, (e * 2 + w) * P, bV[:, (b + w) % TT, h * 64:h * 64 + 64])
                                            for w in range(2)]))
                    h0 = 4 * (j // 2) + j % 2
                    g0 = hf * 8 + h0
                    out.append(task(sc, lambda t, lo=lo, hi=hi: t.rearrange("p (e c) -> p e c", e=2)[:, :, lo:hi],
                                    B_SCALE, BG[:].rearrange("p (h c) -> p h c", h=8)[:, h0:h0 + 3:2, lo:hi], hd, tn, va,
                                    ("copy", heads_of(bON, b, g0, 2), 128),
                                    (bMN[:, b, g0:g0 + 3:2], 2, b)))
            return out
        for r in range(TT):
            for q in range(2):
                sc, hd, tn, va = [], [], [], []
                for e in range(4):
                    h = 2 * e + q
                    j, s = e, 64 * q
                    sc.append((e * P, e * P + P, bQT[s:s + 64, j, r:SEQ:4], bKT[s:s + 64, j, r:SEQ:4]))
                    gh = hf * 8 + h
                    hd.append((e * P, e * P + P, bM[:, g, r, gh:gh + 1], bD[:, g, r, gh:gh + 1]))
                    tn.append((e * P, P))
                    va.append((e * 64, [(P, e * P, bV[:, r, h * 64:h * 64 + 64])]))
                g0 = hf * 8 + q
                out.append(task(sc, lambda t: t.rearrange("p (e c) -> p e c", e=4), B_SCALE,
                                BG[:, 0:1024].rearrange("p (h c) -> p h c", h=8)[:, q:8:2, :], hd, tn, va,
                                ("copy", heads_of(bO[g], r, g0, 4), 256),
                                (bM[:, g, r, g0:g0 + 7:2], 4, r)))
        return out

    def row_task(out, q, k, scale, bias, W, v, h, t, gate=None, first=True, last=True):
        n = len(out)
        s, o = n % 8, 64 * (h % 2)
        tk = task([(0, W, q, k)], lambda t, W=W: t[:, 0:W], scale, bias,
                  [(0, W, NM[:, s:s + 1], DS[:, s:s + 1])],
                  [(P * w, P) for w in range(W // P)],
                  [v(w) for w in range(W // P)], gate, (NM[:, s:s + 1], 1, 0))
        tk.update(bank=6 + (h // 2) % 2, rows=slice(o, o + 64), cols=slice(P * t, P * t + P), first=first, last=last,
                  pair=h // 2, opens=h % 2 == 0 and t == 0 and first, closes=h % 2 == 1 and t == TT - 1 and last)
        out.append(tk)

    def mem_tasks(out, q_mem, kv):
        for h in range(4):
            for t in range(TT):
                j, s = h // 2, 64 * (h % 2)
                row_task(out, q_mem[s:s + 64, j, P * t:P * t + P], kv[s:s + 64, j, :], HD_SCALE, None, N_MEM,
                         lambda w, h=h: kv[:, 2 + w, h * 64:h * 64 + 64], HEADS + h, t)
        return out

    def mla_tasks():
        out = []
        for h in range(HEADS):
            for t in range(TT):
                W = P * (t + 1)
                row_task(out, qT[0:96, h, P * t:P * t + P], kT[0:96, h, 0:W], MLA_SCALE,
                         mCM[:, MW - P * t:MW - P * t + W], W, lambda w, h=h: mV[:, w, h * 64:h * 64 + 64], h, t)
        return mem_tasks(out, mQM, mKV)

    def nsa_tasks():
        out = []
        for h in range(HEADS):
            g, i = h // 6, h % 6
            for t in range(TT):
                for br in range(2):
                    W = P * (t + 1)
                    row_task(out, nQT[64 * g:64 * g + 64, i, P * t:P * t + P], nK[64 * g:64 * g + 64, br, 0:W],
                             HD_SCALE, nAB[h % 2][:, MW - P * t:MW - P * t + W], W,
                             lambda w, g=g, br=br: nV[:, w, br, g * 64:g * 64 + 64], h, t,
                             nG[:, t, h, br + 1:br + 2], br == 0, br == 1)
        return mem_tasks(out, nQM, nKV)

    ATT = {}
    for g in range(3):
        for hf in range(2):
            ATT[("b", g, hf)] = (dilated_tasks(g, hf), bSB, bPT)
    ATT["mla"] = (mla_tasks(), mSB, mPT)
    ATT["nsa"] = (nsa_tasks(), nSB, nPT)

    mixes = {"b": (bO[0], bHH, bHL, True)}
    MIX = {"mla": (mHH, mHL), "nsa": (nHH, nHL)}

    block = ctx.enter_context(nc.Block())

    @block.sync
    def _(sp):
        sp.dma_start(ident[:], A["ident"]).then_inc(sem["ident_loaded"], step("ident_loaded", by=16))
        for t in range(TT):
            sp.dma_start(X[:, t, :], A["x"][t * P:(t + 1) * P, :]).then_inc(sem[f"x_loaded{t}"], step(f"x_loaded{t}", by=16))
        for g, pieces in enumerate(panels):
            if g >= 2:
                sp.wait_ge(sem["w_low_ready"], at("w_low_ready", g - 2))
            for off, n, pitch, w, src in pieces:
                if pitch == w:
                    dst = RAW[g % 2][:, off:off + n * w].rearrange("p (n w) -> p n w", n=n)
                else:
                    dst = bass.AP(RAW[g % 2], off, [[2048, P], [pitch, n], [1, w]])
                sp.dma_start(dst, src).then_inc(sem[f"panel_loaded{g % 2}"], step(f"panel_loaded{g % 2}", g, by=16))
        for t in range(TT):
            sp.wait_ge(sem["rows_done"], at("rows_done", ("l12", t)))
            sp.dma_start(out[t * P:(t + 1) * P, :], X[:, t, :]).then_inc(sem["stored"], step("stored", by=16))
        sp.wait_ge(sem["stored"], 16 * TT)

    @block.tensor
    def _(pe):
        def mm3(o, lh, ll, rh, rl, start, stop):
            pe.matmul(o, lh, rh, start=start, stop=False, skip_group_check=True)
            pe.matmul(o, lh, rl, start=False, stop=False, skip_group_check=True)
            return pe.matmul(o, ll, rh, start=False, stop=stop, skip_group_check=True)

        def early_half(name, jobs, s, panel_done=True):
            g = ids[name][0]
            pe.wait_ge(sem["w_low_ready"], at("w_low_ready", g))
            for a in (0, 1):
                pe.wait_ge(sem["xt_ready"], at("xt_ready", (s, 2 * a + 1)))
                cols = slice(256 * a, 256 * a + 256)
                for o, operands in jobs:
                    for kk in range(4):
                        lh, ll, rh, rl = operands(kk, kk, WH[g % 2], WL[g % 2])
                        pe.matmul(o[:, cols], lh, rh[:, cols], start=a == 0 and kk == 0, stop=False,
                                  skip_group_check=True)
                        pe.matmul(o[:, cols], lh, rl[:, cols], start=False, stop=False, skip_group_check=True)
                        ins = pe.matmul(o[:, cols], ll, rh[:, cols], start=False, stop=False, skip_group_check=True)
            if panel_done:
                ins.then_inc(sem["product_done"], step("product_done", ("panel", g)))

        def product(name, nk, jobs, free, after_rows=None, between=None):
            gs = ids[name]
            for i, g in enumerate(gs):
                if between and i == 1:
                    between()
                if after_rows and i == 0:
                    early_half(name, jobs, after_rows)
                    continue
                pe.wait_ge(sem["w_low_ready"], at("w_low_ready", g))
                for j, (o, operands) in enumerate(jobs):
                    if i == 0:
                        free(j)
                    for kk in range(nk):
                        ins = mm3(o, *operands(kk, i * nk + kk, WH[g % 2], WL[g % 2]),
                                  i == 0 and kk == 0, i == len(gs) - 1 and kk == nk - 1)
                    last = i == len(gs) - 1
                    labels = ([("acc", name, j)] if last else []) + ([("panel", g)] if j == len(jobs) - 1 else [])
                    if labels:
                        ins.then_inc(sem["product_done"], step("product_done", *labels))

        def feature(w, c, xh, xl, n=SEQ):
            def operands(kk, k, wh, wl):
                a = kk * w + c
                return wh[:, a:a + P], wl[:, a:a + P], xh[:, k, 0:n], xl[:, k, 0:n]
            return operands

        def token(w, c, n, tokens, xh, xl):
            def operands(kk, k, wh, wl):
                a = kk * w + c
                return xh[:, k, tokens], xl[:, k, tokens], wh[:, a:a + n], wl[:, a:a + n]
            return operands

        def down(name, kt, hh, hl, ready, free, s):
            gs = ids[name]

            def accumulate(g, i, kk, t, start, stop):
                k = 2 * i + kk
                for half in range(2):
                    a = kk * D + half * 512
                    ins = mm3(ps[2 * t + half][:], hh[:, k, t * P:t * P + P], hl[:, k, t * P:t * P + P],
                              WH[g % 2][:, a:a + 512], WL[g % 2][:, a:a + 512], start, stop)
                return ins
            free()
            for i, g in enumerate(gs[:-2]):
                pe.wait_ge(sem["w_low_ready"], at("w_low_ready", g))
                for kk in range(2):
                    ready(2 * i + kk)
                    for t in range(TT):
                        ins = accumulate(g, i, kk, t, i == 0 and kk == 0, False)
                ins.then_inc(sem["product_done"], step("product_done", ("panel", g)))
            for t in range(TT):
                if t >= 2:
                    turn_row(s, t - 2)
                for i in (len(gs) - 2, len(gs) - 1):
                    g = gs[i]
                    if t == 0:
                        pe.wait_ge(sem["w_low_ready"], at("w_low_ready", g))
                    for kk in range(2):
                        ready(2 * i + kk)
                        ins = accumulate(g, i, kk, t, False, i == len(gs) - 1 and kk == 1)
                labels = [("acc", name, t)]
                if t == TT - 1:
                    labels += [("panel", gs[-2]), ("panel", gs[-1])]
                ins.then_inc(sem["product_done"], step("product_done", *labels))
            for t in (TT - 2, TT - 1):
                turn_row(s, t)

        def turn_row(s, t):
            if s == "l12":
                return
            kind = ROWS[s][0]
            pe.wait_ge(sem["rows_done"], at("rows_done", (s, t)))
            src = R[t % 2][:, :] if kind in ("pre", "post_pre") else X[:, t, :]
            for k in range(KD):
                ins = pe.transpose(ps[2 * t + k // 4][:, (k % 4) * P:(k % 4 + 1) * P],
                                   src[:, k * P:(k + 1) * P], ident[:])
            ins.then_inc(sem["turned"], step("turned", (s, t)))

        def attend(name, first, last):
            tasks = ATT[name][0]
            SBs, PTs = ATT[name][1:]
            N = len(tasks)
            for n in range(first, last):
                if n < N:
                    tk = tasks[n]
                    if name[0] == "b" and n < 4:
                        pe.wait_ge(sem["bv_read"], at("bv_read", (name[1], name[2], n)))
                    if n >= 4:
                        pe.wait_ge(sem["masked"], at("masked", (name, n - 4)))
                    for a, b, q, k in tk["scores"]:
                        ins = pe.matmul(ps[n % 4][:, a:b], q, k, start=True, stop=True)
                    ins.then_inc(sem["scored"], step("scored", (name, n)))
                if 3 <= n < N + 3:
                    m = n - 3
                    pe.wait_ge(sem["exp_done"], at("exp_done", (name, m)))
                    if m >= 2:
                        pe.wait_ge(sem["pt_copied"], at("pt_copied", (name, m - 2)))
                    for i, (a, w) in enumerate(tasks[m]["turns"]):
                        ins = pe.transpose(ps[4 + m % 2][0:w, i * P:(i + 1) * P], SBs[m % 4][:, a:a + w], ident[:])
                    ins.then_inc(sem["p_turned"], step("p_turned", (name, m)))
                if n >= 4:
                    m = n - 4
                    pe.wait_ge(sem["pt_copied"], at("pt_copied", (name, m)))
                    if m >= 2:
                        pe.wait_ge(sem["o_read"], at("o_read", (name, m - 2)))
                    for c, parts in tasks[m]["values"]:
                        for i, (K, a, v) in enumerate(parts):
                            ins = pe.matmul(ps[6 + m % 2][:, c:c + 64], PTs[m % 2][0:K, a:a + P], v,
                                            start=i == 0, stop=i == len(parts) - 1)
                    ins.then_inc(sem["weighted"], step("weighted", (name, m)))

        def attend_pairs(name):
            tasks, SBs, PTs = ATT[name]
            N = len(tasks)
            for n in range(N + 5):
                if n < N:
                    tk = tasks[n]
                    if n >= 4:
                        pe.wait_ge(sem["masked"], at("masked", (name, n - 4)))
                    for a, b, q, k in tk["scores"]:
                        ins = pe.matmul(ps[n % 4][:, a:b], q, k, start=True, stop=True)
                    ins.then_inc(sem["scored"], step("scored", (name, n)))
                if 4 <= n < N + 4:
                    m = n - 4
                    pe.wait_ge(sem["p_scaled"], at("p_scaled", (name, m)))
                    if m >= 2:
                        pe.wait_ge(sem["pt_copied"], at("pt_copied", (name, m - 2)))
                    for i, (a, w) in enumerate(tasks[m]["turns"]):
                        ins = pe.transpose(ps[4 + m % 2][0:w, i * P:(i + 1) * P], SBs[m % 6][:, a:a + w], ident[:])
                    ins.then_inc(sem["p_turned"], step("p_turned", (name, m)))
                if n >= 5:
                    m = n - 5
                    tk = tasks[m]
                    pe.wait_ge(sem["pt_copied"], at("pt_copied", (name, m)))
                    if tk["opens"] and tk["pair"] >= 2:
                        pe.wait_ge(sem["pair_split"], at("pair_split", (name, tk["pair"] - 2)))
                    parts = tk["values"]
                    for i, v in enumerate(parts):
                        ins = pe.matmul(ps[tk["bank"]][tk["rows"], tk["cols"]], v, PTs[m % 2][:, i * P:(i + 1) * P],
                                        start=tk["first"] and i == 0, stop=tk["last"] and i == len(parts) - 1)
                    ins.then_inc(sem["weighted"], step("weighted", (name, m)))

        def attend_tail(name):
            N = len(ATT[name][0])
            attend(name, N, N + 4)

        def turn_mix(name):
            src = mixes[name][0]
            for t in range(TT):
                pe.wait_ge(sem["mix_ready"], at("mix_ready", (name, t)))
                for k in range(KD):
                    ins = pe.transpose(ps[2 * t + k // 4][:, (k % 4) * P:(k % 4 + 1) * P],
                                       src[:, t, k * P:(k + 1) * P], ident[:])
                ins.then_inc(sem["turned"], step("turned", (name, t)))

        pe.wait_ge(sem["ident_loaded"], at("ident_loaded"))
        pe.wait_ge(sem["hot_loaded"], at("hot_loaded"))
        pe.wait_ge(sem["table_ones"], at("table_ones"))
        for g in range(3):
            o = ps[0][0:16, 0:384] if g == 0 else ps[1][0:16, (g - 1) * 256:g * 256]
            ins = pe.matmul(o, RB[0:33, 16 * g:16 * g + 16], HOT[0:33, BIAS_AT[g]:BIAS_AT[g] + BIAS_W[g]],
                            start=True, stop=True)
        ins.then_inc(sem["bias_multiplied"], step("bias_multiplied"))
        pe.wait_ge(sem["mem_loaded"], at("mem_loaded"))
        for k in range(KD):
            for m in range(2):
                ins = pe.transpose(ps[2 + k // 2][:, (k % 2) * 256 + m * P:(k % 2) * 256 + m * P + P],
                                   MEM[:, m, k * P:(k + 1) * P], ident[:])
            if k % 2:
                ins.then_inc(sem["mem_turned"], step("mem_turned", k // 2))
        pe.wait_ge(sem["mem_split"], at("mem_split", 3))
        pe.wait_ge(sem["bias_copied"], at("bias_copied"))
        for l in range(2):
            banks = (0, 1, 6, 7) if l == 0 else (2, 3, 4, 5)
            jobs = [(ps[banks[j]][:, 0:256], feature(512, j * P, MTH, MTL, N_MEM)) for j in range(2)]
            jobs += [(ps[banks[2 + m]][:, 0:256], token(512, 256, 256, slice(m * P, m * P + P), MTH, MTL))
                     for m in range(2)]
            product(("mem", l), 4, jobs, lambda j: None)
        pe.wait_ge(sem["ws_loaded"], at("ws_loaded"))
        pe.wait_ge(sem["mem_kv_copied"], at("mem_kv_copied", (0, 3)))
        pe.wait_ge(sem["mem_kv_copied"], at("mem_kv_copied", (1, 3)))
        for h in range(A_HEADS):
            ins = pe.transpose(ps[h // 4][:, (h % 4) * P:(h % 4 + 1) * P], WS[:, h, :], ident[:])
            if h % 4 == 3:
                ins.then_inc(sem["ws_turned"], step("ws_turned", h // 4))
        pe.wait_ge(sem["ws_copied"], at("ws_copied", 3))
        for t in range(TT):
            turn_row("s0", t)

        setA, setB = (0, 1, 2, 3), (4, 5, 6, 7)

        def tile(t):
            return slice(t * P, t * P + P)

        for c in range(4):
            banks = setA if c % 2 == 0 else setB
            product(("v", c), 4, [(ps[banks[t]][:], token(512, 0, 512, tile(t), XTH, XTL)) for t in range(TT)],
                    lambda j, c=c: pe.wait_ge(sem["v_read"], at("v_read", (c - 2, j))) if c >= 2 else
                    (pe.wait_ge(sem["xt_ready"], at("xt_ready", ("s0", j))) if c == 0 else None))
        for c in range(2):
            banks = setA if c % 2 == 0 else setB
            product(("u", c), 4, [(ps[banks[j]][:], feature(512, j * P, XTH, XTL)) for j in range(4)],
                    lambda j, c=c: pe.wait_ge(sem["v_read"], at("v_read", (c + 2, j))))
        for h in range(A_HEADS):
            b = h % 8
            pe.wait_ge(sem["v_normed"], at("v_normed", h // 8))
            if h < 8:
                pe.wait_ge(sem["u_read"], at("u_read", (h // 4, h % 4)))
            else:
                pe.wait_ge(sem["spatial_read"], at("spatial_read", h - 8))
            for c in range(TT):
                ins = pe.matmul(ps[b][:, tile(c)], V[:, c, h * P:h * P + P], WST[:, h, :], start=True, stop=True)
            ins.then_inc(sem["spatial_done"], step("spatial_done", h))
        for c in range(4):
            if c >= 2:
                product(("u", c), 4, [(ps[setB[j]][:], feature(512, j * P, XTH, XTL)) for j in range(4)],
                        lambda j, c=c: pe.wait_ge(sem["spatial_read"], at("spatial_read", 12 + j)) if c == 2 else pe.wait_ge(sem["u_read"], at("u_read", (c - 1, j))))
            product(("g", c), 4, [(ps[setA[j]][:], feature(512, j * P, XTH, XTL)) for j in range(4)],
                    lambda j, c=c: pe.wait_ge(sem["spatial_read"], at("spatial_read", 8 + j)) if c == 0 else pe.wait_ge(sem["g_read"], at("g_read", (c - 1, j))))

        def gmlp_free():
            pe.wait_ge(sem["u_read"], at("u_read", (3, 3)))
            pe.wait_ge(sem["g_read"], at("g_read", (3, 3)))
        down("a_out", 16, YH, YL, lambda k: pe.wait_ge(sem["y_split"], at("y_split", k)), gmlp_free, "s1")

        for g in range(3):
            for hf in range(2):
                prev = None if (g, hf) == (0, 0) else (("b", g, hf - 1) if hf else ("b", g - 1, 1))
                if prev:
                    pe.wait_ge(sem["masked"], at("masked", (prev, len(ATT[prev][0]) - 1)))
                product(("b", g, hf, "q"), 4, [(ps[setA[j]][:], feature(512, j * P, XTH, XTL)) for j in range(4)],
                        lambda j: None, None if prev else "s1",
                        (lambda prev=prev: attend_tail(prev)) if prev else None)
                product(("b", g, hf, "k"), 4, [(ps[setB[j]][:], feature(512, j * P, XTH, XTL)) for j in range(4)],
                        lambda j, prev=prev: pe.wait_ge(sem["o_read"], at("o_read", (prev, len(ATT[prev][0]) - 1))) if prev else None)
                if g == 0:
                    pe.wait_ge(sem["wrap_ready"], at("wrap_ready"))
                    jobs = [(ps[setA[0]][:], token(512, 0, 512, slice(0, P), XWH, XWL))]
                    jobs += [(ps[setA[t]][:], token(512, 0, 512, slice(t * P - 64, t * P + 64), XTH, XTL))
                             for t in range(1, TT)]
                else:
                    jobs = [(ps[setA[t]][:], token(512, 0, 512, slice(t, SEQ, 4), XTH, XTL)) for t in range(TT)]
                product(("b", g, hf, "v"), 4, jobs, lambda j, g=g, hf=hf: pe.wait_ge(sem["bq_read"], at("bq_read", (g, hf, j))))
                pe.wait_ge(sem["bk_read"], at("bk_read", (g, hf, 3)))
                attend(("b", g, hf), 0, len(ATT["b", g, hf][0]))
        last = ("b", 2, 1)
        for c in range(2):
            product(("b_gate", c), 4, [(ps[4 * c + t][:], token(512, 0, 512, slice(t, SEQ, 4), XTH, XTL))
                                       for t in range(TT)],
                    lambda j, c=c: pe.wait_ge(sem["masked"], at("masked", (last, len(ATT[last][0]) - 1))) if c == 0 else
                    pe.wait_ge(sem["o_read"], at("o_read", (last, len(ATT[last][0]) - 1))),
                    None, (lambda: attend_tail(last)) if c == 0 else None)
        pe.wait_ge(sem["bgate_read"], at("bgate_read", 1))
        turn_mix("b")
        down("b_out", 8, bHH, bHL, lambda k: None, lambda: pe.wait_ge(sem["mix_split"], at("mix_split", ("b", TT - 1))), "s2")

        def ffn(l, i, s, then, between=None):
            f = (l, i)
            for c in range(5):
                product(("gate", l, i, c), 4, [(ps[setA[j]][:], feature(512, j * P, XTH, XTL)) for j in range(4)],
                        lambda j, c=c: pe.wait_ge(sem["gate_read"], at("gate_read", (f, c - 1, j))) if c else None,
                        s if c == 0 else None)
                if between and c == 0:
                    between()
                product(("up", l, i, c), 4, [(ps[setB[j]][:], feature(512, j * P, XTH, XTL)) for j in range(4)],
                        lambda j, c=c: pe.wait_ge(sem["up_read"], at("up_read", (f, c - 1, j))) if c else None)
            product(("last", l, i), 4, [(ps[setA[j]][:], feature(512, j * P, XTH, XTL)) for j in range(4)],
                    lambda j: pe.wait_ge(sem["gate_read"], at("gate_read", (f, 4, j))))

            def free():
                pe.wait_ge(sem["up_read"], at("up_read", (f, 5, 1)))
            down(("down", l, i), KF, HTH, HTL,
                 lambda k: pe.wait_ge(sem["hidden_split"], at("hidden_split", (f, k // 4))) if k % 4 == 0 else None, free, then)

        ffn(0, 0, "s2", "l00")
        product("mla_in", 4, [(ps[t][:, 0:416], token(416, 0, 416, tile(t), XTH, XTL)) for t in range(TT)],
                lambda j: pe.wait_ge(sem["xt_ready"], at("xt_ready", ("l00", j))))
        product("mla_mem", 8, [(ps[4 + j][:], feature(256, j * P, XTH, XTL)) for j in range(2)], lambda j: None)
        for t in range(TT):
            pe.wait_ge(sem["c_normed"], at("c_normed", t))
            if t == 0:
                pe.wait_ge(sem["c_read"], at("c_read", TT - 1))
            for j in range(3):
                ins = pe.transpose(ps[j][:, tile(t)], ZR[:, t, j * P:(j + 1) * P], ident[:])
        ins.then_inc(sem["c_turned"], step("c_turned"))
        pe.wait_ge(sem["c_split"], at("c_split", 2))
        pe.wait_ge(sem["qmem_read"], at("qmem_read", 1))
        product("uq", 2, [(ps[2 * t + n][:], token(1024, 512 * n, 512, tile(t), CTH, CTL))
                          for t in range(TT) for n in range(2)], lambda j: None)
        product("uq_tail", 2, [(ps[2 * t][:, 0:128], token(128, 0, 128, tile(t), CTH, CTL)) for t in range(TT)],
                lambda j: pe.wait_ge(sem["uq_read"], at("uq_read", (j, 0))))
        for which in ("q", "k"):
            if which == "k":
                def kv_operands(t, n):
                    def operands(kk, k, wh, wl):
                        return (CTH[:, 2, tile(t)], CTL[:, 2, tile(t)], wh[:, n * 512:n * 512 + 512],
                                wl[:, n * 512:n * 512 + 512])
                    return operands

                def kv_free(j):
                    pe.wait_ge(sem["heads_turned"], at("heads_turned", ("q", 11)))
                    if j >= 8:
                        pe.wait_ge(sem["ukv_read_k"], at("ukv_read_k", j - 8))
                        pe.wait_ge(sem["ukv_read_v"], at("ukv_read_v", j - 8))
                product("ukv", 1, [(ps[(3 * t + n) % 8][:], kv_operands(t, n)) for t in range(TT) for n in range(3)],
                        kv_free)
                pe.wait_ge(sem["ukv_read_v"], at("ukv_read_v", 11))
            for h in range(HEADS):
                if which == "q" and h == 0:
                    pe.wait_ge(sem["uq_tail_read"], at("uq_tail_read", 3))
                    pe.wait_ge(sem["uq_read"], at("uq_read", (3, 1)))
                if h == 0:
                    pe.wait_ge(sem["roped"], at("roped", which))
                if h >= 8:
                    pe.wait_ge(sem["heads_turned"], at("heads_turned", (which, h - 8)))
                for t in range(TT):
                    ins = pe.transpose(ps[h % 8][0:96, tile(t)], mF[:, t, h, :], ident[:])
                ins.then_inc(sem["head_turned"], step("head_turned", (which, h)))
        pe.wait_ge(sem["heads_turned"], at("heads_turned", ("k", 11)))
        pe.wait_ge(sem["mix_const0"], at("mix_const0"))
        pe.wait_ge(sem["mem_kv_back"], at("mem_kv_back", 0))
        attend_pairs("mla")
        down(("w_out", 0), 8, mHH, mHL, lambda k: None,
             lambda: pe.wait_ge(sem["pair_split"], at("pair_split", ("mla", KD - 1))), "l01")
        ffn(0, 1, "l01", "l02")


        def shared_product(name, w, f_jobs, t_bank, t_col, after_rows=None):
            gs = ids[name]
            jobs = [(ps[b][:], feature(w, c, XTH, XTL)) for b, c in f_jobs]
            for i, g in enumerate(gs):
                pe.wait_ge(sem["w_low_ready"], at("w_low_ready", g))
                if i == 0 and after_rows:
                    early_half(name, jobs, after_rows, panel_done=False)
                else:
                    for o, operands in jobs:
                        for kk in range(4):
                            mm3(o, *operands(kk, 4 * i + kk, WH[g % 2], WL[g % 2]), i == 0 and kk == 0, i == 1 and kk == 3)
                for t in range(TT):
                    for kk in range(4):
                        ins = mm3(ps[t_bank][:, tile(t)],
                                  *token(w, t_col, 128, tile(t), XTH, XTL)(kk, 4 * i + kk, WH[g % 2], WL[g % 2]),
                                  i == 0 and t == 0 and kk == 0, i == 1 and kk == 3)
                labels = [("panel", g)] + ([("acc", name, 0)] if i == 1 else [])
                ins.then_inc(sem["product_done"], step("product_done", *labels))

        shared_product("kv_a", 512, [(0, 0), (1, 128), (2, 256)], 3, 384, "l02")
        shared_product("kv_b", 256, [(4, 0)], 5, 128)
        pe.wait_ge(sem["w1_loaded"], at("w1_loaded"))
        pe.wait_ge(sem["blocks_ready"], at("blocks_ready"))
        for j in range(2):
            for ht in range(2):
                n = 2 * j + ht
                for k in range(LT):
                    ins = pe.matmul(ps[6][:, n * 64:n * 64 + 2 * N_CMP], W1[j][:, k, ht * P:(ht + 1) * P],
                                    FZ[:, j, k, :, :].rearrange("p g n -> p (g n)"), start=k == 0, stop=k == LT - 1)
        ins.then_inc(sem["cmp_hidden_done"], step("cmp_hidden_done"))

        def compress_out():
            pe.wait_ge(sem["cmp_hidden_ready"], at("cmp_hidden_ready"))
            pe.wait_ge(sem["kv_copied"], at("kv_copied"))
            for g in range(2):
                for ht in range(2):
                    pe.matmul(ps[4][64 * g:64 * g + 64, 0:NC], W2[:, 0, ht, :], H1[:, 0, g, ht, 0, :],
                              start=ht == 0, stop=ht == 1)
            for g in range(2):
                for ht in range(2):
                    ins = pe.matmul(ps[5][:, g * 64:64 + g * 64],
                                    H1[:, 1, g, ht].rearrange("p r n -> p (r n)"), W2[:, 1, ht, :],
                                    start=ht == 0, stop=ht == 1)
            ins.then_inc(sem["cmp_done"], step("cmp_done"))
            pe.wait_ge(sem["cmp_kept"], at("cmp_kept"))

        ffn(1, 0, "l02", "l10", compress_out)

        product("nsa_a", 4, [(ps[setA[j]][:], feature(512, j * P, XTH, XTL)) for j in range(4)], lambda j: None, "l10")
        product("nsa_b", 4, [(ps[setB[j]][:], feature(512, j * P, XTH, XTL)) for j in range(4)], lambda j: None)
        def gate_operands(kk, k, wh, wl):
            return wh[:, 36 * kk:36 * kk + 36], wl[:, 36 * kk:36 * kk + 36], XTH[:, k, :], XTL[:, k, :]
        product("nsa_gates", 8, [(ps[4][0:36, :], gate_operands)], lambda j: pe.wait_ge(sem["nq_read"], at("nq_read", ("b", 1))))
        pe.wait_ge(sem["nsa_const"], at("nsa_const"))
        pe.wait_ge(sem["cmp_v_spread"], at("cmp_v_spread"))
        for t in range(TT):
            for i in range(6):
                ins = pe.matmul(ps[t][:, i * 2 * NC:(i + 1) * 2 * NC], nQT[:, i, tile(t)],
                                KBD[:].rearrange("p g n -> p (g n)"), start=True, stop=True)
            ins.then_inc(sem["cmp_scored"], step("cmp_scored", t))
        pe.wait_ge(sem["gates_t_read"], at("gates_t_read"))
        for t in range(TT):
            ins = pe.transpose(ps[5][:, 36 * t:36 * t + 36], nGT[0:36, tile(t)], ident[0:36, 0:36])
        ins.then_inc(sem["gates_turned"], step("gates_turned"))
        pe.wait_ge(sem["nq_read"], at("nq_read", ("b", 3)))
        for t in range(TT + 1):
            if t < TT:
                pe.wait_ge(sem["cmp_p_ready"], at("cmp_p_ready", t))
                for u in range(3):
                    ins = pe.transpose(ps[6 + t % 2][:, u * P:(u + 1) * P],
                                       nCPs[t % 2][:, 4 * u:4 * u + 4, :].rearrange("p h n -> p (h n)"), ident[:])
                ins.then_inc(sem["cmp_p_turned"], step("cmp_p_turned", t))
            if t >= 1:
                m = t - 1
                pe.wait_ge(sem["cmp_pt_copied"], at("cmp_pt_copied", m))
                if m:
                    pe.wait_ge(sem["cmp_o_read"], at("cmp_o_read", m - 1))
                for j in range(6):
                    ins = pe.matmul(ps[4 + j // 4][:, (j % 4) * P:(j % 4 + 1) * P], VBD[:, j // 3, j % 2, :],
                                    nCTs[m % 2][:, j // 2, :], start=True, stop=True)
                ins.then_inc(sem["cmp_weighted"], step("cmp_weighted", m))
        pe.wait_ge(sem["cmp_o_read"], at("cmp_o_read", TT - 1))
        pe.wait_ge(sem["mem_kv_back"], at("mem_kv_back", 1))
        attend_pairs("nsa")
        down(("w_out", 1), 8, nHH, nHL, lambda k: None,
             lambda: pe.wait_ge(sem["pair_split"], at("pair_split", ("nsa", KD - 1))), "l11")
        ffn(1, 1, "l11", "l12")

    @block.scalar
    def _(act):
        done = [0]

        def prepare(g):
            while done[0] <= min(g, len(panels) - 1):
                n = done[0]
                act.wait_ge(sem[f"panel_loaded{n % 2}"], at(f"panel_loaded{n % 2}", n))
                if n >= 2:
                    act.wait_ge(sem["product_done"], at("product_done", ("panel", n - 2)))
                w = widths[n]
                act.activation(WH[n % 2][:, 0:w], RAW[n % 2][:, 0:w], ACT.Copy).then_inc(sem["w_high_ready"], step("w_high_ready", n))
                done[0] += 1

        def after(name, j, labels_only=False):
            if j == 0:
                prepare(ids[name][-1] + 1)
            act.wait_ge(sem["product_done"], at("product_done", ("acc", name, j)))

        def split_turned(s, t, hh, perm=False):
            act.wait_ge(sem["turned"], at("turned", (s, t)))
            for b in range(2):
                dst = hh[:, 4 * b:4 * b + 4, t:SEQ:4] if perm else hh[:, 4 * b:4 * b + 4, t * P:(t + 1) * P]
                ins = act.activation(dst, ps[2 * t + b][:].rearrange("p (k n) -> p k n", k=4), ACT.Copy)
            ins.then_inc(sem["turned_high"], step("turned_high", (s, t)))

        def rows(s, y=None):
            kind = ROWS[s][0]
            if y:
                prepare(ids[y][-1])
            for t in range(TT + 1):
                if t < TT:
                    if kind in ("post", "post_pre"):
                        act.wait_ge(sem["product_done"], at("product_done", ("acc", y, t)))
                        if t >= 2 and kind == "post_pre":
                            act.wait_ge(sem["turned"], at("turned", (s, t - 2)))
                        if t >= 2 and kind == "post":
                            act.wait_ge(sem["rows_done"], at("rows_done", (s, t - 2)))
                        for half in range(2):
                            ins = act.activation(R[t % 2][:, 512 * half:512 * half + 512], ps[2 * t + half][:], ACT.Square,
                                                 accum_out=SS[:, 4 * t + half:4 * t + half + 1])
                        ins.then_inc(sem["squared"], step("squared", (s, t)))
                    if kind == "pre":
                        act.wait_ge(sem[f"x_loaded{t}"], at(f"x_loaded{t}"))
                        if t >= 2:
                            act.wait_ge(sem["turned"], at("turned", (s, t - 2)))
                    if kind == "post_pre":
                        act.wait_ge(sem["x_added"], at("x_added", (s, t)))
                    if kind in ("pre", "post_pre"):
                        act.activation(R[t % 2][:], X[:, t, :], ACT.Square,
                                              accum_out=SS[:, 4 * t + 2:4 * t + 3]).then_inc(sem["squared_x"], step("squared_x", (s, t)))
                if y and t == TT - 1:
                    act.wait_ge(sem["product_done"], at("product_done", ("acc", y, t)))
                    prepare(ids[y][-1] + 1)
                if t >= 1 and s != "l12":
                    split_turned(s, t - 1, XTH)
                if y and t == TT - 1:
                    prepare(ids[y][-1] + 2)

        def attend(name):
            tasks, SBs, PTs = ATT[name]
            N = len(tasks)
            for n in range(N + 2):
                if n < N:
                    act.wait_ge(sem["maxed"], at("maxed", (name, n)))
                    for a, b, m, d in tasks[n]["heads"]:
                        ins = act.activation(SBs[n % 4][:, a:b], SBs[n % 4][:, a:b], ACT.Exp, bias=m, accum_out=d)
                    ins.then_inc(sem["exp_done"], step("exp_done", (name, n)))
                if n == 3:
                    prepare(ids[name + ("v",)][-1] + 2)
                if n >= 2:
                    m = n - 2
                    act.wait_ge(sem["p_turned"], at("p_turned", (name, m)))
                    if m >= 2:
                        act.wait_ge(sem["weighted"], at("weighted", (name, m - 2)))
                    w = P * len(tasks[m]["turns"])
                    act.activation(PTs[m % 2][:, 0:w], ps[4 + m % 2][:, 0:w], ACT.Copy).then_inc(sem["pt_copied"], step("pt_copied", (name, m)))

        def attend_pairs(name):
            tasks, SBs, PTs = ATT[name]
            N = len(tasks)
            HH = MIX[name][0]
            for n in range(N + 6):
                if n < N:
                    act.wait_ge(sem["maxed"], at("maxed", (name, n)))
                    for a, b, m, d in tasks[n]["heads"]:
                        ins = act.activation(SBs[n % 6][:, a:b], SBs[n % 6][:, a:b], ACT.Exp, bias=m, accum_out=d)
                    ins.then_inc(sem["exp_done"], step("exp_done", (name, n)))
                if 3 <= n < N + 3:
                    m = n - 3
                    act.wait_ge(sem["p_turned"], at("p_turned", (name, m)))
                    if m >= 2:
                        act.wait_ge(sem["weighted"], at("weighted", (name, m - 2)))
                    w = P * len(tasks[m]["turns"])
                    act.activation(PTs[m % 2][:, 0:w], ps[4 + m % 2][:, 0:w], ACT.Copy).then_inc(sem["pt_copied"], step("pt_copied", (name, m)))
                if n >= 6 and tasks[n - 6]["closes"]:
                    j = tasks[n - 6]["pair"]
                    if name == "nsa" and j < 6:
                        act.wait_ge(sem["pair_summed"], at("pair_summed", j))
                        src = nOC[:, j, :]
                    else:
                        act.wait_ge(sem["weighted"], at("weighted", (name, n - 6)))
                        src = ps[tasks[n - 6]["bank"]][:]
                    act.activation(HH[:, j, :], src, ACT.Copy).then_inc(sem["pair_high"], step("pair_high", (name, j)))

        def turned_mix(name):
            _, hh, _, perm = mixes[name]
            for t in range(TT):
                split_turned(name, t, hh, perm)

        for b in range(4):
            act.wait_ge(sem["mem_turned"], at("mem_turned", b))
            act.activation(MTH[:, 2 * b:2 * b + 2, :], ps[2 + b][:].rearrange("p (k n) -> p k n", k=2), ACT.Copy).then_inc(sem["mem_high"], step("mem_high", b))
        for l in range(2):
            banks = (0, 1, 6, 7) if l == 0 else (2, 3, 4, 5)
            for j in range(4):
                after(("mem", l), j)
                act.activation(KVS[:, l, j, :], ps[banks[j]][:, 0:256], ACT.Copy).then_inc(sem["mem_kv_copied"], step("mem_kv_copied", (l, j)))
            prepare(ids["mem", l][-1] + 2)
        rows("s0")

        for c in range(4):
            for t in range(TT):
                after(("v", c), t)
                act.activation(V[:, t, 512 * c:512 * c + 512], ps[4 * (c % 2) + t][:], ACT.Gelu_apprx_tanh).then_inc(sem["v_read"], step("v_read", (c, t)))
            prepare(ids["v", c][-1] + 2)

        def u_part(c, bank):
            for j in range(4):
                after(("u", c), j)
                if j == 0 and c >= 2:
                    act.wait_ge(sem["y_split"], at("y_split", 4 * (c - 2) + 3))
                act.activation(U[:, c % 2, j, :], ps[bank + j][:], ACT.Gelu_apprx_tanh).then_inc(sem["u_read"], step("u_read", (c, j)))
            prepare(ids["u", c][-1] + 2)

        def g_part(c):
            for j in range(4):
                after(("g", c), j)
                if c == 0:
                    act.wait_ge(sem["spatial_read"], at("spatial_read", 15))
                if c >= 1:
                    act.wait_ge(sem["y_multiplied"], at("y_multiplied", 4 * (c - 1) + j))
                act.activation(GT[:, j, :], ps[j][:], ACT.Silu).then_inc(sem["g_read"], step("g_read", (c, j)))
            for j in range(4):
                h = 4 * c + j
                act.wait_ge(sem["y_multiplied"], at("y_multiplied", h))
                act.activation(YH[:, h, :], U[:, c % 2, j, :], ACT.Copy).then_inc(sem["y_high_ready"], step("y_high_ready", h))
            prepare(ids["g", c][-1] + 2)

        u_part(0, 0)
        u_part(1, 4)
        g_part(0)
        g_part(1)
        u_part(2, 4)
        g_part(2)
        u_part(3, 4)
        g_part(3)
        rows("s1", "a_out")

        act.wait_ge(sem["xt_ready"], at("xt_ready", ("s1", TT - 1)))
        act.wait_ge(sem["rows_done"], at("rows_done", ("s1", TT - 1)))
        for src, dst, a in ((XTH, XWH, SEQ - 64), (XTH, XWH, 0), (XTL, XWL, SEQ - 64), (XTL, XWL, 0)):
            b = 0 if a else 64
            ins = act.activation(dst[:, :, b:b + 64], src[:, :, a:a + 64].bitcast(F32), ACT.Copy)
        ins.then_inc(sem["wrap_ready"], step("wrap_ready"))
        for g in range(3):
            for hf in range(2):
                for j in range(4):
                    after(("b", g, hf, "q"), j)
                    act.activation(bQT[:, j, :], ps[j][:], ACT.Copy).then_inc(sem["bq_read"], step("bq_read", (g, hf, j)))
                prepare(ids["b", g, hf, "q"][-1] + 2)
                for j in range(4):
                    after(("b", g, hf, "k"), j)
                    act.activation(bKT[:, j, :], ps[4 + j][:], ACT.Copy).then_inc(sem["bk_read"], step("bk_read", (g, hf, j)))
                prepare(ids["b", g, hf, "k"][-1] + 2)
                for t in range(4):
                    after(("b", g, hf, "v"), t)
                    act.activation(bV[:, t, :], ps[t][:], ACT.Copy).then_inc(sem["bv_read"], step("bv_read", (g, hf, t)))
                attend(("b", g, hf))
        act.wait_ge(sem["group_diffs"], at("group_diffs"))
        act.activation(bE[:], bE[:], ACT.Exp).then_inc(sem["group_exps"], step("group_exps"))
        for c in range(2):
            for t in range(TT):
                after(("b_gate", c), t)
                ins = act.activation(bG[:, t, 512 * c:512 * c + 512], ps[4 * c + t][:], ACT.Silu)
            ins.then_inc(sem["bgate_read"], step("bgate_read", c))
            prepare(ids["b_gate", c][-1] + 2)
        turned_mix("b")
        rows("s2", "b_out")

        def ffn(l, i):
            f = (l, i)
            for c in range(6):
                gname = ("gate", l, i, c) if c < 5 else ("last", l, i)
                ng = 4 if c < 5 else 2
                for j in range(ng):
                    after(gname, j)
                    if c:
                        act.wait_ge(sem["hidden_split"], at("hidden_split", (f, c - 1)))
                    act.activation(G[:, j, :], ps[j][:], ACT.Silu).then_inc(sem["gate_read"], step("gate_read", (f, c, j)))
                prepare(ids[gname][-1] + 2)
                if c < 5:
                    prepare(ids["up", l, i, c][-1] + 1)
                for j in range(ng):
                    act.wait_ge(sem["up_read"], at("up_read", (f, c, j)))
                    ins = act.activation(HTH[:, 4 * c + j, :], G[:, j, :], ACT.Copy)
                ins.then_inc(sem["hidden_high"], step("hidden_high", (f, c)))
                if c < 5:
                    prepare(ids["up", l, i, c][-1] + 2)

        ffn(0, 0)
        rows("l00", ("down", 0, 0))

        for t in range(TT):
            after("mla_in", t)
            act.activation(ZR[:, t, :], ps[t][:, 0:416], ACT.Copy).then_inc(sem["c_rows"], step("c_rows", t))
            act.wait_ge(sem["c_rows"], at("c_rows", t))
            act.activation(mPT[1][:, 0:128], ZR[:, t, 256:384], ACT.Square, accum_out=SS[:, 4 + t:5 + t])
            act.activation(mPT[0][:, 0:256], ZR[:, t, 0:256], ACT.Square,
                                  accum_out=SS[:, t:t + 1]).then_inc(sem["c_read"], step("c_read", t))
        prepare(ids["mla_in"][-1] + 2)
        for j in range(2):
            after("mla_mem", j)
            act.activation(mQM[:, j, :], ps[4 + j][:], ACT.Copy).then_inc(sem["qmem_read"], step("qmem_read", j))
        prepare(ids["mla_mem"][-1] + 2)
        act.wait_ge(sem["c_turned"], at("c_turned"))
        for j in range(3):
            act.activation(CTH[:, j, :], ps[j][:], ACT.Copy).then_inc(sem["c_high"], step("c_high", j))
        qv = mF[:].rearrange("p t h d -> p t (h d)")
        for t in range(TT):
            for n in range(2):
                after("uq", 2 * t + n)
                act.activation(qv[:, t, 512 * n:512 * n + 512], ps[2 * t + n][:], ACT.Copy).then_inc(sem["uq_read"], step("uq_read", (t, n)))
        prepare(ids["uq"][-1] + 2)
        for t in range(TT):
            after("uq_tail", t)
            act.activation(qv[:, t, 1024:1152], ps[2 * t][:, 0:128], ACT.Copy).then_inc(sem["uq_tail_read"], step("uq_tail_read", t))
        prepare(ids["uq_tail"][-1] + 2)
        for h in range(HEADS):
            act.wait_ge(sem["head_turned"], at("head_turned", ("q", h)))
            act.activation(qT[0:96, h, :], ps[h % 8][0:96, :], ACT.Copy).then_inc(sem["heads_turned"], step("heads_turned", ("q", h)))
        for t in range(TT):
            for n in range(3):
                j = 3 * t + n
                after("ukv", j)
                act.activation(mF[:, t, 4 * n:4 * n + 4, 0:64],
                                      ps[j % 8][:].rearrange("p (h d) -> p h d", h=4)[:, :, 0:64], ACT.Copy).then_inc(sem["ukv_read_k"], step("ukv_read_k", j))
        prepare(ids["ukv"][-1] + 2)
        for h in range(HEADS):
            act.wait_ge(sem["head_turned"], at("head_turned", ("k", h)))
            act.activation(kT[0:96, h, :], ps[h % 8][0:96, :], ACT.Copy).then_inc(sem["heads_turned"], step("heads_turned", ("k", h)))
        attend_pairs("mla")
        rows("l01", ("w_out", 0))
        ffn(0, 1)
        rows("l02", ("down", 0, 1))

        after("kv_a", 0)
        for j in range(3):
            act.activation(KVF[:, j, :], ps[j][:], ACT.Copy).then_inc(sem["kvf_read"], step("kvf_read", j))
        ins = act.activation(VV[:, :, 0, :], ps[3][:].rearrange("p (t n) -> p t n", t=TT), ACT.Copy)
        ins.then_inc(sem["kvf_read"], step("kvf_read", 3))
        prepare(ids["kv_a"][-1] + 2)
        after("kv_b", 0)
        act.activation(KVF[:, 3, :], ps[4][:], ACT.Copy)
        act.activation(VV[:, :, 1, :], ps[5][:].rearrange("p (t n) -> p t n", t=TT), ACT.Copy).then_inc(sem["kv_copied"], step("kv_copied"))
        prepare(ids["kv_b"][-1] + 2)
        act.wait_ge(sem["cmp_hidden_done"], at("cmp_hidden_done"))
        act.wait_ge(sem["h1_zeroed"], at("h1_zeroed"))
        for j in range(2):
            for g in range(2):
                for ht in range(2):
                    n = 2 * j + ht
                    src = ps[6][:, n * 64 + g * N_CMP:n * 64 + (g + 1) * N_CMP].rearrange("p (r n) -> p r n", r=1).to_broadcast([P, 4, N_CMP])
                    ins = act.activation(H1[:, j, g, ht, :, 0:N_CMP], src, ACT.Gelu_apprx_tanh, bias=B1[:, j, ht:ht + 1])
        ins.then_inc(sem["cmp_hidden_ready"], step("cmp_hidden_ready"))
        prepare(ids["gate", 1, 0, 0][-1] + 1)
        act.wait_ge(sem["cmp_done"], at("cmp_done"))
        act.activation(KCT[:], ps[4][:, 0:NC], ACT.Copy)
        act.activation(VC4[:], ps[5][:, 0:128].rearrange("p (g d) -> p g d", g=2), ACT.Copy).then_inc(sem["cmp_kept"], step("cmp_kept"))
        act.wait_ge(sem["kv_kept"], at("kv_kept"))
        ffn(1, 0)
        rows("l10", ("down", 1, 0))

        for j in range(4):
            after("nsa_a", j)
            act.activation(nQT[:, j, :], ps[j][:], ACT.Copy).then_inc(sem["nq_read"], step("nq_read", ("a", j)))
        prepare(ids["nsa_a"][-1] + 2)
        for j in range(4):
            after("nsa_b", j)
            dst = nQT[:, 4 + j, :] if j < 2 else nQM[:, j - 2, :]
            act.activation(dst, ps[4 + j][:], ACT.Copy).then_inc(sem["nq_read"], step("nq_read", ("b", j)))
        prepare(ids["nsa_b"][-1] + 2)
        after("nsa_gates", 0)
        act.activation(nGT[0:36, :], ps[4][0:36, :], ACT.Sigmoid).then_inc(sem["gates_t_read"], step("gates_t_read"))
        act.wait_ge(sem["gates_turned"], at("gates_turned"))
        act.activation(nG[:].rearrange("p t h b -> p (t h b)"), ps[5][:, 0:144], ACT.Copy).then_inc(sem["ngates_read"], step("ngates_read"))
        for n in range(TT + 1):
            if n < TT:
                act.wait_ge(sem["cmp_shifted"], at("cmp_shifted", n))
                act.activation(nCPs[n % 2][:], nCPs[n % 2][:], ACT.Exp).then_inc(sem["cmp_exp"], step("cmp_exp", n))
            t = n - 1
            if t < 0:
                continue
            act.wait_ge(sem["cmp_p_turned"], at("cmp_p_turned", t))
            if t >= 2:
                act.wait_ge(sem["cmp_weighted"], at("cmp_weighted", t - 2))
            act.activation(nCTs[t % 2][:], ps[6 + t % 2][:, 0:384].rearrange("p (u n) -> p u n", u=3), ACT.Copy).then_inc(sem["cmp_pt_copied"], step("cmp_pt_copied", t))
        prepare(ids["nsa_gates"][-1] + 2)
        attend_pairs("nsa")
        rows("l11", ("w_out", 1))
        ffn(1, 1)
        prepare(len(panels) - 1)

    @block.vector
    def _(dve):
        done = [0]
        chain = [0]

        def prepare(g):
            while done[0] <= min(g, len(panels) - 1):
                n = done[0]
                w = widths[n]
                dve.wait_ge(sem["w_high_ready"], at("w_high_ready", n))
                dve.tensor_tensor(WL[n % 2][:, 0:w], RAW[n % 2][:, 0:w], WH[n % 2][:, 0:w].bitcast(F32),
                                         ALU.subtract).then_inc(sem["w_low_ready"], step("w_low_ready", n))
                done[0] += 1

        def link(ins):
            chain[0] += 1
            ins.then_inc(sem["dve_step"], 1)
            dve.wait_ge(sem["dve_step"], chain[0])

        def after(name, j):
            if j == 0:
                prepare(ids[name][-1] + 1)
            dve.wait_ge(sem["product_done"], at("product_done", ("acc", name, j)))

        def low_turned(s, t, hh, hl, signal, perm=False):
            dve.wait_ge(sem["turned_high"], at("turned_high", (s, t)))
            for b in range(2):
                cols = slice(t, SEQ, 4) if perm else slice(t * P, (t + 1) * P)
                ins = dve.tensor_tensor(hl[:, 4 * b:4 * b + 4, cols], ps[2 * t + b][:].rearrange("p (k n) -> p k n", k=4),
                                        hh[:, 4 * b:4 * b + 4, cols].bitcast(F32), ALU.subtract)
            ins.then_inc(sem[signal], step(signal, (s, t)))

        def rows(s, y=None):
            kind, coef = ROWS[s]
            if y:
                prepare(ids[y][-1])
            for t in range(TT + 1):
                if t < TT:
                    r = R[t % 2]
                    if t == 0:
                        dve.wait_ge(sem["gains_loaded"], at("gains_loaded", s))
                    if kind == "ln":
                        dve.wait_ge(sem["product_done"], at("product_done", ("acc", y, t)))
                        for half in range(2):
                            c = slice(512 * half, 512 * half + 512)
                            link(dve.scalar_tensor_tensor(out=r[:, c], in0=ps[2 * t + half][:], scalar=coef,
                                                          in1=X[:, t, c], op0=ALU.mult, op1=ALU.add))
                            link(dve.bn_stats(BN[:, 6 * half:6 * half + 6], r[:, c]))
                        dve.bn_aggr(SS[:, 4 * t:4 * t + 2], BN[:, 0:12]).then_inc(sem["variance"], step("variance", (s, t)))
                    if kind in ("post", "post_pre"):
                        dve.wait_ge(sem["rstd"], at("rstd", (s, t)))
                        dve.wait_ge(sem["squared"], at("squared", (s, t)))
                        for half in range(2):
                            c = slice(512 * half, 512 * half + 512)
                            link(dve.scalar_tensor_tensor(out=r[:, c], in0=ps[2 * t + half][:], scalar=RS[:, 4 * t:4 * t + 1],
                                                          in1=GB[0][:, c], op0=ALU.mult, op1=ALU.mult))
                        ins = dve.tensor_tensor(X[:, t, :], X[:, t, :], r[:], ALU.add)
                        if kind == "post":
                            ins.then_inc(sem["rows_done"], step("rows_done", (s, t)))
                        else:
                            ins.then_inc(sem["x_added"], step("x_added", (s, t)))
                if t < TT:
                    if kind == "ln":
                        dve.wait_ge(sem["variance"], at("variance", (s, t)))
                        link(dve.scalar_tensor_tensor(out=r[:], in0=r[:], scalar=SS[:, 4 * t:4 * t + 1], in1=GB[0][:],
                                                      op0=ALU.subtract, op1=ALU.mult))
                        dve.wait_ge(sem["rstd"], at("rstd", (s, t)))
                        dve.scalar_tensor_tensor(out=X[:, t, :], in0=r[:], scalar=RS[:, 4 * t:4 * t + 1], in1=GB[1][:],
                                                        op0=ALU.mult, op1=ALU.add).then_inc(sem["rows_done"], step("rows_done", (s, t)))
                    if kind in ("pre", "post_pre"):
                        dve.wait_ge(sem["rstd_x"], at("rstd_x", (s, t)))
                        dve.wait_ge(sem["squared_x"], at("squared_x", (s, t)))
                        dve.scalar_tensor_tensor(out=r[:], in0=X[:, t, :], scalar=RS[:, 4 * t + 2:4 * t + 3],
                                                        in1=GB[0 if kind == "pre" else 1][:], op0=ALU.mult, op1=ALU.mult).then_inc(sem["rows_done"], step("rows_done", (s, t)))
                if y and t == TT - 1:
                    prepare(ids[y][-1] + 1)
                if t >= 1 and s != "l12":
                    low_turned(s, t - 1, XTH, XTL, "xt_ready")

        def attend(name):
            tasks, SBs, PTs = ATT[name]
            N = len(tasks)
            for n in range(N + 4):
                if n < N:
                    tk = tasks[n]
                    m_ap, nh, b = tk["width"]
                    if n >= 4:
                        dve.wait_ge(sem["p_turned"], at("p_turned", (name, n - 4)))
                    if name[1] == 0 and (n < 4 or n >= 12):
                        if n < 4 and name[2] == 1:
                            dve.wait_ge(sem["p_turned"], at("p_turned", (("b", 0, 0), 12 + n)))
                        c = 0 if n < 4 else 192
                        dve.memset(SBs[n % 4][:].rearrange("p (e c) -> p e c", e=2)[:, :, c:c + 64], 0.0)
                    dve.wait_ge(sem["scored"], at("scored", (name, n)))
                    sv = tk["view"]
                    dve.scalar_tensor_tensor(out=sv(SBs[n % 4][:]), in0=sv(ps[n % 4][:]), scalar=tk["scale"],
                                             in1=tk["bias"], op0=ALU.mult, op1=ALU.add).then_inc(sem["masked"], step("masked", (name, n)))
                    dve.wait_ge(sem["masked"], at("masked", (name, n)))
                    dve.tensor_reduce(m_ap, sv(SBs[n % 4][:]), AX.X, ALU.max, negate=True).then_inc(sem["maxed"], step("maxed", (name, n)))
                if n == 5:
                    prepare(ids[name + ("v",)][-1] + 2)
                if n >= 4:
                    m = n - 4
                    kind, dst, arg = tasks[m]["finish"]
                    if m == 0 and name == ("b", 1, 0):
                        dve.wait_ge(sem["o0_permuted"], at("o0_permuted"))
                    dve.wait_ge(sem["weighted"], at("weighted", (name, m)))
                    dve.tensor_copy(dst, ps[6 + m % 2][:, 0:arg].rearrange("p (h d) -> p h d", d=64)).then_inc(sem["o_read"], step("o_read", (name, m)))

        def attend_pairs(name):
            tasks, SBs, PTs = ATT[name]
            N = len(tasks)
            HH, HL = MIX[name]
            for n in range(N + 7):
                if n < N:
                    tk = tasks[n]
                    m_ap = tk["width"][0]
                    sb, sc = tk["view"](SBs[n % 6]), tk["view"](ps[n % 4])
                    if name == "nsa" and n < 96 and n % 8 == 0:
                        h = n // 8
                        if h >= 2:
                            dve.wait_ge(sem["masked"], at("masked", (name, 8 * (h - 1) - 1)))
                        link(dve.scalar_tensor_tensor(out=nAB[h % 2][:], in0=nDI[:], scalar=-slopes[h], in1=nCM[:],
                                                      op0=ALU.mult, op1=ALU.add))
                    if n >= 6:
                        dve.wait_ge(sem["p_turned"], at("p_turned", (name, n - 6)))
                    dve.wait_ge(sem["scored"], at("scored", (name, n)))
                    if tk["bias"] is not None:
                        dve.scalar_tensor_tensor(out=sb, in0=sc, scalar=tk["scale"], in1=tk["bias"],
                                                 op0=ALU.mult, op1=ALU.add).then_inc(sem["masked"], step("masked", (name, n)))
                    else:
                        dve.tensor_scalar(sb, sc, tk["scale"], None, ALU.mult).then_inc(sem["masked"], step("masked", (name, n)))
                    dve.wait_ge(sem["masked"], at("masked", (name, n)))
                    dve.tensor_reduce(m_ap, sb, AX.X, ALU.max, negate=True).then_inc(sem["maxed"], step("maxed", (name, n)))
                if 2 <= n < N + 2:
                    m = n - 2
                    tk = tasks[m]
                    rd = RD[:, m % 8:m % 8 + 1]
                    dve.wait_ge(sem["exp_done"], at("exp_done", (name, m)))
                    sb = tk["view"](SBs[m % 6])
                    link(dve.reciprocal(rd, DS[:, m % 8:m % 8 + 1]))
                    if tk["finish"] is not None:
                        dve.tensor_scalar(sb, sb, rd, tk["finish"], ALU.mult, ALU.mult).then_inc(sem["p_scaled"], step("p_scaled", (name, m)))
                    else:
                        dve.tensor_scalar(sb, sb, rd, None, ALU.mult).then_inc(sem["p_scaled"], step("p_scaled", (name, m)))
                if 6 <= n < N + 6 and tasks[n - 6]["closes"] and name == "nsa" and tasks[n - 6]["pair"] < 6:
                    j = tasks[n - 6]["pair"]
                    dve.wait_ge(sem["weighted"], at("weighted", (name, n - 6)))
                    dve.tensor_tensor(nOC[:, j, :], ps[tasks[n - 6]["bank"]][:], nOC[:, j, :],
                                      ALU.add).then_inc(sem["pair_summed"], step("pair_summed", j))
                if n >= 7 and tasks[n - 7]["closes"]:
                    j = tasks[n - 7]["pair"]
                    src = nOC[:, j, :] if name == "nsa" and j < 6 else ps[tasks[n - 7]["bank"]][:]
                    dve.wait_ge(sem["pair_high"], at("pair_high", (name, j)))
                    dve.tensor_tensor(HL[:, j, :], src, HH[:, j, :].bitcast(F32),
                                      ALU.subtract).then_inc(sem["pair_split"], step("pair_split", (name, j)))

        def low_mix(name):
            _, hh, hl, perm = mixes[name]
            for t in range(TT):
                low_turned(name, t, hh, hl, "mix_split", perm)

        dve.memset(HALF, -0.5).then_inc(sem["half_ready"], step("half_ready"))
        dve.memset(RB[32:33, :], 1.0).then_inc(sem["table_ones"], step("table_ones"))
        dve.wait_ge(sem["bias_multiplied"], at("bias_multiplied"))
        dve.tensor_copy(BROW[0:16, 0:384], ps[0][0:16, 0:384])
        dve.tensor_copy(BROW[0:16, 384:896], ps[1][0:16, :]).then_inc(sem["bias_copied"], step("bias_copied"))
        for b in range(4):
            dve.wait_ge(sem["mem_high"], at("mem_high", b))
            dve.tensor_tensor(MTL[:, 2 * b:2 * b + 2, :], ps[2 + b][:].rearrange("p (k n) -> p k n", k=2),
                                     MTH[:, 2 * b:2 * b + 2, :].bitcast(F32), ALU.subtract).then_inc(sem["mem_split"], step("mem_split", b))
        prepare(ids["mem", 1][-1] + 1)
        for b in range(4):
            dve.wait_ge(sem["ws_turned"], at("ws_turned", b))
            dve.tensor_copy(WST[:, 4 * b:4 * b + 4, :], ps[b][:].rearrange("p (h n) -> p h n", h=4)).then_inc(sem["ws_copied"], step("ws_copied", b))
        prepare(ids["mem", 1][-1] + 2)
        rows("s0")

        for c in range(4):
            prepare(ids["v", c][-1] + 1)
            for t in range(TT):
                dve.wait_ge(sem["v_read"], at("v_read", (c, t)))
                link(dve.bn_stats(BN[:, 24 * t + 6 * c:24 * t + 6 * c + 6], V[:, t, 512 * c:512 * c + 512]))
            prepare(ids["v", c][-1] + 2)
        for t in range(TT):
            ins = dve.bn_aggr(SS[:, 4 * t:4 * t + 2], BN[:, 24 * t:24 * t + 24])
        ins.then_inc(sem["variance"], step("variance", "v"))
        prepare(ids["u", 0][-1] + 1)
        for hh in range(2):
            dve.wait_ge(sem["gains_loaded"], at("gains_loaded", ("v", hh)))
            if hh == 0:
                dve.wait_ge(sem["variance"], at("variance", "v"))
                dve.wait_ge(sem["rstd"], at("rstd", "v"))
            if hh == 1:
                prepare(ids["u", 0][-1] + 2)
            for t in range(TT):
                v = V[:, t, 1024 * hh:1024 * hh + 1024]
                link(dve.scalar_tensor_tensor(out=v, in0=v, scalar=SS[:, 4 * t:4 * t + 1], in1=GB[0][:],
                                              op0=ALU.subtract, op1=ALU.mult))
                ins = dve.scalar_tensor_tensor(out=v, in0=v, scalar=RS[:, t:t + 1], in1=GB[1][:],
                                               op0=ALU.mult, op1=ALU.add)
            ins.then_inc(sem["v_normed"], step("v_normed", hh))
        prepare(ids["u", 1][-1] + 2)
        dve.wait_ge(sem["b_s_loaded"], at("b_s_loaded"))
        dve.wait_ge(sem["mem_kv_stored"], at("mem_kv_stored"))
        for h in range(A_HEADS):
            dve.wait_ge(sem["spatial_done"], at("spatial_done", h))
            bias = BS[:, h * P:h * P + P].rearrange("p (c n) -> p c n", c=1).to_broadcast([P, TT, P])
            dve.tensor_tensor(SG[:, h, :].rearrange("p (c n) -> p c n", c=TT),
                                     ps[h % 8][:].rearrange("p (c n) -> p c n", c=TT), bias, ALU.add).then_inc(sem["spatial_read"], step("spatial_read", h))

        def y_part(c):
            prepare(ids["g", c][-1] + 1)
            for j in range(4):
                h = 4 * c + j
                u = U[:, c % 2, j, :]
                dve.wait_ge(sem["spatial_read"], at("spatial_read", h))
                dve.wait_ge(sem["u_read"], at("u_read", (c, j)))
                link(dve.tensor_tensor(u, u, SG[:, h, :], ALU.mult))
                dve.wait_ge(sem["g_read"], at("g_read", (c, j)))
                dve.tensor_tensor(u, u, GT[:, j, :], ALU.mult).then_inc(sem["y_multiplied"], step("y_multiplied", h))
            for j in range(4):
                h = 4 * c + j
                dve.wait_ge(sem["y_high_ready"], at("y_high_ready", h))
                dve.tensor_tensor(YL[:, h, :], U[:, c % 2, j, :], YH[:, h, :].bitcast(F32), ALU.subtract).then_inc(sem["y_split"], step("y_split", h))
            prepare(ids["g", c][-1] + 2)

        y_part(0)
        y_part(1)
        prepare(ids["u", 2][-1] + 2)
        y_part(2)
        prepare(ids["u", 3][-1] + 2)
        y_part(3)
        rows("s1", "a_out")

        for g in range(3):
            for hf in range(2):
                prepare(ids["b", g, hf, "v"][-1] + 1)
                dve.wait_ge(sem["bias_loaded"], at("bias_loaded", (g, hf)))
                attend(("b", g, hf))
        link(dve.tensor_tensor(bS[:], bM[:, 0], bM[:, 1], ALU.min))
        link(dve.tensor_tensor(bS[:], bS[:], bM[:, 2], ALU.min))
        for g in range(3):
            ins = dve.tensor_tensor(bE[:, g], bS[:], bM[:, g], ALU.subtract)
        ins.then_inc(sem["group_diffs"], step("group_diffs"))
        dve.wait_ge(sem["group_exps"], at("group_exps"))
        link(dve.tensor_tensor(bD[:], bD[:], bE[:], ALU.mult))
        link(dve.tensor_tensor(bS[:], bD[:, 0], bD[:, 1], ALU.add))
        link(dve.tensor_tensor(bS[:], bS[:], bD[:, 2], ALU.add))
        link(dve.reciprocal(bS[:], bS[:]))
        for g in range(3):
            ins = dve.tensor_tensor(bE[:, g], bE[:, g], bS[:], ALU.mult)
        ins.then_inc(sem["group_weights"], step("group_weights"))
        dve.wait_ge(sem["group_weights"], at("group_weights"))
        prepare(ids["b_gate", 0][-1] + 1)

        def weighted(g, t):
            o = bO[g][:, t, :].rearrange("p (h d) -> p h d", d=64)
            w = bE[:, g, t, :].rearrange("p (h d) -> p h d", d=1).to_broadcast([P, 16, 64])
            return o, w
        for t in range(TT):
            if t == 1:
                prepare(ids["b_gate", 0][-1] + 2)
            if t == 2:
                prepare(ids["b_gate", 1][-1] + 1)
            for g in (0, 2):
                o, w = weighted(g, t)
                link(dve.tensor_tensor(o, o, w, ALU.mult))
            link(dve.tensor_tensor(bO[0][:, t, :], bO[0][:, t, :], bO[2][:, t, :], ALU.add))
            dve.wait_ge(sem["o1_weighted"], at("o1_weighted", t))
            link(dve.tensor_tensor(bO[0][:, t, :], bO[0][:, t, :], bO[1][:, t, :], ALU.add))
        dve.wait_ge(sem["bgate_read"], at("bgate_read", 1))
        prepare(ids["b_gate", 1][-1] + 2)
        for t in range(TT):
            ins = dve.tensor_tensor(bO[0][:, t, :], bO[0][:, t, :], bG[:, t, :], ALU.mult)
            ins.then_inc(sem["mix_ready"], step("mix_ready", ("b", t)))
        low_mix("b")
        rows("s2", "b_out")

        def ffn(l, i):
            f = (l, i)
            for c in range(6):
                if c < 5:
                    prepare(ids["gate", l, i, c][-1] + 2)
                    uname, ng, bank = ("up", l, i, c), 4, 4
                else:
                    uname, ng, bank = ("last", l, i), 2, 2
                for j in range(ng):
                    if j == 0:
                        prepare(ids[uname][-1] + 1)
                    dve.wait_ge(sem["product_done"], at("product_done", ("acc", uname, j if c < 5 else j + 2)))
                    dve.wait_ge(sem["gate_read"], at("gate_read", (f, c, j)))
                    dve.tensor_tensor(G[:, j, :], ps[bank + j][:], G[:, j, :], ALU.mult).then_inc(sem["up_read"], step("up_read", (f, c, j)))
                dve.wait_ge(sem["hidden_high"], at("hidden_high", (f, c)))
                a = 4 * c
                dve.tensor_tensor(HTL[:, a:a + ng, :], G[:, 0:ng, :], HTH[:, a:a + ng, :].bitcast(F32),
                                         ALU.subtract).then_inc(sem["hidden_split"], step("hidden_split", (f, c)))
                prepare(ids[uname][-1] + 2)

        ffn(0, 0)
        rows("l00", ("down", 0, 0))

        prepare(ids["mla_in"][-1] + 1)
        dve.wait_ge(sem["gains_loaded"], at("gains_loaded", "mla"))
        dve.wait_ge(sem["rstd"], at("rstd", "mla"))
        for t in range(TT):
            dve.wait_ge(sem["c_read"], at("c_read", t))
            dve.scalar_tensor_tensor(out=ZR[:, t, 0:256], in0=ZR[:, t, 0:256], scalar=RS[:, t:t + 1], in1=GB[0][:, 0:256],
                                     op0=ALU.mult, op1=ALU.mult)
            dve.scalar_tensor_tensor(out=ZR[:, t, 256:384], in0=ZR[:, t, 256:384], scalar=RS[:, 4 + t:5 + t],
                                            in1=GB[0][:, 256:384], op0=ALU.mult, op1=ALU.mult).then_inc(sem["c_normed"], step("c_normed", t))
        prepare(ids["mla_mem"][-1] + 1)
        for j in range(3):
            dve.wait_ge(sem["c_high"], at("c_high", j))
            dve.tensor_tensor(CTL[:, j, :], ps[j][:], CTH[:, j, :].bitcast(F32), ALU.subtract).then_inc(sem["c_split"], step("c_split", j))
        prepare(ids["mla_mem"][-1] + 2)
        dve.wait_ge(sem["rope_loaded"], at("rope_loaded"))

        def rope(x1, x2, o1, o2, c, s, shape, tmp):
            for i, (a, b) in enumerate(((x1, c), (x2, s), (x2, c), (x1, s))):
                ins = dve.tensor_tensor(tmp[i], a, b, ALU.mult)
            link(ins)
            dve.tensor_tensor(o1, tmp[0], tmp[1], ALU.subtract)
            return dve.tensor_tensor(o2, tmp[2], tmp[3], ALU.add)

        tmp = [RT[:, i, 0:64].rearrange("p (t d) -> p t d", t=TT) for i in range(4)]
        link(rope(ZR[:, :, 384:400], ZR[:, :, 400:416], KR[:, :, 0:16], KR[:, :, 16:32], COS[:], SIN[:], None, tmp))
        prepare(ids["uq"][-1] + 2)
        tmp = [RT[:, i, :].rearrange("p (h d) -> p h d", h=HEADS) for i in range(4)]
        dve.wait_ge(sem["uq_read"], at("uq_read", (3, 1)))
        for t in range(TT):
            dve.wait_ge(sem["uq_tail_read"], at("uq_tail_read", t))
            x1, x2 = mF[:, t, :, 64:80], mF[:, t, :, 80:96]
            cb, sn = (z[:, t, :].rearrange("p (h d) -> p h d", h=1).to_broadcast([P, HEADS, 16]) for z in (COS, SIN))
            ins = rope(x1, x2, x1, x2, cb, sn, None, tmp)
            if t < TT - 1:
                link(ins)
        ins.then_inc(sem["roped"], step("roped", "q"))
        prepare(ids["uq_tail"][-1] + 2)
        for t in range(TT):
            for n in range(3):
                j = 3 * t + n
                after("ukv", j)
                dve.wait_ge(sem["ukv_read_k"], at("ukv_read_k", j))
                dve.tensor_copy(mV[:, t, 256 * n:256 * n + 256].rearrange("p (h d) -> p h d", h=4),
                                       ps[j % 8][:].rearrange("p (h d) -> p h d", h=4)[:, :, 64:128]).then_inc(sem["ukv_read_v"], step("ukv_read_v", j))
            ins = dve.tensor_copy(mF[:, t, :, 64:96],
                                  KR[:, t, :].rearrange("p (h d) -> p h d", h=1).to_broadcast([P, HEADS, 32]))
        ins.then_inc(sem["roped"], step("roped", "k"))
        prepare(ids["ukv"][-1] + 2)
        dve.wait_ge(sem["mix_const0"], at("mix_const0"))
        attend_pairs("mla")
        rows("l01", ("w_out", 0))
        ffn(0, 1)
        rows("l02", ("down", 0, 1))

        prepare(ids["kv_a"][-1] + 1)
        dve.wait_ge(sem["pos_loaded"], at("pos_loaded"))
        dve.memset(H1[:].rearrange("p a b c r n -> p (a b c r n)"), 0.0).then_inc(sem["h1_zeroed"], step("h1_zeroed"))
        for j in range(2):
            dve.wait_ge(sem["kvf_read"], at("kvf_read", j))
            for g in range(2):
                for odd in range(2):
                    src = bass.AP(KVF, 64 * g * 4 * SEQ + j * SEQ + odd, [[4 * SEQ, 64], [2, LT], [CMP_STRIDE, N_CMP]])
                    pos = POS[64 * g:64 * g + 64, j, odd:CMP_LEN:2].rearrange("p (l n) -> p l n", n=1).to_broadcast([64, LT, N_CMP])
                    ins = dve.tensor_tensor(FZ[64 * odd:64 * odd + 64, j, :, g, :], src, pos, ALU.add)
        ins.then_inc(sem["blocks_ready"], step("blocks_ready"))
        prepare(ids["kv_a"][-1] + 2)
        prepare(ids["kv_b"][-1] + 2)
        prepare(ids["gate", 1, 0, 0][-1] + 1)
        dve.wait_ge(sem["kv_kept"], at("kv_kept"))
        ffn(1, 0)
        rows("l10", ("down", 1, 0))

        prepare(ids["nsa_a"][-1] + 1)
        dve.wait_ge(sem["nsa_const"], at("nsa_const"))
        dve.memset(KBD[:].rearrange("p g n -> p (g n)"), 0.0)
        link(dve.memset(VBD[:].rearrange("p g q n -> p (g q n)"), 0.0))
        for g in range(2):
            dve.tensor_copy(KBD[64 * g:64 * g + 64, g, :], KCT[64 * g:64 * g + 64, :])
        for e in range(4):
            q = slice(32 * e, 32 * e + 32)
            ins = dve.tensor_copy(VBD[q, :, e // 2, 64 * (e % 2):64 * (e % 2) + 64], VC4[q, :, :])
        ins.then_inc(sem["cmp_v_spread"], step("cmp_v_spread"))
        for h in range(HEADS):
            ins = dve.scalar_tensor_tensor(out=nBC[:, :, h, :], in0=nCD[:], scalar=-slopes[h], in1=nCN[:],
                                           op0=ALU.mult, op1=ALU.add)
        link(ins)
        prepare(ids["nsa_gates"][-1] + 1)
        dve.wait_ge(sem["product_done"], at("product_done", ("acc", "nsa_gates", 0)))

        def over_keys(v):
            return v.rearrange("p (h n) -> p h n", n=1).to_broadcast([P, HEADS, NC])
        def shift(t):
            dve.wait_ge(sem["cmp_scored"], at("cmp_scored", t))
            nCP = nCPs[t % 2]
            if t >= 2:
                dve.wait_ge(sem["cmp_p_turned"], at("cmp_p_turned", t - 2))
            for g in range(2):
                ins = dve.scalar_tensor_tensor(out=nCP[:, 6 * g:6 * g + 6, :],
                                               in0=ps[t][:, 0:384].rearrange("p (i g n) -> p i g n", i=6, g=2)[:, :, g, :],
                                               scalar=HD_SCALE, in1=nBC[:, t, 6 * g:6 * g + 6, :], op0=ALU.mult, op1=ALU.add)
            link(ins)
            link(dve.tensor_reduce(CM_[:, 0:HEADS], nCP[:], AX.X, ALU.max))
            dve.tensor_tensor(nCP[:], nCP[:], over_keys(CM_[:, 0:HEADS]), ALU.subtract).then_inc(sem["cmp_shifted"], step("cmp_shifted", t))

        def keep(t):
            dve.wait_ge(sem["cmp_weighted"], at("cmp_weighted", t))
            cols = slice(t * P, t * P + P)
            dve.tensor_copy(nOC[:, 0:4, cols], ps[4][:].rearrange("p (j n) -> p j n", j=4))
            dve.tensor_copy(nOC[:, 4:6, cols], ps[5][:, 0:256].rearrange("p (j n) -> p j n", j=2)).then_inc(sem["cmp_o_read"], step("cmp_o_read", t))

        shift(0)
        for t in range(TT):
            nCP = nCPs[t % 2]
            dve.wait_ge(sem["cmp_exp"], at("cmp_exp", t))
            mask = nC1[:, t, :].rearrange("p (h n) -> p h n", h=1).to_broadcast([P, HEADS, NC])
            link(dve.tensor_tensor(nCP[:], nCP[:], mask, ALU.mult))
            link(dve.tensor_reduce(CD_[:, 0:HEADS], nCP[:], AX.X, ALU.add))
            link(dve.tensor_scalar(CD_[:, 0:HEADS], CD_[:, 0:HEADS], 1e-30, None, ALU.max))
            link(dve.reciprocal(CF_[:, 0:HEADS], CD_[:, 0:HEADS]))
            dve.wait_ge(sem["ngates_read"], at("ngates_read"))
            link(dve.tensor_tensor(CF_[:, 0:HEADS], CF_[:, 0:HEADS], nG[:, t, :, 0], ALU.mult))
            dve.tensor_tensor(nCP[:], nCP[:], over_keys(CF_[:, 0:HEADS]), ALU.mult).then_inc(sem["cmp_p_ready"], step("cmp_p_ready", t))
            if t + 1 < TT:
                shift(t + 1)
            if t >= 1:
                keep(t - 1)
        keep(TT - 1)
        prepare(ids["nsa_gates"][-1] + 2)
        attend_pairs("nsa")
        rows("l11", ("w_out", 1))
        ffn(1, 1)
        rows("l12", ("down", 1, 1))

    @block.gpsimd
    def _(pool):
        chain = [0]

        def load(dst, src, name, label=None):
            pool.dma_start(dst, src).then_inc(sem[name], step(name, label, by=16))

        def gains(label, a, b, wa=D, wb=D):
            load(GB[0][:, 0:wa], row(a, wa), "gains_loaded", label)
            if b is not None:
                load(GB[1][:, 0:wb], row(b, wb), "gains_loaded", label)
            pool.wait_ge(sem["gains_loaded"], at("gains_loaded", label))

        def link(ins):
            chain[0] += 1
            ins.then_inc(sem["pool_step"], 1)
            pool.wait_ge(sem["pool_step"], chain[0])

        def rsqrt(ss, n, scale, eps, rs, name, label):
            link(pool.tensor_scalar(RM[:, 0:n], ss, scale, eps, ALU.mult, ALU.add))
            pool.tensor_tensor(rs, RM[:, 0:n], HALF[:, 0:n], ALU.pow).then_inc(sem[name], step(name, label))
            pool.wait_ge(sem[name], at(name, label))

        def rows(s):
            kind, coef = ROWS[s]
            for t in range(TT):
                a = 4 * t
                if kind == "ln":
                    pool.wait_ge(sem["variance"], at("variance", (s, t)))
                    rsqrt(SS[:, a + 1:a + 2], 1, 1.0, LN_EPS / ALPHA ** 2, RS[:, a:a + 1], "rstd", (s, t))
                if kind in ("post", "post_pre"):
                    pool.wait_ge(sem["squared"], at("squared", (s, t)))
                    link(pool.tensor_tensor(SS[:, a:a + 1], SS[:, a:a + 1], SS[:, a + 1:a + 2], ALU.add))
                    rsqrt(SS[:, a:a + 1], 1, 1.0 / D, RMS_EPS, RS[:, a:a + 1], "rstd", (s, t))
                if kind in ("pre", "post_pre"):
                    pool.wait_ge(sem["squared_x"], at("squared_x", (s, t)))
                    rsqrt(SS[:, a + 2:a + 3], 1, 1.0 / D, RMS_EPS, RS[:, a + 2:a + 3], "rstd_x", (s, t))

        load(HOT[0:33, :], A["hot"], "hot_loaded")
        load(RB[0:32, :], A["rel_bias"], "hot_loaded")
        load(MEM[:], A["mem_2"].rearrange("(m p) d -> p m d", p=P), "mem_loaded")
        gains("s0", *GAINS["s0"])
        load(WS[:], A["a_w_s"][0].rearrange("h p q -> p h q"), "ws_loaded")
        pool.wait_ge(sem["half_ready"], at("half_ready"))
        rows("s0")
        pool.wait_ge(sem["bias_copied"], at("bias_copied"))
        for g in range(3):
            L = BIAS_W[g]
            src = BROW[0:16, BIAS_AT[g]:BIAS_AT[g] + L].rearrange("h (p x) -> h p x", p=1).to_broadcast([16, P, L])
            load(bass.AP(scratch[f"bias{g}"].tensor, 0, [[P * (L + 1), 16], [L + 1, P], [1, L]]), src, "bias_stored")
        pool.wait_ge(sem["bias_stored"], at("bias_stored"))
        for l in range(2):
            pool.wait_ge(sem["mem_kv_copied"], at("mem_kv_copied", (l, 3)))
            load(scratch["mem_kv"][l], KVS[:, l].rearrange("p j n -> p (j n)"), "mem_kv_stored")
        for hh in range(2):
            if hh == 0:
                pool.wait_ge(sem["rows_done"], at("rows_done", ("s0", 3)))
                pool.wait_ge(sem["turned"], at("turned", ("s0", 3)))
                load(BS[:], row(A["a_b_s"][0].rearrange("h p -> (h p)"), 2048), "b_s_loaded")
            else:
                pool.wait_ge(sem["v_normed"], at("v_normed", 0))
            gains(("v", hh), A["a_vnorm_g"][0, 1024 * hh:1024 * hh + 1024], A["a_vnorm_b"][0, 1024 * hh:1024 * hh + 1024])
            if hh == 0:
                pool.wait_ge(sem["variance"], at("variance", "v"))
                var = bass.AP(small, 1, [[512, P], [4, TT]])
                rsqrt(var, 4, 1.0, 1e-6, RS[:, 0:4], "rstd", "v")
        pool.wait_ge(sem["v_normed"], at("v_normed", 1))
        gains("s1", *GAINS["s1"])
        rows("s1")
        pool.wait_ge(sem["rows_done"], at("rows_done", ("s1", 3)))
        for g in range(3):
            for hf in range(2):
                if (g, hf) != (0, 0):
                    prev = ("b", g, hf - 1) if hf else ("b", g - 1, 1)
                    pool.wait_ge(sem["masked"], at("masked", (prev, len(ATT[prev][0]) - 1)))
                L, w = BIAS_W[g], 256 if g == 0 else 128
                src = bass.AP(scratch[f"bias{g}"].tensor, hf * 8 * P * (L + 1) + 127, [[L, P], [P * (L + 1), 8], [1, w]])
                load(BG[:, 0:8 * w].rearrange("p (h w) -> p h w", h=8), src, "bias_loaded", (g, hf))
                pool.wait_ge(sem["bias_loaded"], at("bias_loaded", (g, hf)))
                if (g, hf) == (0, 1):
                    pool.wait_ge(sem["o_read"], at("o_read", (("b", 0, 1), 15)))
                    pool.wait_ge(sem["exp_done"], at("exp_done", (("b", 0, 1), 15)))
                    for b in range(TT):
                        for r in range(4):
                            q = slice(32 * b, 32 * b + 32)
                            for dst, srct in ((bO[0][q, r, :], bON[r:P:4, b, :]), (bM[q, 0, r, :], bMN[r:P:4, b, :]),
                                              (bD[q, 0, r, :], bDN[r:P:4, b, :])):
                                load(dst, srct, "o0_permuted")
                    pool.wait_ge(sem["o0_permuted"], at("o0_permuted"))
        pool.wait_ge(sem["group_weights"], at("group_weights"))
        for t in range(TT):
            o = bO[1][:, t, :].rearrange("p (h d) -> p h d", d=64)
            w = bE[:, 1, t, :].rearrange("p (h d) -> p h d", d=1).to_broadcast([P, 16, 64])
            pool.tensor_tensor(o, o, w, ALU.mult).then_inc(sem["o1_weighted"], step("o1_weighted", t))
        gains("s2", *GAINS["s2"])
        rows("s2")
        pool.wait_ge(sem["rows_done"], at("rows_done", ("s2", 3)))
        gains("l00", *GAINS["l00"])
        rows("l00")
        pool.wait_ge(sem["rows_done"], at("rows_done", ("l00", 3)))
        load(GB[0][:, 0:256], row(A["mla_q_norm_g_2"][0], 256), "gains_loaded", "mla")
        load(GB[0][:, 256:384], row(A["mla_kv_norm_g_2"][0], 128), "gains_loaded", "mla")
        load(COS[:], A["cos"].rearrange("(t p) d -> p t d", p=P), "rope_loaded")
        load(SIN[:], A["sin"].rearrange("(t p) d -> p t d", p=P), "rope_loaded")
        load(mCM[:], A["causal"], "mix_const0")
        load(mKV[:].rearrange("p j n -> p (j n)"), scratch["mem_kv"][0], "mem_kv_back", 0)
        pool.wait_ge(sem["gains_loaded"], at("gains_loaded", "mla"))
        pool.wait_ge(sem["c_read"], at("c_read", TT - 1))
        rsqrt(SS[:, 0:4], 4, 1.0 / MLA_QR, RMS_EPS, RS[:, 0:4], "rstd", "mla_q")
        rsqrt(SS[:, 4:8], 4, 1.0 / MLA_KVR, RMS_EPS, RS[:, 4:8], "rstd", "mla")
        pool.wait_ge(sem["c_normed"], at("c_normed", TT - 1))
        gains("l01", *GAINS["l01"])
        rows("l01")
        pool.wait_ge(sem["rows_done"], at("rows_done", ("l01", 3)))
        gains("l02", *GAINS["l02"])
        pool.wait_ge(sem["product_done"], at("product_done", ("panel", ids["down", 0, 1][-3])))
        for j in range(2):
            load(W1[j][:], A["cmp_w1_2"][j].rearrange("(k p) n -> p k n", p=P), "w1_loaded")
            for half in range(2):
                q = slice(64 * half, 64 * half + 64)
                with nc.allow_non_contiguous_dma(reason="4 KB of positions"):
                    load(POS[q, j, :], A["cmp_pos_2"][j].rearrange("l d -> d l"), "pos_loaded")
        with nc.allow_non_contiguous_dma(reason="512 biases"):
            load(B1[:], A["cmp_b1_2"].rearrange("j (h p) -> p j h", p=P), "w1_loaded")
        load(W2[:], A["cmp_w2_2"].rearrange("j (h p) d -> p j h d", p=P), "w1_loaded")
        rows("l02")
        pool.wait_ge(sem["kv_copied"], at("kv_copied"))
        load(scratch["kv"][0], KVF[:, 2:4].rearrange("p j n -> p (j n)"), "kv_kept")
        load(scratch["kv"][1], VV[:].rearrange("p t b n -> p (t b n)"), "kv_kept")
        pool.wait_ge(sem["kv_kept"], at("kv_kept"))
        pool.wait_ge(sem["rows_done"], at("rows_done", ("l02", 3)))
        gains("l10", *GAINS["l10"])
        rows("l10")
        pool.wait_ge(sem["rows_done"], at("rows_done", ("l10", 3)))
        load(nK[:].rearrange("p j n -> p (j n)"), scratch["kv"][0], "nsa_const")
        load(nV[:].rearrange("p t b n -> p (t b n)"), scratch["kv"][1], "nsa_const")
        load(nCM[:], A["causal"], "nsa_const")
        load(nDI[:], A["dist"], "nsa_const")
        load(nCD[:], A["cmp_dist"], "nsa_const")
        load(nCN[:], A["cmp_add"], "nsa_const")
        load(nC1[:], A["cmp_mask"], "nsa_const")
        load(nKV[:].rearrange("p j n -> p (j n)"), scratch["mem_kv"][1], "mem_kv_back", 1)
        gains("l11", *GAINS["l11"])
        rows("l11")
        pool.wait_ge(sem["rows_done"], at("rows_done", ("l11", 3)))
        gains("l12", *GAINS["l12"])
        rows("l12")


def constants():
    def bucket(rel):
        n = np.abs(rel)
        large = 8 + (np.log(np.maximum(n, 1) / 8) / math.log(128) * 8).astype(np.int64)
        return np.where(rel > 0, 16, 0) + np.where(n < 8, n, np.minimum(large, 15))

    hot = np.zeros((33, BIAS_ALL), np.float32)
    for g, (w, at) in enumerate(zip(BIAS_W, BIAS_AT)):
        x = np.arange(w)
        diff = x - 191 if g == 0 else x - 127
        valid = np.abs(diff) <= HALF_W if g < 2 else diff % 4 == 0
        tokens = diff if g == 0 else 4 * diff
        b = bucket(tokens)
        for i in range(w):
            if valid[i]:
                hot[b[i], at + i] = 1.0
            else:
                hot[32, at + i] = NEG
    p, x = np.arange(P)[:, None], np.arange(896)[None, :]
    causal = np.where(x <= 384 + p, 0.0, NEG).astype(np.float32)
    dist = (384 + p - x).astype(np.float32)
    tq = (np.arange(TT)[None, :, None] * P + np.arange(P)[:, None, None])
    n = np.arange(NC)[None, None, :]
    seen = (n * CMP_STRIDE + CMP_LEN - 1 <= tq) & (n < N_CMP)
    half = MLA_ROPE // 2
    freq = (np.float32(10000.0) ** (-np.arange(half, dtype=np.float32) / half)).astype(np.float32)
    ang = np.arange(SEQ, dtype=np.float32)[:, None] * freq[None, :]
    return {"ident": np.eye(P, dtype=np.float32), "hot": hot, "causal": causal, "dist": dist,
            "cmp_dist": (tq - (n * CMP_STRIDE + (CMP_LEN - 1) * 0.5)).astype(np.float32),
            "cmp_add": np.where(seen, 0.0, NEG).astype(np.float32), "cmp_mask": seen.astype(np.float32),
            "cos": np.cos(ang).astype(np.float32), "sin": np.sin(ang).astype(np.float32)}


def kernel(**inputs):
    import concourse.bacc as bacc
    from concourse.bass_utils import run_bass_kernel_spmd

    arrays = {k: np.ascontiguousarray(v) for k, v in inputs.items()}
    arrays["x"] = arrays["x"].reshape(SEQ, D)
    arrays["mem_2"] = arrays["mem_2"].reshape(N_MEM, D)
    arrays.update(constants())

    known = {}
    for _ in range(2):
        nc = bacc.Bacc("TRN2", target_bir_lowering=False, num_devices=1)
        A = {k: nc.dram_tensor(f"in_{k}", v.shape, F32, kind="ExternalInput").ap() for k, v in arrays.items()}
        out = nc.dram_tensor("out_rows", (SEQ, D), F32, kind="ExternalOutput").ap()
        scratch = {f"bias{g}": nc.dram_tensor(f"bias{g}", (16, P * (w + 1)), F32, kind="Internal").ap()
                   for g, w in enumerate(BIAS_W)}
        scratch["mem_kv"] = nc.dram_tensor("mem_kv", (2, P, 1024), F32, kind="Internal").ap()
        scratch["kv"] = nc.dram_tensor("kv", (2, P, 1024), F32, kind="Internal").ap()
        counts = Counts(known)
        with ExitStack() as ctx:
            build(nc, A, out, scratch, ctx, counts)
        known = counts.value
    r = run_bass_kernel_spmd(nc, [{f"in_{k}": v for k, v in arrays.items()}], core_ids=[0])
    return r.results[0]["out_rows"].reshape(1, SEQ, D)
```
